# Optimizing a Trainium2 kernel written in Bass

```python
import math
import jax
import jax.numpy as jnp
from jax import lax
import numpy as np

D_MODEL = 1024
BATCH = 1
SEQ = 1024
DEPTH = 2

CONV_WIDTH = 5
NORM_EPS = 1e-5
SSD_HEADS = 16
SSD_HEAD_DIM = 64
SSD_INNER = SSD_HEADS * SSD_HEAD_DIM
SSD_STATE = 128
SSD_GROUPS = 2
SSD_CHUNK = 128
SSD_CONV_CH = SSD_INNER + 2 * SSD_GROUPS * SSD_STATE
GDN_HEADS = 8
GDN_HEAD_DIM = 128
GDN_INNER = GDN_HEADS * GDN_HEAD_DIM
GDN_CHUNK = 64
GDN_CONV_CH = 3 * GDN_INNER
EVEN_SPLITS = (SSD_INNER, SSD_CONV_CH, 2 * SSD_HEADS, GDN_CONV_CH, GDN_INNER, 2 * GDN_HEADS, 2 * GDN_HEADS)
EVEN_IN_COLS = sum(EVEN_SPLITS)
EVEN_MIX_WIDTH = SSD_INNER + GDN_INNER
ATTN_HEADS = 16
ATTN_KV_HEADS = 4
ATTN_REP = ATTN_HEADS // ATTN_KV_HEADS
ATTN_HEAD_DIM = 64
ATTN_WINDOW = 128
ATTN_BLOCK = ATTN_WINDOW
ATTN_SPLITS = (ATTN_HEADS * ATTN_HEAD_DIM, ATTN_KV_HEADS * ATTN_HEAD_DIM, ATTN_KV_HEADS * ATTN_HEAD_DIM)
ATTN_IN_COLS = sum(ATTN_SPLITS)
D_FF = 4 * D_MODEL
N_EVEN = (DEPTH + 1) // 2
N_ODD = DEPTH // 2
DEEPNORM_ALPHA = (2 * DEPTH) ** 0.25
DEEPNORM_BETA = (8 * DEPTH) ** -0.25

kernel_name = 'bidir_hybrid_ssd_gdn_swa_deepnorm'

def split_cols(t, sizes):
    return jnp.split(t, np.cumsum(sizes)[:-1].tolist(), axis=-1)

def seq_flip(t):
    return jnp.flip(t, axis=1)

def layer_norm(x, g, b):
    xf = x.astype(jnp.float32)
    mu = jnp.mean(xf, axis=-1, keepdims=True)
    var = jnp.mean(jnp.square(xf - mu), axis=-1, keepdims=True)
    return ((xf - mu) * lax.rsqrt(var + NORM_EPS) * g.astype(jnp.float32) + b.astype(jnp.float32)).astype(x.dtype)

def rms_norm(x, w):
    xf = x.astype(jnp.float32)
    return (xf * lax.rsqrt(jnp.mean(xf * xf, axis=-1, keepdims=True) + NORM_EPS) * w.astype(jnp.float32)).astype(x.dtype)

def l2_normalize(x):
    return x * lax.rsqrt(jnp.sum(x * x, axis=-1, keepdims=True) + 1e-6)

def centred_depthwise_conv(x, w):
    pad = (CONV_WIDTH - 1) // 2
    return lax.conv_general_dilated(x, w[:, None, :].astype(x.dtype), window_strides=(1,), padding=[(pad, pad)], dimension_numbers=('NWC', 'WIO', 'NWC'), feature_group_count=x.shape[-1])

def masked_exp_tril(cs):
    q = cs.shape[-1]
    tri = jnp.tril(jnp.ones((q, q), bool))
    return jnp.exp(jnp.where(tri, cs[..., :, None] - cs[..., None, :], -jnp.inf))

def ssd_scan(x, a, b, c):
    bsz, s, h, p = x.shape
    g, n = b.shape[-2:]
    r = h // g
    nc = s // SSD_CHUNK
    xc = x.reshape(bsz, nc, SSD_CHUNK, g, r, p)
    bc = b.reshape(bsz, nc, SSD_CHUNK, g, n)
    cc = c.reshape(bsz, nc, SSD_CHUNK, g, n)
    a_cs = jnp.cumsum(a.reshape(bsz, nc, SSD_CHUNK, g, r).transpose(0, 3, 4, 1, 2), axis=-1)
    cb = jnp.einsum('bclgn,bcsgn->bgcls', cc, bc)
    scores = cb[:, :, None] * masked_exp_tril(a_cs)
    y_diag = jnp.einsum('bgrcls,bcsgrp->bclgrp', scores, xc)
    decay_to_end = jnp.exp(a_cs[..., -1:] - a_cs)
    chunk_states = jnp.einsum('bclgn,bgrcl,bclgrp->bcgrpn', bc, decay_to_end, xc)
    chunk_decay = jnp.exp(a_cs[..., -1])

    def step(state, inp):
        st, dec = inp
        return state * dec[..., None, None] + st, state

    init = jnp.zeros((bsz, g, r, p, n), jnp.float32)
    _, prev_states = lax.scan(step, init, (jnp.moveaxis(chunk_states, 1, 0), jnp.moveaxis(chunk_decay, 3, 0)))
    prev_states = jnp.moveaxis(prev_states, 0, 1)
    y_off = jnp.einsum('bclgn,bcgrpn,bgrcl->bclgrp', cc, prev_states, jnp.exp(a_cs))
    return (y_diag + y_off).reshape(bsz, s, h, p)

def gated_delta_scan(q, k, v, g, beta):
    bsz, s, h, dk = k.shape
    dv = v.shape[-1]
    nc = s // GDN_CHUNK
    cq = GDN_CHUNK

    def chunks(t):
        t = t.reshape(bsz, nc, cq, h, *t.shape[3:])
        return jnp.moveaxis(t, (1, 3), (0, 2))

    qc, kc, vc, gc, bc = chunks(q), chunks(k), chunks(v), chunks(g), chunks(beta)
    g_cs = jnp.cumsum(gc, axis=-1)
    decay = masked_exp_tril(g_cs)
    strict = jnp.tril(jnp.ones((cq, cq), bool), -1)
    k_beta = kc * bc[..., None]
    v_beta = vc * bc[..., None]
    lower = jnp.where(strict, jnp.einsum('nbhid,nbhjd->nbhij', k_beta, kc) * decay, 0.0)
    eye = jnp.eye(cq, dtype=lower.dtype)
    t_inv = lax.linalg.triangular_solve(lower + eye, jnp.broadcast_to(eye, lower.shape), left_side=True, lower=True, unit_diagonal=True)
    u = t_inv @ v_beta
    w = t_inv @ (k_beta * jnp.exp(g_cs)[..., None])
    qk = jnp.einsum('nbhid,nbhjd->nbhij', qc, kc) * decay
    q_dec = qc * jnp.exp(g_cs)[..., None]
    k_dec = kc * jnp.exp(g_cs[..., -1:] - g_cs)[..., None]
    last = jnp.exp(g_cs[..., -1])

    def step(state, inp):
        u_i, w_i, qk_i, q_i, k_i, l_i = inp
        v_new = u_i - w_i @ state
        o_i = q_i @ state + qk_i @ v_new
        state = state * l_i[..., None, None] + jnp.swapaxes(k_i, -1, -2) @ v_new
        return state, o_i

    init = jnp.zeros((bsz, h, dk, dv), jnp.float32)
    _, o = lax.scan(step, init, (u, w, qk, q_dec, k_dec, last))
    return jnp.moveaxis(o, (0, 2), (1, 3)).reshape(bsz, s, h, dv)

def even_mixer(x, w_in, ssd_conv_w, ssd_conv_b, ssd_dt_bias, ssd_a_log, ssd_d, ssd_norm_w, gdn_conv_w, gdn_dt_bias, gdn_a_log, gdn_norm_w, w_out):
    bsz, s, _ = x.shape
    f32 = jnp.float32
    z, xbc, dt_raw, qkv, gate, a_raw, b_raw = split_cols(x @ w_in, EVEN_SPLITS)
    xbc = jax.nn.silu(centred_depthwise_conv(xbc, ssd_conv_w) + ssd_conv_b).astype(f32)
    xs, bs, cs = split_cols(xbc, (SSD_INNER, SSD_GROUPS * SSD_STATE, SSD_GROUPS * SSD_STATE))
    xs = xs.reshape(bsz, s, SSD_HEADS, SSD_HEAD_DIM)
    bs = bs.reshape(bsz, s, SSD_GROUPS, SSD_STATE)
    cs = cs.reshape(bsz, s, SSD_GROUPS, SSD_STATE)
    dt = jax.nn.softplus(dt_raw.astype(f32).reshape(bsz, s, 2, SSD_HEADS) + ssd_dt_bias.astype(f32))
    a = -jnp.exp(ssd_a_log.astype(f32)) * dt
    x_dt = xs[:, :, None] * dt[..., None]
    y_f = ssd_scan(x_dt[:, :, 0], a[:, :, 0], bs, cs)
    y_b = seq_flip(ssd_scan(seq_flip(x_dt[:, :, 1]), seq_flip(a[:, :, 1]), seq_flip(bs), seq_flip(cs)))
    y = (y_f + y_b + ssd_d.astype(f32)[:, None] * xs).reshape(bsz, s, SSD_INNER) * jax.nn.silu(z.astype(f32))
    y_a = rms_norm(y.reshape(bsz, s, SSD_GROUPS, -1), ssd_norm_w.reshape(SSD_GROUPS, -1)).reshape(bsz, s, SSD_INNER)
    qkv = jax.nn.silu(centred_depthwise_conv(qkv, gdn_conv_w)).astype(f32)
    q, k, v = split_cols(qkv, (GDN_INNER, GDN_INNER, GDN_INNER))
    hshape = (bsz, s, GDN_HEADS, GDN_HEAD_DIM)
    q = l2_normalize(q.reshape(hshape)) * GDN_HEAD_DIM ** -0.5
    k = l2_normalize(k.reshape(hshape))
    v = v.reshape(hshape)
    g = -jnp.exp(gdn_a_log.astype(f32)) * jax.nn.softplus(a_raw.astype(f32).reshape(bsz, s, 2, GDN_HEADS) + gdn_dt_bias.astype(f32))
    beta = jax.nn.sigmoid(b_raw.astype(f32).reshape(bsz, s, 2, GDN_HEADS))
    o = gated_delta_scan(q, k, v, g[:, :, 0], beta[:, :, 0]) + seq_flip(gated_delta_scan(seq_flip(q), seq_flip(k), seq_flip(v), seq_flip(g[:, :, 1]), seq_flip(beta[:, :, 1])))
    y_b_grp = (rms_norm(o, gdn_norm_w) * jax.nn.silu(gate.astype(f32).reshape(hshape))).reshape(bsz, s, GDN_INNER)
    return jnp.concatenate([y_a, y_b_grp], axis=-1).astype(x.dtype) @ w_out

def alibi_slopes(n_heads):
    return 2.0 ** (-8.0 * jnp.arange(1, n_heads + 1, dtype=jnp.float32) / n_heads)

def windowed_attention(x, w_qkv, sink, w_o):
    bsz, s, _ = x.shape
    nb = s // ATTN_BLOCK
    f32 = jnp.float32
    q, k, v = split_cols(x @ w_qkv, ATTN_SPLITS)
    q = q.reshape(bsz, nb, ATTN_BLOCK, ATTN_KV_HEADS, ATTN_REP, ATTN_HEAD_DIM)

    def banded(t):
        tp = jnp.pad(t.reshape(bsz, s, ATTN_KV_HEADS, ATTN_HEAD_DIM), ((0, 0), (ATTN_BLOCK, ATTN_BLOCK), (0, 0), (0, 0)))
        tp = tp.reshape(bsz, nb + 2, ATTN_BLOCK, ATTN_KV_HEADS, ATTN_HEAD_DIM)
        return jnp.concatenate([tp[:, :-2], tp[:, 1:-1], tp[:, 2:]], axis=2)

    kb, vb = banded(k), banded(v)
    scores = jnp.einsum('bnqgrd,bnkgd->bgrnqk', q, kb, preferred_element_type=f32) * ATTN_HEAD_DIM ** -0.5
    qi = jnp.arange(ATTN_BLOCK)[:, None]
    kj = jnp.arange(3 * ATTN_BLOCK)[None, :]
    dist = jnp.abs(qi + ATTN_BLOCK - kj)
    key_pos = jnp.arange(nb)[:, None] * ATTN_BLOCK + kj - ATTN_BLOCK
    valid = (dist <= ATTN_WINDOW)[None] & ((key_pos >= 0) & (key_pos < s))[:, None, :]
    bias = -alibi_slopes(ATTN_HEADS).reshape(ATTN_KV_HEADS, ATTN_REP)[:, :, None, None] * dist.astype(f32)
    scores = jnp.where(valid, scores + bias[:, :, None], -jnp.inf)
    sink_logit = sink.astype(f32).reshape(ATTN_KV_HEADS, ATTN_REP)[:, :, None, None, None]
    m = jnp.maximum(jnp.max(scores, axis=-1, keepdims=True), sink_logit)
    p = jnp.exp(scores - m)
    denom = jnp.sum(p, axis=-1, keepdims=True) + jnp.exp(sink_logit - m)
    out = jnp.einsum('bgrnqk,bnkgd->bgrnqd', p, vb.astype(f32)) / denom
    out = jnp.transpose(out, (0, 3, 4, 1, 2, 5)).reshape(bsz, s, ATTN_HEADS * ATTN_HEAD_DIM)
    return out.astype(x.dtype) @ w_o

def setup_inputs(seed: int = 0) -> dict:
    key = jax.random.key(seed)
    ks = jax.random.split(key, 22)
    f32 = jnp.float32

    def normal(k, shape, scale):
        return jax.random.normal(k, shape, f32) * scale

    def around_one(k, shape):
        return 1.0 + 0.05 * jax.random.normal(k, shape, f32)

    def dt_bias(k, shape):
        dt = jnp.exp(jax.random.uniform(k, shape, f32, math.log(1e-3), math.log(1e-1)))
        return dt + jnp.log(-jnp.expm1(-dt))

    def a_log(k, shape):
        return jnp.log(jax.random.uniform(k, shape, f32, 1.0, 16.0))

    ne, no = N_EVEN, N_ODD
    attn_width = ATTN_HEADS * ATTN_HEAD_DIM
    return {
        'x': normal(ks[0], (BATCH, SEQ, D_MODEL), 1.0),
        'even_w_in': normal(ks[1], (ne, D_MODEL, EVEN_IN_COLS), D_MODEL ** -0.5),
        'ssd_conv_w': normal(ks[2], (ne, CONV_WIDTH, SSD_CONV_CH), CONV_WIDTH ** -0.5),
        'ssd_conv_b': normal(ks[3], (ne, SSD_CONV_CH), 0.02),
        'ssd_dt_bias': dt_bias(ks[4], (ne, 2, SSD_HEADS)),
        'ssd_a_log': a_log(ks[5], (ne, 2, SSD_HEADS)),
        'ssd_d': around_one(ks[6], (ne, SSD_HEADS)),
        'ssd_norm_w': around_one(ks[7], (ne, SSD_INNER)),
        'gdn_conv_w': normal(ks[8], (ne, CONV_WIDTH, GDN_CONV_CH), CONV_WIDTH ** -0.5),
        'gdn_dt_bias': dt_bias(ks[9], (ne, 2, GDN_HEADS)),
        'gdn_a_log': a_log(ks[10], (ne, 2, GDN_HEADS)),
        'gdn_norm_w': around_one(ks[11], (ne, GDN_HEAD_DIM)),
        'even_w_out': normal(ks[12], (ne, EVEN_MIX_WIDTH, D_MODEL), DEEPNORM_BETA * EVEN_MIX_WIDTH ** -0.5),
        'attn_w_qkv': normal(ks[13], (no, D_MODEL, ATTN_IN_COLS), D_MODEL ** -0.5),
        'attn_sink': normal(ks[14], (no, ATTN_HEADS), 1.0),
        'attn_w_o': normal(ks[15], (no, attn_width, D_MODEL), DEEPNORM_BETA * attn_width ** -0.5),
        'ln_mix_g': around_one(ks[16], (DEPTH, D_MODEL)),
        'ln_mix_b': normal(ks[17], (DEPTH, D_MODEL), 0.02),
        'mlp_w1': normal(ks[18], (DEPTH, D_MODEL, D_FF), D_MODEL ** -0.5),
        'mlp_w2': normal(ks[19], (DEPTH, D_FF, D_MODEL), DEEPNORM_BETA * D_FF ** -0.5),
        'ln_ffn_g': around_one(ks[20], (DEPTH, D_MODEL)),
        'ln_ffn_b': normal(ks[21], (DEPTH, D_MODEL), 0.02),
    }

def reference(x, even_w_in, ssd_conv_w, ssd_conv_b, ssd_dt_bias, ssd_a_log, ssd_d, ssd_norm_w, gdn_conv_w, gdn_dt_bias, gdn_a_log, gdn_norm_w, even_w_out, attn_w_qkv, attn_sink, attn_w_o, ln_mix_g, ln_mix_b, mlp_w1, mlp_w2, ln_ffn_g, ln_ffn_b):
    for layer in range(DEPTH):
        i = layer // 2
        if layer % 2 == 0:
            mix = even_mixer(x, even_w_in[i], ssd_conv_w[i], ssd_conv_b[i], ssd_dt_bias[i], ssd_a_log[i], ssd_d[i], ssd_norm_w[i], gdn_conv_w[i], gdn_dt_bias[i], gdn_a_log[i], gdn_norm_w[i], even_w_out[i])
        else:
            mix = windowed_attention(x, attn_w_qkv[i], attn_sink[i], attn_w_o[i])
        x = layer_norm(DEEPNORM_ALPHA * x + mix, ln_mix_g[layer], ln_mix_b[layer])
        h = jnp.square(jax.nn.relu(x @ mlp_w1[layer]))
        x = layer_norm(DEEPNORM_ALPHA * x + h @ mlp_w2[layer], ln_ffn_g[layer], ln_ffn_b[layer])
    return x


_drawn_inputs = setup_inputs


def setup_inputs(seed=0):
    import zlib

    import numpy as np

    out = dict(_drawn_inputs(seed))
    spreads = {}
    factors = {'ssd_conv_b': 7.717,
     'ssd_d': 8.0,
     'ssd_norm_w': 4.534,
     'gdn_norm_w': 7.166,
     'attn_sink': 5.009}
    for name, (base, spread) in spreads.items():
        noise = np.random.default_rng([zlib.crc32(name.encode()), seed]).standard_normal(out[name].shape)
        drawn = base * np.exp(spread * noise) if base else spread * noise
        out[name] = jnp.asarray(drawn.astype(out[name].dtype))
    for name, factor in factors.items():
        out[name] = (out[name] * factor).astype(out[name].dtype)
    return out
```

```python
from contextlib import ExitStack

import concourse.bass as bass
from concourse import mybir

F32 = mybir.dt.float32
F32R = mybir.dt.float32r
ALU = mybir.AluOpType
ACT = mybir.ActivationFunctionType
AX = mybir.AxisListType.X
ds = bass.ds

P = 128
S = 1024
D = 1024
NT = S // P
KT = D // P
HALF = 512
CONV = 5
PAD = CONV // 2
EPS = 1e-5

SSD_H, SSD_HD, SSD_G, SSD_N = 16, 64, 2, 128
SSD_GH = SSD_H // SSD_G
GDN_H, GDN_D = 8, 128
DIR_H = SSD_H + GDN_H
COL_DT, COL_A, COL_B = 2560, 6688, 6704
IN_TILES = 52
Z0, XS0, BC0, Q0, K0, V0, G0 = (P * (1 + n) for n in (0, 8, 16, 20, 28, 36, 44))
SCR_COLS = P * (1 + IN_TILES)

SLAB = 256
RING = 2

ALPHA = 4 ** 0.25


class Phase:

    def __init__(self, nc, ctx, name):
        self.nc, self.ctx, self.name, self.sems = nc, ctx, name, []
        ctx.callback(self.clear)

    def sb(self, name, shape, dt=F32):
        return self.ctx.enter_context(self.nc.sbuf_tensor(f"{self.name}_{name}", shape, dt))

    def sem(self, name):
        self.sems.append(self.nc.alloc_semaphore(name=f"{self.name}_{name}"))
        return self.sems[-1]

    def clear(self):
        self.nc.clear_and_free_semaphores(self.sems)
        self.nc.all_engine_barrier()


def product(pe, out, wh, wl, xh, xl, first=True, last=True):
    pe.matmul(out, wh, xh, start=first, stop=False)
    pe.matmul(out, wh, xl, start=False, stop=False)
    return pe.matmul(out, wl, xh, start=False, stop=last)


def phase_masks(nc, A, mem):
    masks = {"le": (1, -1, 0), "gt": (-1, 1, -1), "ge": (-1, 1, 0), "lt": (1, -1, -1)}
    with ExitStack() as ctx:
        ph = Phase(nc, ctx, "mk")
        s_ones = ph.sem("ones")
        s_mask = ph.sem("mask")
        with nc.Block() as block:
            @block.gpsimd
            def _(pool):
                names = ["ident", "ones", *masks]
                for n in names:
                    last = pool.memset(mem[n][:, :], 0.0 if n == "ident" else 1.0)
                last.then_inc(s_ones, 1)
                pool.wait_ge(s_ones, 1)
                pool.affine_select(out=mem["ident"][:, :], in_=mem["ident"][:, :], compare_op=ALU.not_equal,
                                   fill=1.0, base=0, pattern=[[-1, P]], channel_multiplier=1).then_inc(s_mask, 1)
                for n, (col, row, base) in masks.items():
                    pool.affine_select(out=mem[n][:, :], in_=mem[n][:, :], compare_op=ALU.is_ge, fill=0.0,
                                       base=base, pattern=[[col, P]], channel_multiplier=row).then_inc(s_mask, 1)
                pool.wait_ge(s_mask, 5)


def phase_in(nc, A, mem):
    ps, ident = mem["ps"], mem["ident"]
    with ExitStack() as ctx:
        ph = Phase(nc, ctx, "in")
        sb, sem = ph.sb, ph.sem
        xh, xl = sb("xh", [P, KT, S], F32R), sb("xl", [P, KT, S], F32R)
        raw = sb("raw", [P, RING, KT, SLAB])
        wh, wl = sb("wh", [P, RING, KT, SLAB], F32R), sb("wl", [P, RING, KT, SLAB], F32R)
        xrow = sb("xrow", [P, RING, D])
        SC, GC = 12, 24
        cw_rows = sb("cw_rows", [P, 3, P])
        cw = sb("cw", [P, CONV * (SC + GC)])
        cb = sb("cb", [P, SC + GC])
        cbuf = sb("cbuf", [P, RING, S + 2 * PAD])
        cacc = sb("cacc", [P, RING, S])
        sil = sb("sil", [P, RING, S])
        tok = sb("tok", [P, RING, NT, P])
        sq = sb("sq", [P, NT, P])
        nraw = sb("nraw", [P, KT, P])
        nwh, nwl = sb("nwh", [P, KT, P], F32R), sb("nwl", [P, KT, P], F32R)
        hcol = sb("hcol", [P, 4])

        s_x = [sem("x0"), sem("x1")]
        s_small = sem("small")
        s_zero = sem("zero")
        s_xt = sem("xt")
        s_xh = sem("xh_done")
        s_xl = sem("xl_done")
        s_cwt = sem("cwt")
        s_cw = sem("cw_done")
        s_raw = [sem("raw0"), sem("raw1")]
        s_wh = sem("wh_done")
        s_wl = sem("wl_done")
        s_mm = sem("mm")
        s_ev = sem("ev")
        s_tap = sem("tap")
        s_conv = sem("conv")
        s_sil = sem("sil_done")
        s_tr = sem("tr")
        s_tok = sem("tok_done")
        s_sq = sem("sq_done")
        s_ss = sem("ss_done")
        s_st = [sem("st0"), sem("st1")]
        s_stc = [sem("stc0"), sem("stc1")]
        s_nw = sem("nw")
        s_nmm = sem("nmm")
        s_na = sem("na")
        s_nv = sem("nv")
        s_nt = sem("nt")
        s_sum = sem("sum")

        CLASSES = [(0, 4, False, False, False), (1024, 4, True, False, False), (2048, 2, True, True, False),
                   (2592, 12, True, False, True), (5664, 4, False, False, False)]
        CONV_T, SUM_T = 8, 20
        SMALL = 10 * 16
        w_in = A["even_w_in"][0].rearrange("(k p) n -> p k n", p=P)
        scr = A["scr"].rearrange("(t p) n -> p t n", p=P)

        def by_class(eng, body, between=None):
            first = 0
            for c in CLASSES:
                if between:
                    between(c)
                with eng.Fori(0, c[1] // 2) as i:
                    for u in range(2):
                        body(c, i * 2 + (first + u), u, i * 2 + u)
                first += c[1]

        one = mem["ones"][:, 0:1].unsqueeze(1).broadcast_to([P, KT, SLAB])

        with nc.Block() as block:
            @block.sync
            def _(sp):
                for t in range(NT):
                    if t >= RING:
                        sp.wait_ge(s_xt, 2 * (t - 1))
                    sp.dma_start(xrow[:, t % 2, :], A["x"][0, t * P:(t + 1) * P, :]).then_inc(s_x[t % 2], 16)
                sp.wait_ge(s_zero, 1)
                for o, c, n in ((0, COL_DT, 32), (32, COL_A, 16), (64, COL_B, 16)):
                    sp.dma_start(nraw[:, :, o:o + n], w_in[:, :, c:c + n]).then_inc(s_small, 16)

                def body(c, j, u, m):
                    sp.wait_ge(s_wl, j + 1)
                    sp.dma_start(raw[:, u], w_in[:, :, ds(m * SLAB + c[0], SLAB)]).then_inc(s_raw[u], 16)
                by_class(sp, body)

            @block.gpsimd
            def _(pool):
                pool.memset(nraw[:, :, :], 0.0)
                pool.memset(cb[:, :], 0.0)
                pool.memset(sil[:, 1, :], 0.0)
                pool.memset(cbuf[:, :, :], 0.0).then_inc(s_zero, 1)
                pool.sem_inc(s_wl, RING)

                def body(c, j, u, m):
                    pool.wait_ge(s_raw[u], j * 8 + (16 - 8 * u))
                    pool.wait_ge(s_mm, j * 2 + 2)
                    pool.tensor_tensor(wh[:, u], raw[:, u], one, ALU.mult).then_inc(s_wh, 1)
                    pool.wait_ge(s_wh, j + 1)
                    pool.tensor_tensor(wl[:, u], raw[:, u], wh[:, u].bitcast(F32), ALU.subtract).then_inc(s_wl, 1)
                by_class(pool, body)
                pool.wait_ge(s_small, SMALL)
                pool.tensor_copy(nwh[:, :, :], nraw[:, :, :]).then_inc(s_nw, 1)
                pool.wait_ge(s_nw, 1)
                pool.tensor_tensor(nwl[:, :, :], nraw[:, :, :], nwh[:, :, :].bitcast(F32), ALU.subtract).then_inc(s_nw, 1)

            @block.tensor
            def _(pe):
                for n in range(2 * NT):
                    t, q = n // 2, n % 2
                    pe.wait_ge(s_x[t % 2], 16 * (t // 2 + 1))
                    if n >= 4:
                        pe.wait_ge(s_xl, n - 3)
                    for k in range(4):
                        last = pe.transpose(ps[:, n % 4, k * P:(k + 1) * P],
                                            xrow[:, t % 2, (4 * q + k) * P:(4 * q + k + 1) * P], ident[:, :])
                    last.then_inc(s_xt, 1)
                pe.wait_ge(s_small, SMALL)
                pe.transpose(ps[:, 4, 0:CONV * SC], cw_rows[0:CONV * SC, 0, :], ident[0:CONV * SC, 0:CONV * SC])
                pe.transpose(ps[:, 4, CONV * SC:CONV * (SC + GC)], cw_rows[0:CONV * GC, 1, :],
                             ident[0:CONV * GC, 0:CONV * GC])
                pe.transpose(ps[:, 4, 256:256 + SC], cw_rows[0:SC, 2, :], ident[0:SC, 0:SC]).then_inc(s_cwt, 1)
                pe.wait_ge(s_xl, 2 * NT)
                pe.wait_ge(s_cw, 2)
                pe.wait_ge(s_zero, 1)
                pe.sem_inc(s_mm, 2 * RING)

                def turn(n, par):
                    pe.wait_ge(s_sil, n + 1)
                    pe.wait_ge(s_tok, n + 1)
                    for t in range(NT):
                        last = pe.transpose(ps[:, 4 + 2 * par + t // 4, (t % 4) * P:(t % 4 + 1) * P],
                                            sil[:, 1 - par, t * P:(t + 1) * P], ident[:, :])
                    last.then_inc(s_tr, 1)

                def body(c, j, u, m):
                    pe.wait_ge(s_wl, j + 1 + RING)
                    for h in range(2):
                        T = j * 2 + h
                        pe.wait_ge(s_ev, T + 1)
                        for half in range(2):
                            for k in range(KT):
                                last = product(pe, ps[:, 2 * h + half, :], wh[:, u, k, h * P:(h + 1) * P],
                                               wl[:, u, k, h * P:(h + 1) * P],
                                               xh[:, k, half * HALF:(half + 1) * HALF],
                                               xl[:, k, half * HALF:(half + 1) * HALF],
                                               k == 0, k == KT - 1)
                        last.then_inc(s_mm, 1)
                        turn(T, h)
                by_class(pe, body)
                turn(IN_TILES, 0)
                pe.wait_ge(s_nw, 2)
                for half in range(2):
                    for k in range(KT):
                        last = product(pe, ps[:, half, :], nwh[:, k, :], nwl[:, k, :],
                                       xh[:, k, half * HALF:(half + 1) * HALF],
                                       xl[:, k, half * HALF:(half + 1) * HALF], k == 0, k == KT - 1)
                last.then_inc(s_nmm, 1)
                pe.wait_ge(s_nv, 13)
                pe.wait_ge(s_na, 4)
                step, decay, beta = cacc[:, 0, :], cacc[:, 1, :], sil[:, 0, :]
                for t in range(NT):
                    pe.transpose(ps[:, 2, t * 32:(t + 1) * 32], step[0:32, t * P:(t + 1) * P], ident[0:32, 0:32])
                    pe.transpose(ps[:, 3, t * 48:(t + 1) * 48], decay[0:48, t * P:(t + 1) * P], ident[0:48, 0:48])
                    last = pe.transpose(ps[:, 7, t * 16:(t + 1) * 16], beta[64:80, t * P:(t + 1) * P],
                                        ident[64:80, 64:80])
                last.then_inc(s_nt, 1)
                pe.wait_ge(s_na, 7)
                dec = mem["dec"]
                for b, forward, backward in ((4, "le", "ge"), (5, "gt", "lt")):
                    out = ps[:, b, 0:NT * 48].rearrange("p (t c) -> p t c", c=48)
                    for c0, c1, m in ((0, 16, forward), (16, 32, backward), (32, 40, forward), (40, 48, backward)):
                        pe.matmul(out[:, :, c0:c1], mem[m][:, :], dec[:, :, c0:c1], start=True, stop=True)
                pe.matmul(ps[:, 6, 0:NT * 48], mem["ones"][:, :], dec[:, :, :].rearrange("p t c -> p (t c)"),
                          start=True, stop=True).then_inc(s_sum, 1)

            @block.scalar
            def _(act):
                for dst, src in ((cw_rows[0:CONV * SC, 0, :], A["ssd_conv_w"][0].rearrange("j (c p) -> (j c) p", p=P)),
                                 (cw_rows[0:CONV * GC, 1, :], A["gdn_conv_w"][0].rearrange("j (c p) -> (j c) p", p=P)),
                                 (cw_rows[0:SC, 2, :], A["ssd_conv_b"][0].rearrange("(c p) -> c p", p=P))):
                    act.dma_start(dst, src).then_inc(s_small, 16)
                for col, names in ((0, ("ssd_dt_bias", "gdn_dt_bias")), (1, ("ssd_a_log", "gdn_a_log"))):
                    for r, n in zip((0, 32), names):
                        src = A[n][0].rearrange("a (h o) -> (a h) o", o=1)
                        act.dma_start(hcol[r:r + src.shape[0], col:col + 1], src).then_inc(s_small, 16)
                for n in range(2 * NT):
                    t, q = n // 2, n % 2
                    act.wait_ge(s_xt, n + 1)
                    act.activation(xh[:, 4 * q:4 * q + 4, t * P:(t + 1) * P],
                                   ps[:, n % 4, :].rearrange("p (k c) -> p k c", k=4), ACT.Copy).then_inc(s_xh, 1)
                act.wait_ge(s_cwt, 1)
                act.wait_ge(s_zero, 1)
                act.activation(cw[:, :], ps[:, 4, 0:CONV * (SC + GC)], ACT.Copy).then_inc(s_cw, 1)
                act.activation(cb[:, 0:SC], ps[:, 4, 256:256 + SC], ACT.Copy).then_inc(s_cw, 1)
                act.sem_inc(s_ev, RING)
                act.sem_inc(s_tok, RING)
                act.sem_inc(s_sil, 1)
                for q in range(2):
                    act.sem_inc(s_st[q], 16)
                act.wait_ge(s_cw, 2)

                def rows_out(n, par, stores, sums):
                    act.wait_ge(s_tr, n + 1)
                    if sums:
                        act.wait_ge(s_ss, n - SUM_T + 1)
                    act.wait_ge(s_st[par], stores)
                    act.activation(tok[:, par], ps[:, 4 + 2 * par:6 + 2 * par, :].rearrange("p b (t c) -> p (b t) c", c=P),
                                   ACT.Copy).then_inc(s_tok, 1)
                    act.wait_ge(s_tok, n + 1 + RING)
                    act.dma_start(scr[:, :, ds(n * P, P)], tok[:, par]).then_inc(s_st[par], 16)

                def between(c):
                    if c[0] == 2592:
                        for q in range(2):
                            act.wait_ge(s_stc[q], 32)
                    if c[0] == 5664:
                        act.wait_ge(s_ss, 24 + RING)

                def body(c, j, u, m):
                    for h in range(2):
                        T = j * 2 + h
                        act.wait_ge(s_mm, T + 1 + 2 * RING)
                        if c[2]:
                            act.wait_ge(s_conv, T - CONV_T + 1)
                        act.activation(cbuf[:, h, PAD:PAD + S], ps[:, 2 * h:2 * h + 2, :].rearrange("p b n -> p (b n)"),
                                       ACT.Copy).then_inc(s_ev, 1)
                        rows_out(T, h, j * 16 + 16, c[4])
                        if c[2]:
                            act.wait_ge(s_conv, T - CONV_T + 1 + RING)
                            if c[3] and u == 1:
                                act.wait_ge(s_stc[h], 16)
                            act.activation(sil[:, h, :], cacc[:, h, :], ACT.Silu,
                                           bias=cb[:, ds(T - CONV_T, 1)]).then_inc(s_sil, 1)
                        else:
                            act.wait_ge(s_ev, T + 1 + RING)
                            act.activation(sil[:, h, :], cbuf[:, h, PAD:PAD + S], ACT.Silu).then_inc(s_sil, 1)
                        if c[3]:
                            act.wait_ge(s_sil, T + 2)
                            act.dma_start(A["scr_t"][(2 * u + h) * P:(2 * u + h + 1) * P, :], sil[:, h, :]
                                          ).then_inc(s_stc[h], 16)
                by_class(act, body, between)
                rows_out(IN_TILES, 0, IN_TILES * 8 + 16, False)
                act.activation(hcol[0:48, 2:3], hcol[0:48, 1:2], ACT.Exp).then_inc(s_na, 1)
                act.wait_ge(s_nv, 2)
                act.activation(cbuf[0:48, 1, 0:S], cbuf[0:48, 0, 0:S], ACT.Exp, scale=-1.0).then_inc(s_na, 1)
                act.wait_ge(s_nv, 3)
                act.activation(sil[0:48, 1, :], sq[0:48, :, :].rearrange("p a b -> p (a b)"), ACT.Ln).then_inc(s_na, 1)
                act.wait_ge(s_nmm, 1)
                act.activation(sil[64:80, 0, :], ps[64:80, 0:2, :].rearrange("p b n -> p (b n)"),
                               ACT.Sigmoid).then_inc(s_na, 1)
                act.wait_ge(s_nt, 1)
                act.activation(mem["step"][:, :, :], ps[:, 2, 0:256].rearrange("p (t c) -> p t c", c=32),
                               ACT.Copy).then_inc(s_na, 1)
                act.activation(mem["beta"][:, :, :], ps[:, 7, 0:128].rearrange("p (t c) -> p t c", c=16),
                               ACT.Copy).then_inc(s_na, 1)
                act.activation(mem["dec"][:, :, :], ps[:, 3, 0:384].rearrange("p (t c) -> p t c", c=48),
                               ACT.Copy).then_inc(s_na, 1)
                act.wait_ge(s_sum, 1)
                for b, n in ((4, "ein"), (5, "eout"), (6, "etot")):
                    act.activation(mem[n][:, :, :], ps[:, b, 0:384].rearrange("p (t c) -> p t c", c=48),
                                   ACT.Exp).then_inc(s_na, 1)
                act.wait_ge(s_na, 10)
                act.wait_ge(s_st[0], 16 * (IN_TILES // 2 + 2))
                act.wait_ge(s_st[1], 16 * (IN_TILES // 2 + 1))

            @block.vector
            def _(dve):
                for n in range(2 * NT):
                    t, q = n // 2, n % 2
                    out = (slice(None), slice(4 * q, 4 * q + 4), slice(t * P, (t + 1) * P))
                    dve.wait_ge(s_xh, n + 1)
                    dve.tensor_tensor(xl[out], ps[:, n % 4, :].rearrange("p (k c) -> p k c", k=4),
                                      xh[out].bitcast(F32), ALU.subtract).then_inc(s_xl, 1)
                dve.sem_inc(s_conv, RING)
                dve.sem_inc(s_ss, RING)
                dve.wait_ge(s_cw, 1)

                def body(c, j, u, m):
                    if not c[2]:
                        return
                    for h in range(2):
                        T = j * 2 + h
                        ct = T - CONV_T
                        off, st = (ct, SC) if c[0] < COL_DT else (ct + (CONV * SC - SC), GC)
                        dve.wait_ge(s_ev, T + 1 + RING)
                        dve.wait_ge(s_sil, T)
                        dve.tensor_scalar(cacc[:, h, :], cbuf[:, h, 0:S], cw[:, ds(off, 1)], None,
                                          ALU.mult).then_inc(s_tap, 1)
                        for k in range(1, CONV):
                            dve.wait_ge(s_tap, ct * (CONV - 1) + k)
                            ins = dve.scalar_tensor_tensor(out=cacc[:, h, :], in0=cbuf[:, h, k:k + S],
                                                           scalar=cw[:, ds(off + k * st, 1)], in1=cacc[:, h, :],
                                                           op0=ALU.mult, op1=ALU.add)
                            ins.then_inc(s_tap if k < CONV - 1 else s_conv, 1)
                        if c[4]:
                            g = T - SUM_T
                            dve.wait_ge(s_tok, T + 1 + RING)
                            dve.tensor_tensor(sq[:, :, :], tok[:, h], tok[:, h], ALU.mult).then_inc(s_sq, 1)
                            dve.wait_ge(s_sq, g + 1)
                            dve.tensor_reduce(mem["ssq"][:, ds(g * NT, NT)], sq[:, :, :], AX, ALU.add).then_inc(s_ss, 1)
                by_class(dve, body)
                R = slice(0, 48)
                pre, mag, expo, onep = tok[R, 0].rearrange("p t c -> p (t c)"), cbuf[R, 0, 0:S], cbuf[R, 1, 0:S], \
                    sq[R, :, :].rearrange("p a b -> p (a b)")
                eqz, lnp, step, decay = tok[R, 1].rearrange("p t c -> p (t c)"), sil[R, 1, :], cacc[R, 0, :], cacc[R, 1, :]
                n = 0

                def done(ins):
                    nonlocal n
                    n += 1
                    ins.then_inc(s_nv, 1)
                    dve.wait_ge(s_nv, n)

                dve.wait_ge(s_nmm, 1)
                dve.wait_ge(s_small, SMALL)
                dve.wait_ge(s_st[0], 16 * (IN_TILES // 2 + 2))
                dve.wait_ge(s_st[1], 16 * (IN_TILES // 2 + 1))
                done(dve.tensor_scalar(pre, ps[R, 0:2, :].rearrange("p b n -> p (b n)"), hcol[R, 0:1], None, ALU.add))
                done(dve.scalar_tensor_tensor(out=mag, in0=pre, scalar=-1.0, in1=pre, op0=ALU.mult, op1=ALU.max))
                dve.wait_ge(s_na, 2)
                done(dve.tensor_scalar(onep, expo, 1.0, None, ALU.add))
                done(dve.tensor_scalar(mag, onep, -1.0, None, ALU.add))
                done(dve.tensor_scalar(eqz, mag, 0.0, None, ALU.is_equal))
                done(dve.tensor_tensor(mag, mag, eqz, ALU.add))
                done(dve.reciprocal(mag, mag))
                dve.wait_ge(s_na, 3)
                done(dve.tensor_tensor(lnp, lnp, eqz, ALU.add))
                done(dve.tensor_tensor(lnp, lnp, mag, ALU.mult))
                done(dve.tensor_tensor(lnp, lnp, expo, ALU.mult))
                done(dve.scalar_tensor_tensor(out=step, in0=pre, scalar=0.0, in1=lnp, op0=ALU.max, op1=ALU.add))
                done(dve.tensor_scalar(hcol[R, 3:4], hcol[R, 2:3], -1.0, None, ALU.mult))
                done(dve.tensor_scalar(decay, step, hcol[R, 3:4], None, ALU.mult))


def phase_ssd(nc, A, mem):
    ps = mem["ps"]
    W = SSD_H * SSD_HD
    GW = W // SSD_G
    QH = 4
    D0 = 16
    with ExitStack() as ctx:
        ph = Phase(nc, ctx, "sd")
        sb, sem = ph.sb, ph.sem
        xs, y, z = (sb(n, [P, NT, W]) for n in ("x", "y", "z"))
        bc = sb("bc", [P, 4, 4, P])
        bt = sb("bt", [P, 4, SSD_G, SSD_N])
        state = sb("state", [P, 2, SSD_G, GW])
        faded = sb("faded", [P, 2, SSD_G, GW])
        xdt, xde = sb("xdt", [P, 2, SSD_H, SSD_HD]), sb("xde", [P, 2, SSD_H, SSD_HD])
        am, ed, sc = (sb(n, [P, 2, QH, P]) for n in ("am", "ed", "sc"))
        cbm = sb("cbm", [P, 2, SSD_G, P])
        part = sb("part", [P, 2, SSD_G, GW])
        drow = sb("drow", [P, SSD_H])
        wrow = sb("wrow", [P, W])
        sq = sb("sq", [P, GW])
        ss, rstd = sb("ss", [P, NT * SSD_G]), sb("rstd", [P, NT * SSD_G])
        eps = sb("eps", [P, 1])

        s_in = sem("in")
        s_ld = [sem(f"ld{k}") for k in range(4)]
        s_zero = sem("zero")
        s_y0 = sem("y0")
        s_xdt = sem("xdt_done")
        s_xde = sem("xde_done")
        s_cb = sem("cb")
        s_cbm = sem("cbm_done")
        s_am = sem("am_done")
        s_seg = sem("seg")
        s_exp = sem("exp")
        s_sc = sem("sc_done")
        s_diag = sem("diag")
        s_off = sem("off")
        s_part = sem("part_done")
        s_both = sem("both")
        s_y = sem("y_done")
        s_fade = sem("fade")
        s_new = sem("new")
        s_state = sem("state_done")
        s_gate = sem("gate")
        s_sq = sem("sq_done")
        s_rt = sem("rt")
        s_rs = sem("rs")
        s_nrm = sem("nrm")
        s_st = sem("st")

        scr = A["scr"].rearrange("(t p) n -> p t n", p=P)
        within = ("le", "ge")
        past = ("gt", "lt")

        def units(eng, body):
            with eng.Fori(0, NT // 2) as i:
                for u in range(4):
                    cc, d = u // 2, u % 2
                    body(i * 4 + u, u, d, i * 2 + cc if d == 0 else i * (-2) + (NT - 1 - cc), i)

        with nc.Block() as block:
            @block.sync
            def _(sp):
                sp.dma_start(xs[:, :, :], scr[:, :, XS0:XS0 + W]).then_inc(s_in, 16)
                sp.dma_start(drow[:, :], A["ssd_d"][0].partition_broadcast(P)).then_inc(s_in, 16)
                sp.dma_start(wrow[:, :], A["ssd_norm_w"][0].partition_broadcast(P)).then_inc(s_in, 16)
                sp.dma_start(z[:, :, :], scr[:, :, Z0:Z0 + W]).then_inc(s_in, 16)

                def load(n, u, d, t, i):
                    sp.wait_ge(s_diag, n * 4 + (D0 - 12))
                    sp.dma_start(bc[:, u], A["scr_t"].rearrange("(a p) s -> p a s", p=P)[:, :, ds(t * P, P)]
                                 ).then_inc(s_ld[u], 16)
                    sp.dma_start(bt[:, u], A["scr"][ds(t * P, P), BC0:BC0 + SSD_G * SSD_N].rearrange(
                        "p (g n) -> p g n", g=SSD_G)).then_inc(s_ld[u], 16)
                units(sp, load)
                for t in range(NT):
                    sp.wait_ge(s_nrm, 2 * (t + 1))
                    sp.dma_start(A["mix"][t * P:(t + 1) * P, 0:W], y[:, t, :]).then_inc(s_st, 16)
                sp.wait_ge(s_st, 16 * NT)

            @block.gpsimd
            def _(pool):
                pool.memset(eps[:, :], EPS)
                pool.memset(state[:, :, :, :], 0.0).then_inc(s_zero, 1)
                pool.sem_inc(s_xde, 2)
                pool.wait_ge(s_in, 64)

                def unit(n, u, d, t, i):
                    pool.wait_ge(s_diag, n * 4 + (D0 - 4))
                    stp = mem["step"][:, ds(t, 1), d * SSD_H:(d + 1) * SSD_H].rearrange("p o h -> p (o h)")
                    out = mem["eout"][:, ds(t, 1), d * SSD_H:(d + 1) * SSD_H].rearrange("p o h -> p (o h)")
                    tot = mem["etot"][:, ds(t, 1), d * SSD_H:(d + 1) * SSD_H].rearrange("p o h -> p (o h)")
                    wide = [P, SSD_H, SSD_HD]
                    pool.tensor_tensor(xdt[:, d], xs[:, ds(t, 1), :].rearrange("p o (h c) -> p (o h) c", h=SSD_H),
                                       stp.unsqueeze(2).broadcast_to(wide), ALU.mult).then_inc(s_xdt, 1)
                    pool.wait_ge(s_new, n * 2 + 2)
                    pool.wait_ge(s_xdt, n + 1)
                    pool.tensor_tensor(xde[:, d], xdt[:, d], out.unsqueeze(2).broadcast_to(wide),
                                       ALU.mult).then_inc(s_xde, 1)
                    for g in range(SSD_G):
                        pool.wait_ge(s_state, n * 2 + (g + 1))
                        pool.tensor_tensor(faded[:, d, g, :].rearrange("p (h c) -> p h c", c=SSD_HD),
                                           state[:, d, g, :].rearrange("p (h c) -> p h c", c=SSD_HD),
                                           tot[:, g * SSD_GH:(g + 1) * SSD_GH].unsqueeze(2).broadcast_to(
                                               [P, SSD_GH, SSD_HD]), ALU.mult).then_inc(s_fade, 1)
                units(pool, unit)

            @block.tensor
            def _(pe):
                pe.sem_inc(s_seg, 2)
                pe.sem_inc(s_diag, D0)
                pe.sem_inc(s_new, 4)
                pe.wait_ge(s_zero, 1)

                def unit(n, u, d, t, i):
                    pe.wait_ge(s_ld[u], i * 32 + 32)
                    pe.wait_ge(s_cbm, n + 1)
                    for g in range(SSD_G):
                        last = pe.matmul(ps[:, 0, g * P:(g + 1) * P], bc[:, u, g, :], bc[:, u, 2 + g, :],
                                         start=True, stop=True)
                    last.then_inc(s_cb, 1)

                    def seg(q):
                        Q = n * 4 + q
                        pe.wait_ge(s_am, Q + 1)
                        pe.wait_ge(s_exp, Q + 1)
                        pe.matmul(ps[:, 1 + q % 2, :], mem[past[d]][:, :], am[:, q % 2].rearrange("p h l -> p (h l)"),
                                  start=True, stop=True).then_inc(s_seg, 1)

                    def off(g):
                        pe.wait_ge(s_part, n * 2 + (g + 1))
                        pe.wait_ge(s_state, n * 2 + (g + 1))
                        pe.matmul(ps[:, 5 + g, :], bc[:, u, 2 + g, :], state[:, d, g, :],
                                  start=True, stop=True).then_inc(s_off, 1)

                    def diag(q):
                        Q = n * 4 + q
                        pe.wait_ge(s_sc, Q + 1 + 2)
                        if q == 0:
                            pe.wait_ge(s_xdt, n + 1)
                        if q % 2 == 0:
                            pe.wait_ge(s_both, n * 2 + (q // 2 + 1))
                        for k in range(QH):
                            h = q * QH + k
                            last = pe.matmul(ps[:, 3 + q // 2, (h % 8) * SSD_HD:(h % 8 + 1) * SSD_HD],
                                             sc[:, q % 2, k, :], xdt[:, d, h, :], start=True, stop=True)
                        last.then_inc(s_diag, 1)

                    def new(g):
                        if g == 0:
                            pe.wait_ge(s_xde, n + 1 + 2)
                        pe.wait_ge(s_state, n * 2 + (g + 4))
                        pe.matmul(ps[:, 7, :], bt[:, u, g, :], xde[:, d].rearrange("p h c -> p (h c)")[:, g * GW:(g + 1) * GW],
                                  start=True, stop=True).then_inc(s_new, 1)

                    seg(0)
                    seg(1)
                    off(0)
                    off(1)
                    diag(0)
                    seg(2)
                    diag(1)
                    seg(3)
                    new(0)
                    diag(2)
                    new(1)
                    diag(3)
                units(pe, unit)

            @block.scalar
            def _(act):
                act.sem_inc(s_exp, 2)

                def unit(n, u, d, t, i):
                    def masks(q):
                        Q = n * 4 + q
                        act.wait_ge(s_seg, Q + 1)
                        for k in range(QH):
                            a = mem["dec"][:, ds(t, 1), d * SSD_H + q * QH + k:d * SSD_H + q * QH + k + 1]
                            last = act.activation(am[:, q % 2, k, :], mem[within[d]][:, :], ACT.Copy,
                                                  scale=a.rearrange("p o h -> p (o h)"))
                        last.then_inc(s_am, 1)

                    def exps(q):
                        Q = n * 4 + q
                        act.wait_ge(s_seg, Q + 1 + 2)
                        act.wait_ge(s_sc, Q + 1)
                        act.activation(ed[:, q % 2].rearrange("p h l -> p (h l)"), ps[:, 1 + q % 2, :],
                                       ACT.Exp).then_inc(s_exp, 1)
                    masks(0)
                    masks(1)
                    exps(0)
                    masks(2)
                    exps(1)
                    masks(3)
                    exps(2)
                    exps(3)
                units(act, unit)
                for t in range(NT):
                    act.wait_ge(s_gate, t + 1)
                    for g in range(SSD_G):
                        k = SSD_G * t + g
                        if k >= 1:
                            act.wait_ge(s_sq, k)
                        act.activation(sq[:, :], y[:, t, g * GW:(g + 1) * GW], ACT.Square,
                                       accum_out=ss[:, k:k + 1]).then_inc(s_sq, 1)
                act.wait_ge(s_sq, SSD_G * NT)
                act.activation(rstd[:, :], ss[:, :], ACT.Sqrt, bias=eps[:, 0:1], scale=1.0 / GW).then_inc(s_rt, 1)

            @block.vector
            def _(dve):
                dve.sem_inc(s_cbm, 1)
                dve.sem_inc(s_part, 2)
                dve.sem_inc(s_sc, 2)
                dve.sem_inc(s_both, 2)
                dve.sem_inc(s_state, 4)
                dve.wait_ge(s_in, 64)
                for t in range(NT):
                    last = dve.tensor_tensor(y[:, t, :].rearrange("p (h c) -> p h c", c=SSD_HD),
                                             xs[:, t, :].rearrange("p (h c) -> p h c", c=SSD_HD),
                                             drow[:, :].unsqueeze(2).broadcast_to([P, SSD_H, SSD_HD]), ALU.mult)
                last.then_inc(s_y0, 1)
                dve.wait_ge(s_zero, 1)
                dve.wait_ge(s_y0, 1)

                def unit(n, u, d, t, i):
                    ein = mem["ein"][:, ds(t, 1), d * SSD_H:(d + 1) * SSD_H].rearrange("p o h -> p (o h)")
                    dve.wait_ge(s_cb, n + 1)
                    dve.tensor_tensor(cbm[:, d], ps[:, 0, 0:SSD_G * P].rearrange("p (g l) -> p g l", g=SSD_G),
                                      mem[within[d]][:, :].unsqueeze(1).broadcast_to([P, SSD_G, P]),
                                      ALU.mult).then_inc(s_cbm, 1)
                    dve.wait_ge(s_cbm, n + 2)

                    def score(q):
                        Q = n * 4 + q
                        dve.wait_ge(s_exp, Q + 1 + 2)
                        dve.wait_ge(s_diag, Q + (D0 - 1))
                        dve.tensor_tensor(sc[:, q % 2], ed[:, q % 2],
                                          cbm[:, d, q // 2, :].unsqueeze(1).broadcast_to([P, QH, P]),
                                          ALU.mult).then_inc(s_sc, 1)

                    def from_state(g):
                        dve.wait_ge(s_off, n * 2 + (g + 1))
                        dve.tensor_tensor(part[:, d, g, :].rearrange("p (h c) -> p h c", c=SSD_HD),
                                          ps[:, 5 + g, :].rearrange("p (h c) -> p h c", c=SSD_HD),
                                          ein[:, g * SSD_GH:(g + 1) * SSD_GH].unsqueeze(2).broadcast_to(
                                              [P, SSD_GH, SSD_HD]), ALU.mult).then_inc(s_part, 1)

                    def to_y(g):
                        dve.wait_ge(s_part, n * 2 + (g + 1 + 2))
                        dve.wait_ge(s_diag, n * 4 + (2 * g + 2 + D0))
                        dve.tensor_tensor(part[:, d, g, :], ps[:, 3 + g, :], part[:, d, g, :],
                                          ALU.add).then_inc(s_both, 1)
                        dve.wait_ge(s_both, n * 2 + (g + 1 + 2))
                        out = y[:, ds(t, 1), g * GW:(g + 1) * GW].rearrange("p o c -> p (o c)")
                        dve.tensor_tensor(out, out, part[:, d, g, :], ALU.add).then_inc(s_y, 1)

                    def to_state(g):
                        dve.wait_ge(s_fade, n * 2 + (g + 1))
                        dve.wait_ge(s_new, n * 2 + (g + 1 + 4))
                        dve.tensor_tensor(state[:, d, g, :], ps[:, 7, :], faded[:, d, g, :],
                                          ALU.add).then_inc(s_state, 1)
                    score(0)
                    score(1)
                    from_state(0)
                    from_state(1)
                    score(2)
                    to_y(0)
                    score(3)
                    to_state(0)
                    to_state(1)
                    to_y(1)
                units(dve, unit)
                dve.wait_ge(s_y, 4 * NT)
                for t in range(NT):
                    dve.tensor_tensor(y[:, t, :], y[:, t, :], z[:, t, :], ALU.mult).then_inc(s_gate, 1)
                dve.wait_ge(s_rt, 1)
                dve.reciprocal(rstd[:, :], rstd[:, :]).then_inc(s_rs, 1)
                dve.wait_ge(s_rs, 1)
                for t in range(NT):
                    for g in range(SSD_G):
                        k = SSD_G * t + g
                        dve.scalar_tensor_tensor(out=y[:, t, g * GW:(g + 1) * GW], in0=y[:, t, g * GW:(g + 1) * GW],
                                                 scalar=rstd[:, k:k + 1], in1=wrow[:, g * GW:(g + 1) * GW],
                                                 op0=ALU.mult, op1=ALU.mult).then_inc(s_nrm, 1)


def phase_gdn(nc, A, mem):
    ps, ident = mem["ps"], mem["ident"]
    H0 = 2 * SSD_H
    B = 32
    NB = P // B
    HB = B // 2
    UN = 2 * NT
    LN = 2 * (B - 1) + 1
    with ExitStack() as ctx:
        ph = Phase(nc, ctx, "gd")
        sb, sem = ph.sb, ph.sem
        kraw, qraw = sb("kraw", [P, NT, P]), sb("qraw", [P, NT, P])
        khat, qhat = sb("khat", [P, NT, P]), sb("qhat", [P, NT, P])
        v = sb("v", [P, 2, NT, P])
        kqt = sb("kqt", [P, 2, NT, 2, P])
        kdec = sb("kdec", [P, 2, 2, NT, P])
        qk = sb("qk", [P, 2, 2, NT, P])
        ut = sb("ut", [P, 2, 2, NT, P])
        nt = sb("nt", [P, 2, NT, P])
        nf = sb("nf", [P, NT, P])
        m5 = sb("m5", [P, 2, NT, P])
        x, xt = sb("x", [P, 2, NT, P]), sb("xt", [P, 2, NT, P])
        xs = sb("xs", [P, 2 * NT, 2, HB])
        y5 = sb("y5", [P, 2, NT, P])
        t64 = sb("t64", [P, NT, 64])
        y6 = sb("y6", [P, NT, 64])
        am, ed = sb("am", [P, 2, 4, P]), sb("ed", [P, 2, 4, P])
        low = sb("low", [P, B, B])
        inv, tmp, inv0 = sb("inv", [P, B, HB]), sb("tmp", [P, B, HB]), sb("inv0", [P, B, HB])
        mask5 = sb("mask5", [P, P])
        st = sb("st", [P, 2, P])
        rv, vn = sb("rv", [P, 2, P]), sb("vn", [P, 2, P])
        o = sb("o", [P, 2, NT, P])
        nein = sb("nein", [P, NT, 2 * GDN_H])
        rn = sb("rn", [P, 16, NT])
        eps6 = sb("eps6", [P, 1])

        s_own = sem("own")
        s_sp = sem("sp")
        s_pre = sem("pre")
        s_prv = sem("prv")
        s_kq = [sem("kq0"), sem("kq1")]
        s_v = [sem("v0"), sem("v1")]
        s_hat = sem("hat")
        s_pt = sem("pt")
        s_kqt = sem("kqt_done")
        s_kk = sem("kk")
        s_km = sem("km")
        s_am = sem("am_done")
        s_seg = sem("seg")
        s_exp = sem("exp")
        s_nt = sem("nt_done")
        s_qk = sem("qk_done")
        s_pnf = sem("pnf")
        s_nf = sem("nf_done")
        s_m5 = sem("m5_done")
        s_lo = sem("lo")
        s_li = sem("li")
        s_ln = sem("ln")
        s_go = sem("go")
        s_xi = sem("xi")
        s_x = sem("x_done")
        s_pxt = sem("pxt")
        s_xt = sem("xt_done")
        s_py5 = sem("py5")
        s_y5 = sem("y5_done")
        s_pu5 = sem("pu5")
        s_u5 = sem("u5_done")
        s_pt5 = sem("pt5")
        s_t5 = sem("t5_done")
        s_py6 = sem("py6")
        s_y6 = sem("y6_done")
        s_pu6 = sem("pu6")
        s_u6 = sem("u6_done")
        s_ks = sem("ks")
        s_rv = sem("rv_done")
        s_oq = sem("oq")
        s_tr = sem("tr")
        s_vn = sem("vn_done")
        s_c = sem("c")
        s_st = sem("st_done")
        s_o = sem("o_done")
        s_os = [sem("os0"), sem("os1")]

        scr = A["scr"].rearrange("(t p) n -> p t n", p=P)
        strict = ("lt", "gt")
        within = ("le", "ge")
        past = ("gt", "lt")
        low_d, inv_d = A["low"], A["inv"]
        quads = [(d, 4 * q) for d in range(2) for q in range(2)]

        def heads(eng, prepare, scan, finish):
            prepare(0, 0)
            scan(None, 1, 0)
            finish(0, 0)
            with eng.Fori(0, GDN_H // 2 - 1) as i:
                for u in range(2):
                    h = i * 2 + u
                    prepare(h + 1, 1 - u)
                    scan(h, u, h + 1)
                    finish(h + 1, 1 - u)
            prepare(GDN_H - 1, 1)
            scan(GDN_H - 2, 0, GDN_H - 1)
            finish(GDN_H - 1, 1)
            scan(GDN_H - 1, 1, None)

        def column(name, t, c):
            return mem[name][:, t, ds(c, 1)]

        with nc.Block() as block:
            @block.sync
            def _(sp):
                def load_kq(h, par):
                    sp.dma_start(kraw[:, :, :], scr[:, :, ds(h * P + K0, P)]).then_inc(s_kq[par], 16)
                    sp.dma_start(qraw[:, :, :], scr[:, :, ds(h * P + Q0, P)]).then_inc(s_kq[par], 16)

                def load_v(h, par):
                    sp.dma_start(v[:, par], scr[:, :, ds(h * P + V0, P)]).then_inc(s_v[par], 16)

                load_kq(0, 0)
                load_v(0, 0)
                load_v(1, 1)

                def prepare(h, par):
                    first = isinstance(h, int) and h == 0
                    last = isinstance(h, int) and h == GDN_H - 1
                    if not first:
                        sp.wait_ge(s_li, h * 32)
                    sp.wait_ge(s_nf, h * 2 + 2)
                    sp.wait_ge(s_nt, h * 4 + 4 + 2)
                    for b in range(NB):
                        for d, src in ((0, nf), (1, nt[:, 1])):
                            sp.dma_start(low_d[d * NT:(d + 1) * NT, b].rearrange("c r k -> r c k"),
                                         src[b * B:(b + 1) * B, :, b * B:(b + 1) * B]).then_inc(s_lo, 16)
                    if not first:
                        sp.wait_ge(s_ln, h * LN)
                        sp.sem_inc(s_sp, 1)
                    sp.wait_ge(s_lo, h * 128 + 128)
                    for half in range(2):
                        sp.dma_start(low[64 * half:64 * half + 64, :, :],
                                     low_d[:, :, :, :].rearrange("x b r k -> (x b) r k")).then_inc(s_li, 16)
                    if not last:
                        sp.wait_ge(s_hat, h * 4 + 2)
                        load_kq(h + 1, 1 - par)

                def scan(h, par, nxt):
                    pass

                def finish(h, par):
                    first = isinstance(h, int) and h == 0
                    last = isinstance(h, int) and h == GDN_H - 1
                    if not first:
                        sp.wait_ge(s_xi, h * 128)
                        sp.sem_inc(s_sp, 1)
                    sp.wait_ge(s_ln, h * LN + LN)
                    for half in range(2):
                        sp.dma_start(inv_d[:, :, half].rearrange("x b r m -> (x b) r m"),
                                     inv[64 * half:64 * half + 64, :, :]).then_inc(s_go, 16)
                    sp.wait_ge(s_go, h * 32 + 32)
                    if not first:
                        sp.wait_ge(s_x, h * 4)
                    for b in range(NB):
                        for half in range(2):
                            sp.dma_start(xs[b * B:(b + 1) * B, :, half, :],
                                         inv_d[:, b, half].rearrange("x r m -> r x m")).then_inc(s_xi, 16)
                    if not first and not last:
                        sp.wait_ge(s_c, h * 16 + 16)
                        load_v(h + 1, 1 - par)
                heads(sp, prepare, scan, finish)

            @block.gpsimd
            def _(pool):
                pool.memset(eps6[:, :], 1e-6)
                pool.memset(inv0[:, :, :], 0.0)
                pool.memset(mask5[:, :], 0.0)
                pool.memset(x[:, :, :, :], 0.0).then_inc(s_pre, 1)
                pool.wait_ge(s_pre, 1)
                for half in range(2):
                    q = slice(64 * half, 64 * half + 64)
                    pool.affine_select(out=inv0[q, :, :], in_=inv0[q, :, :], compare_op=ALU.not_equal, fill=1.0,
                                       base=-half, pattern=[[1, B], [-2, HB]], channel_multiplier=0).then_inc(s_pre, 1)
                    pool.wait_ge(s_pre, 2 + half)
                for b in range(NB):
                    c = (b ^ 1) * B
                    pool.memset(mask5[b * B:(b + 1) * B, c:c + B], 1.0).then_inc(s_pre, 1)
                pool.wait_ge(s_pre, 7)

                def prepare(h, par):
                    first = isinstance(h, int) and h == 0
                    pool.wait_ge(s_kq[par], (h - par) * 16 + 32)
                    if not first:
                        pool.wait_ge(s_pt, h * 4)
                        pool.wait_ge(s_c, h * 16)
                    rk = rn[:, ds(h + 8, 1), :].rearrange("p o t -> p (o t)").unsqueeze(2).broadcast_to([P, NT, P])
                    rq = rn[:, ds(h, 1), :].rearrange("p o t -> p (o t)").unsqueeze(2).broadcast_to([P, NT, P])
                    pool.tensor_tensor(khat[:, :, :], kraw[:, :, :], rk, ALU.mult).then_inc(s_hat, 1)
                    pool.tensor_tensor(qhat[:, :, :], qraw[:, :, :], rq, ALU.mult).then_inc(s_hat, 1)
                    pool.wait_ge(s_hat, h * 4 + 2)
                    for d in range(2):
                        out = mem["eout"][:, :, ds(h + (H0 + d * GDN_H), 1)].broadcast_to([P, NT, P])
                        pool.tensor_tensor(kdec[:, par, d], khat[:, :, :], out, ALU.mult).then_inc(s_hat, 1)
                    for q, (d, c) in enumerate(quads):
                        pool.wait_ge(s_km, h * 4 + (c // 2 + 2))
                        pool.wait_ge(s_exp, h * 4 + (q + 1 + 2))
                        s = qk[:, par, d, c:c + 4, :]
                        pool.tensor_tensor(s, s, ed[:, q % 2], ALU.mult).then_inc(s_qk, 1)
                    pool.wait_ge(s_nt, h * 4 + 4 + 2)
                    if not first:
                        pool.wait_ge(s_py5, h * 4)
                    pool.tensor_tensor(m5[:, :, :, :].rearrange("p d t i -> p (d t) i"),
                                       nt[:, :, :, :].rearrange("p d t i -> p (d t) i"),
                                       mask5[:, :].unsqueeze(1).broadcast_to([P, 2 * NT, P]), ALU.mult).then_inc(s_m5, 1)

                pool.wait_ge(s_prv, 4)
                heads(pool, prepare, lambda *a: None, lambda *a: None)

            @block.tensor
            def _(pe):
                pe.sem_inc(s_seg, 2)
                pe.sem_inc(s_c, 16)

                def prepare(h, par):
                    first = isinstance(h, int) and h == 0
                    pe.wait_ge(s_hat, h * 4 + 2)
                    if not first:
                        pe.wait_ge(s_u6, h * 2)
                        pe.wait_ge(s_u5, h * 4)
                    for g in range(4):
                        src = khat if g < 2 else qhat
                        for k in range(4):
                            t = 4 * (g % 2) + k
                            last = pe.transpose(ps[:, 4 + g, k * P:(k + 1) * P], src[:, t, :], ident[:, :])
                        last.then_inc(s_pt, 1)
                    pe.wait_ge(s_kqt, h * 4 + 4)
                    for pair in range(4):
                        for k in range(2):
                            t = 2 * pair + k
                            last = pe.matmul(ps[:, 2 + pair, 256 * k:256 * k + 256], kqt[:, par, t, 0, :],
                                             kqt[:, par, t, :, :].rearrange("p a i -> p (a i)"), start=True, stop=True)
                        last.then_inc(s_kk, 1)
                    for q, (d, c) in enumerate(quads):
                        pe.wait_ge(s_am, h * 4 + (q + 1))
                        pe.wait_ge(s_exp, h * 4 + (q + 1))
                        pe.matmul(ps[:, q % 2, :], mem[past[d]][:, :], am[:, q % 2].rearrange("p t i -> p (t i)"),
                                  start=True, stop=True).then_inc(s_seg, 1)
                    for g in range(2):
                        pe.wait_ge(s_nt, h * 4 + (g + 1 + 2))
                        for k in range(4):
                            last = pe.transpose(ps[:, 6 + g, k * P:(k + 1) * P], nt[:, 0, 4 * g + k, :], ident[:, :])
                        last.then_inc(s_pnf, 1)

                def scan(h, par, nxt):
                    if h is None:
                        return
                    if nxt is not None:
                        pe.wait_ge(s_km, nxt * 4 + 4)
                        pe.wait_ge(s_nf, nxt * 2 + 2)
                    pe.wait_ge(s_u6, h * 2 + 2)
                    pe.wait_ge(s_u5, h * 4 + 4)
                    pe.wait_ge(s_qk, h * 4 + 4 + 2)
                    pe.wait_ge(s_hat, h * 4 + 4)
                    pe.wait_ge(s_v[par], (h - par) * 8 + 16)

                    def from_state(c, d):
                        t = c if d == 0 else NT - 1 - c
                        pe.wait_ge(s_st, h * 16 + (2 * (c - 1) + d + 1))
                        pe.wait_ge(s_oq, h * 14 + (2 * (c - 2) + d + 1)) if c >= 2 else None
                        pe.matmul(ps[:, 2 + d, 0:P], kqt[:, par, t, 0, :], st[:, d, :], start=True, stop=True)
                        pe.matmul(ps[:, 2 + d, P:2 * P], kqt[:, par, t, 1, :], st[:, d, :],
                                  start=True, stop=True).then_inc(s_ks, 1)

                    def solve(c, d):
                        t = c if d == 0 else NT - 1 - c
                        if c >= 1:
                            pe.wait_ge(s_rv, h * 14 + (2 * (c - 1) + d + 1))
                            pe.wait_ge(s_vn, h * 16 + (2 * (c - 1) + d + 1))
                        pe.matmul(ps[:, 4 + d, 0:P], ut[:, par, d, t, :], v[:, par, t, :] if c == 0 else rv[:, d, :],
                                  start=True, stop=True).then_inc(s_tr, 1)

                    def use(c, d):
                        t = c if d == 0 else NT - 1 - c
                        pe.wait_ge(s_vn, h * 16 + (2 * c + d + 1))
                        if c >= 1:
                            pe.wait_ge(s_o, h * 16 + (2 * (c - 1) + d + 1))
                        pe.matmul(ps[:, 6 + d, P:2 * P], kdec[:, par, d, t, :], vn[:, d, :], start=True, stop=True)
                        pe.matmul(ps[:, 6 + d, 0:P], qk[:, par, d, t, :], vn[:, d, :],
                                  start=True, stop=True).then_inc(s_c, 1)
                    for c in range(NT):
                        for d in range(2):
                            if c >= 1:
                                from_state(c, d)
                        for d in range(2):
                            solve(c, d)
                        for d in range(2):
                            use(c, d)

                def finish(h, par):
                    if not (isinstance(h, int) and h == 0):
                        pe.wait_ge(s_o, h * 16)
                        pe.wait_ge(s_st, h * 16)
                        pe.wait_ge(s_oq, h * 14)
                    pe.wait_ge(s_exp, h * 4 + 4 + 2)
                    pe.wait_ge(s_nf, h * 2 + 2)
                    pe.wait_ge(s_x, h * 4 + 4)
                    for q, (d, c) in enumerate(quads):
                        for k in range(4):
                            last = pe.transpose(ps[:, q, k * P:(k + 1) * P], x[:, d, c + k, :], ident[:, :])
                        last.then_inc(s_pxt, 1)
                    pe.wait_ge(s_m5, h + 1)
                    tm, um = (x, xt), (xt, x)
                    for q, (d, c) in enumerate(quads):
                        if d == 1:
                            pe.wait_ge(s_xt, h * 4 + (q + 1))
                        for k in range(4):
                            last = pe.matmul(ps[:, 4 + q, k * P:(k + 1) * P], m5[:, d, c + k, :], tm[d][:, d, c + k, :],
                                             start=True, stop=True)
                        last.then_inc(s_py5, 1)
                    pe.wait_ge(s_xt, h * 4 + 4)
                    for q, (d, c) in enumerate(quads):
                        pe.wait_ge(s_y5, h * 4 + (q + 1))
                        for k in range(4):
                            last = pe.matmul(ps[:, q, k * P:(k + 1) * P], y5[:, d, c + k, :], um[d][:, d, c + k, :],
                                             start=True, stop=True)
                        last.then_inc(s_pu5, 1)
                    pe.sem_inc(s_own, 1)
                    for d in range(2):
                        e = 64 * d
                        for t in range(NT):
                            last = pe.matmul(ps[e:e + 64, 4 + d, t * 64:(t + 1) * 64], um[d][:, d, t, e:e + 64],
                                             y5[:, d, t, e:e + 64], start=True, stop=True)
                        last.then_inc(s_pt5, 1)
                    for d in range(2):
                        e, f = 64 * d, 64 - 64 * d
                        pe.wait_ge(s_t5, h * 2 + (d + 1))
                        pe.sem_inc(s_own, 1)
                        for t in range(NT):
                            last = pe.matmul(ps[f:f + 64, 6 + d, t * 64:(t + 1) * 64], nt[e:e + 64, d, t, f:f + 64],
                                             t64[e:e + 64, t, :], start=True, stop=True)
                        last.then_inc(s_py6, 1)
                    pe.wait_ge(s_u5, h * 4 + 4)
                    for d in range(2):
                        e, f = 64 * d, 64 - 64 * d
                        pe.wait_ge(s_y6, h * 2 + (d + 1))
                        pe.sem_inc(s_own, 1)
                        for t in range(NT):
                            last = pe.matmul(ps[e:e + 64, 4 + d, t * 64:(t + 1) * 64], y6[f:f + 64, t, :],
                                             ut[f:f + 64, par, d, t, f:f + 64], start=True, stop=True)
                        last.then_inc(s_pu6, 1)
                heads(pe, prepare, scan, finish)

            @block.scalar
            def _(act):
                act.sem_inc(s_exp, 2)
                for q in range(2):
                    act.sem_inc(s_os[q], 16)
                act.wait_ge(s_pre, 7)
                act.activation(rn[:, :, :].rearrange("p a t -> p (a t)"), mem["ssq"][:, NT:17 * NT], ACT.Sqrt,
                               bias=eps6[:, 0:1]).then_inc(s_prv, 1)

                def prepare(h, par):
                    first = isinstance(h, int) and h == 0
                    if not first:
                        act.wait_ge(s_c, h * 16)
                    for g in range(4):
                        act.wait_ge(s_pt, h * 4 + (g + 1))
                        act.activation(kqt[:, par, 4 * (g % 2):4 * (g % 2) + 4, g // 2, :],
                                       ps[:, 4 + g, :].rearrange("p (t i) -> p t i", t=4), ACT.Copy).then_inc(s_kqt, 1)

                    def masks(q):
                        d, c = quads[q]
                        act.wait_ge(s_seg, h * 4 + (q + 1))
                        for k in range(4):
                            last = act.activation(am[:, q % 2, k, :], mem[within[d]][:, :], ACT.Copy,
                                                  scale=column("dec", c + k, h + (H0 + d * GDN_H)))
                        last.then_inc(s_am, 1)

                    def exps(q):
                        act.wait_ge(s_seg, h * 4 + (q + 1 + 2))
                        act.wait_ge(s_nt, h * 4 + (q + 1))
                        act.wait_ge(s_qk, h * 4 + (q + 1))
                        act.activation(ed[:, q % 2], ps[:, q % 2, :].rearrange("p (t i) -> p t i", t=4),
                                       ACT.Exp).then_inc(s_exp, 1)
                    masks(0)
                    masks(1)
                    exps(0)
                    masks(2)
                    exps(1)
                    masks(3)
                    exps(2)
                    exps(3)
                    if not first:
                        act.wait_ge(s_lo, h * 128)
                    for g in range(2):
                        act.wait_ge(s_pnf, h * 2 + (g + 1))
                        act.activation(nf[:, 4 * g:4 * g + 4, :], ps[:, 6 + g, :].rearrange("p (t i) -> p t i", t=4),
                                       ACT.Copy).then_inc(s_nf, 1)

                def scan(h, par, nxt):
                    if h is None:
                        return
                    for c in range(NT):
                        for d in range(2):
                            t = c if d == 0 else NT - 1 - c
                            act.wait_ge(s_tr, h * 16 + (2 * c + d + 1))
                            if c >= 1:
                                act.wait_ge(s_c, h * 16 + (2 * (c - 1) + d + 1 + 16))
                            act.activation(vn[:, d, :], ps[:, 4 + d, 0:P], ACT.Copy,
                                           scale=column("beta", t, h + d * GDN_H)).then_inc(s_vn, 1)
                    act.wait_ge(s_o, h * 16 + 16)
                    act.dma_start(A["mix"].rearrange("(t p) n -> p t n", p=P)[:, :, ds(h * P + D, P)], o[:, par]
                                  ).then_inc(s_os[par], 16)

                def finish(h, par):
                    first = isinstance(h, int) and h == 0
                    if not first:
                        act.wait_ge(s_pu6, h * 2)
                    act.wait_ge(s_xi, h * 128 + 128)
                    for b in range(NB):
                        q = slice(b * B, (b + 1) * B)
                        act.activation(x[q, :, :, b * B:(b + 1) * B].rearrange("p d t (m s) -> p (d t) s m", s=2),
                                       xs[q, :, :, :], ACT.Copy).then_inc(s_x, 1)
                    for q, (d, c) in enumerate(quads):
                        act.wait_ge(s_pxt, h * 4 + (q + 1))
                        act.activation(xt[:, d, c:c + 4, :], ps[:, q, :].rearrange("p (t i) -> p t i", t=4),
                                       ACT.Copy).then_inc(s_xt, 1)
                    for q, (d, c) in enumerate(quads):
                        act.wait_ge(s_py5, h * 4 + (q + 1))
                        act.activation(y5[:, d, c:c + 4, :], ps[:, 4 + q, :].rearrange("p (t i) -> p t i", t=4),
                                       ACT.Copy).then_inc(s_y5, 1)
                    for d in range(2):
                        f = slice(64 - 64 * d, 128 - 64 * d)
                        act.wait_ge(s_py6, h * 2 + (d + 1))
                        act.activation(y6[f, :, :], ps[f, 6 + d, :].rearrange("p (t i) -> p t i", t=NT),
                                       ACT.Copy).then_inc(s_y6, 1)
                    act.wait_ge(s_u5, h * 4 + 4)
                    for d in range(2):
                        e, f = slice(64 * d, 64 * d + 64), slice(64 - 64 * d, 128 - 64 * d)
                        act.wait_ge(s_pu6, h * 2 + (d + 1))
                        act.activation(ut[e, par, d, :, f], ps[e, 4 + d, :].rearrange("p (t i) -> p t i", t=NT),
                                       ACT.Copy, scale=-1.0).then_inc(s_u6, 1)
                heads(act, prepare, scan, finish)
                for q in range(2):
                    act.wait_ge(s_os[q], 16 * (GDN_H // 2 + 1))

            @block.vector
            def _(dve):
                dve.sem_inc(s_nt, 2)
                dve.sem_inc(s_qk, 2)
                dve.tensor_scalar(nein[:, :, :], mem["ein"][:, :, H0:], -1.0, None, ALU.mult).then_inc(s_prv, 1)
                dve.wait_ge(s_prv, 2)
                dve.reciprocal(rn[:, :, :], rn[:, :, :]).then_inc(s_prv, 1)
                dve.wait_ge(s_prv, 3)
                dve.tensor_scalar(rn[:, 0:8, :], rn[:, 0:8, :], GDN_D ** -0.5, None, ALU.mult).then_inc(s_prv, 1)
                dve.wait_ge(s_pre, 7)

                def prepare(h, par):
                    if not (isinstance(h, int) and h == 0):
                        dve.wait_ge(s_py6, h * 2)
                        dve.wait_ge(s_lo, h * 128)
                        dve.wait_ge(s_m5, h)
                        dve.wait_ge(s_c, h * 16)
                    for pair in range(4):
                        dve.wait_ge(s_kk, h * 4 + (pair + 1))
                        for d in range(2):
                            for k in range(2):
                                t = 2 * pair + k
                                dve.scalar_tensor_tensor(out=nt[:, d, t, :], in0=ps[:, 2 + pair, 256 * k:256 * k + P],
                                                         scalar=column("beta", t, h + d * GDN_H),
                                                         in1=mem[strict[d]][:, :], op0=ALU.mult, op1=ALU.mult)
                            last = dve.tensor_tensor(
                                qk[:, par, d, 2 * pair:2 * pair + 2, :],
                                ps[:, 2 + pair, :].rearrange("p (t a i) -> p t a i", t=2, a=2)[:, :, 1, :],
                                mem[within[d]][:, :].unsqueeze(1).broadcast_to([P, 2, P]), ALU.mult)
                        last.then_inc(s_km, 1)
                    dve.wait_ge(s_km, h * 4 + 4)
                    for q, (d, c) in enumerate(quads):
                        dve.wait_ge(s_exp, h * 4 + (q + 1 + 2))
                        dve.tensor_tensor(nt[:, d, c:c + 4, :], nt[:, d, c:c + 4, :], ed[:, q % 2],
                                          ALU.mult).then_inc(s_nt, 1)

                def substitution(h, first, count):
                    for s in range(first, min(first + count, LN)):
                        if s == 0:
                            dve.wait_ge(s_li, h * 32 + 32)
                            if not (isinstance(h, int) and h == 0):
                                dve.wait_ge(s_go, h * 32)
                            dve.tensor_copy(inv[:, :, :], inv0[:, :, :]).then_inc(s_ln, 1)
                            continue
                        k, w = (s - 1) // 2, (s - 1) // 4 + 1
                        rows, shape = slice(k + 1, B), [P, B - 1 - k, (s - 1) // 4 + 1]
                        dve.wait_ge(s_ln, h * LN + s)
                        if s % 2:
                            dve.tensor_tensor(tmp[:, rows, 0:w], low[:, rows, k:k + 1].broadcast_to(shape),
                                              inv[:, k:k + 1, 0:w].broadcast_to(shape), ALU.mult).then_inc(s_ln, 1)
                        else:
                            dve.tensor_tensor(inv[:, rows, 0:w], inv[:, rows, 0:w], tmp[:, rows, 0:w],
                                              ALU.subtract).then_inc(s_ln, 1)

                def scan(h, par, nxt):
                    if h is None:
                        substitution(nxt, 0, LN)
                        return
                    dve.wait_ge(s_os[par], (h - par) * 8 + 16)
                    dve.wait_ge(s_v[par], (h - par) * 8 + 16)
                    for c in range(NT):
                        for d in range(2):
                            t = c if d == 0 else NT - 1 - c
                            n14, n16 = h * 14 + (2 * (c - 1) + d), h * 16 + (2 * c + d)
                            ein = H0 + d * GDN_H
                            if c >= 1:
                                dve.wait_ge(s_ks, n14 + 1)
                                dve.wait_ge(s_tr, n16 - 1)
                                dve.scalar_tensor_tensor(out=rv[:, d, :], in0=ps[:, 2 + d, 0:P],
                                                         scalar=nein[:, t, ds(h + d * GDN_H, 1)], in1=v[:, par, t, :],
                                                         op0=ALU.mult, op1=ALU.add).then_inc(s_rv, 1)
                        for d in range(2):
                            t = c if d == 0 else NT - 1 - c
                            n16 = h * 16 + (2 * c + d)
                            if 1 <= c < NT // 2:
                                dve.tensor_scalar(o[:, par, t, :], ps[:, 2 + d, P:2 * P],
                                                  column("ein", t, h + (H0 + d * GDN_H)), None, ALU.mult).then_inc(s_oq, 1)
                            if c >= NT // 2:
                                dve.wait_ge(s_o, h * 16 + (2 * (NT - 1 - c) + (1 - d) + 1))
                                dve.scalar_tensor_tensor(out=o[:, par, t, :], in0=ps[:, 2 + d, P:2 * P],
                                                         scalar=column("ein", t, h + (H0 + d * GDN_H)),
                                                         in1=o[:, par, t, :], op0=ALU.mult, op1=ALU.add).then_inc(s_oq, 1)
                        if nxt is not None and c >= 1:
                            substitution(nxt, 9 * (c - 1), 9)
                        for d in range(2):
                            t = c if d == 0 else NT - 1 - c
                            n16 = h * 16 + (2 * c + d)
                            dve.wait_ge(s_c, n16 + 1 + 16)
                            if c == 0:
                                dve.tensor_copy(st[:, d, :], ps[:, 6 + d, P:2 * P]).then_inc(s_st, 1)
                                dve.tensor_copy(o[:, par, t, :], ps[:, 6 + d, 0:P]).then_inc(s_o, 1)
                            else:
                                dve.wait_ge(s_st, n16 - 1)
                                dve.scalar_tensor_tensor(out=st[:, d, :], in0=st[:, d, :],
                                                         scalar=column("etot", t, h + (H0 + d * GDN_H)),
                                                         in1=ps[:, 6 + d, P:2 * P], op0=ALU.mult, op1=ALU.add
                                                         ).then_inc(s_st, 1)
                                dve.wait_ge(s_oq, h * 14 + (2 * (c - 1) + d + 1))
                                dve.tensor_tensor(o[:, par, t, :], ps[:, 6 + d, 0:P], o[:, par, t, :],
                                                  ALU.add).then_inc(s_o, 1)

                def finish(h, par):
                    tm, um = (x, xt), (xt, x)
                    for q, (d, c) in enumerate(quads):
                        dve.wait_ge(s_pu5, h * 4 + (q + 1))
                        dve.tensor_tensor(ut[:, par, d, c:c + 4, :], um[d][:, d, c:c + 4, :],
                                          ps[:, q, :].rearrange("p (t i) -> p t i", t=4), ALU.subtract).then_inc(s_u5, 1)
                    for d in range(2):
                        e = slice(64 * d, 64 * d + 64)
                        dve.wait_ge(s_pt5, h * 2 + (d + 1))
                        dve.tensor_tensor(t64[e, :, :], tm[d][e, d, :, e],
                                          ps[e, 4 + d, :].rearrange("p (t i) -> p t i", t=NT),
                                          ALU.subtract).then_inc(s_t5, 1)
                heads(dve, prepare, scan, finish)


class LayerNorm:

    STEPS = NT + 4

    def __init__(self, ph, mem, gain, shift, out=None):
        self.ps, self.ident, self.acc, self.xh, self.xl = (mem[n] for n in ("ps", "ident", "acc", "xh", "xl"))
        self.out = out
        self.gain, self.shift = ph.sb("ln_g", [P, D]), ph.sb("ln_b", [P, D])
        self.sources = gain, shift
        self.stats, self.mv = ph.sb("ln_stats", [P, 2, 2, 6]), ph.sb("ln_mv", [P, NT, 2])
        self.dev, self.rstd, self.off = ph.sb("ln_dev", [P, NT]), ph.sb("ln_rstd", [P, NT]), ph.sb("ln_off", [P, NT])
        self.eps = ph.sb("ln_eps", [P, 1])
        self.s_par = ph.sem("ln_par")
        self.s_eps = ph.sem("ln_eps")
        self.s_sta = ph.sem("ln_sta")
        self.s_var = ph.sem("ln_var")
        self.s_dev = ph.sem("ln_dev")
        self.s_rec = ph.sem("ln_rec")
        self.s_nrm = ph.sem("ln_nrm")
        self.s_gain = ph.sem("ln_gain")
        self.s_done = ph.sem("ln_done")
        self.s_turn = ph.sem("ln_turn")
        self.s_hi = ph.sem("ln_hi")
        self.s_lo = ph.sem("ln_lo")
        self.s_out = ph.sem("ln_out")

    def banks(self, t):
        return self.ps[:, 2 * (t % 2):2 * (t % 2) + 2, :].rearrange("p b (k c) -> p (b k) c", c=P)

    def load(self, sp):
        for dst, src in zip((self.gain, self.shift), self.sources):
            sp.dma_start(dst[:, :], src.partition_broadcast(P)).then_inc(self.s_par, 16)

    def prepare(self, pool):
        pool.memset(self.eps[:, :], EPS).then_inc(self.s_eps, 1)

    def vector(self, dve, i):
        if i < NT:
            for half in range(2):
                if i >= 2:
                    dve.wait_ge(self.s_var, i - 1)
                dve.bn_stats(self.stats[:, i % 2, half, :], self.acc[:, i, half * HALF:(half + 1) * HALF]
                             ).then_inc(self.s_sta, 1)
            dve.wait_ge(self.s_sta, 2 * i + 2)
            dve.bn_aggr(self.mv[:, i, :], self.stats[:, i % 2]).then_inc(self.s_var, 1)
        t = i - 1
        if 0 <= t < NT:
            dve.wait_ge(self.s_dev, t + 1)
            dve.reciprocal(self.rstd[:, t:t + 1], self.dev[:, t:t + 1]).then_inc(self.s_rec, 1)
            dve.wait_ge(self.s_rec, 2 * t + 1)
            dve.scalar_tensor_tensor(out=self.off[:, t:t + 1], in0=self.mv[:, t, 0:1], scalar=-1.0,
                                     in1=self.rstd[:, t:t + 1], op0=ALU.mult, op1=ALU.mult).then_inc(self.s_rec, 1)
        t = i - 2
        if 0 <= t < NT:
            dve.wait_ge(self.s_nrm, t + 1)
            dve.wait_ge(self.s_par, 32)
            dve.tensor_tensor(self.acc[:, t, :], self.acc[:, t, :], self.gain[:, :], ALU.mult).then_inc(self.s_gain, 1)
        t = i - 4
        if self.out is None and 0 <= t < NT:
            out = (slice(None), slice(None), slice(t * P, (t + 1) * P))
            dve.wait_ge(self.s_hi, t + 1)
            dve.tensor_tensor(self.xl[out], self.banks(t), self.xh[out].bitcast(F32), ALU.subtract).then_inc(self.s_lo, 1)

    def scalar(self, act, i):
        if i < NT:
            act.wait_ge(self.s_var, i + 1)
            act.wait_ge(self.s_eps, 1)
            act.activation(self.dev[:, i:i + 1], self.mv[:, i, 1:2], ACT.Sqrt, bias=self.eps[:, 0:1]
                           ).then_inc(self.s_dev, 1)
        t = i - 1
        if 0 <= t < NT:
            act.wait_ge(self.s_rec, 2 * t + 2)
            act.activation(self.acc[:, t, :], self.acc[:, t, :], ACT.Identity, scale=self.rstd[:, t:t + 1],
                           bias=self.off[:, t:t + 1]).then_inc(self.s_nrm, 1)
        t = i - 3
        if self.out is None and 0 <= t < NT:
            act.wait_ge(self.s_turn, t + 1)
            act.activation(self.xh[:, :, t * P:(t + 1) * P], self.banks(t), ACT.Copy).then_inc(self.s_hi, 1)

    def gpsimd(self, pool):
        pool.wait_ge(self.s_par, 32)
        for t in range(NT):
            pool.wait_ge(self.s_gain, t + 1)
            pool.tensor_tensor(self.acc[:, t, :], self.acc[:, t, :], self.shift[:, :], ALU.add).then_inc(self.s_done, 1)

    def tensor(self, pe, t):
        if self.out is not None:
            return
        pe.wait_ge(self.s_done, t + 1)
        if t >= 2:
            pe.wait_ge(self.s_lo, t - 1)
        for k in range(KT):
            last = pe.transpose(self.banks(t)[:, k, :], self.acc[:, t, k * P:(k + 1) * P], self.ident[:, :])
        last.then_inc(self.s_turn, 1)

    def store(self, sp):
        if self.out is not None:
            for t in range(NT):
                sp.wait_ge(self.s_done, t + 1)
                sp.dma_start(self.out[t * P:(t + 1) * P, :], self.acc[:, t, :]).then_inc(self.s_out, 16)
            sp.wait_ge(self.s_out, 16 * NT)


def phase_project(nc, A, mem, layer):
    ps, ident, acc, xh, xl = (mem[n] for n in ("ps", "ident", "acc", "xh", "xl"))
    mixed = layer == 0
    rows_d, w = (A["mix"], A["even_w_out"][0]) if mixed else (A["ao"], A["attn_w_o"][0])
    QK = HALF // P
    NQ = w.shape[0] // HALF
    GQ = NQ // 2 if mixed else NQ
    NR = NQ * NT
    GR = GQ * NT
    with ExitStack() as ctx:
        ph = Phase(nc, ctx, f"pr{layer}")
        sb, sem = ph.sb, ph.sem
        ln = LayerNorm(ph, mem, A["ln_mix_g"][layer], A["ln_mix_b"][layer])
        raw = sb("raw", [P, RING, QK, HALF])
        wh, wl = sb("wh", [P, RING, QK, HALF], F32R), sb("wl", [P, RING, QK, HALF], F32R)
        rows = sb("rows", [P, RING, HALF])

        s_res = sem("res")
        s_al = sem("al")
        s_row = [sem("row0"), sem("row1")]
        s_rows = sem("rows_done")
        s_turn = sem("turn")
        s_hi = sem("hi")
        s_lo = sem("lo")
        s_raw = [sem("raw0"), sem("raw1")]
        s_wh = sem("wh_done")
        s_wl = sem("wl_done")
        s_mm = sem("mm")
        s_ac = sem("ac")
        if mixed:
            orow, grow = sb("orow", [P, RING, HALF]), sb("grow", [P, RING, HALF])
            osq, ogw = sb("osq", [P, RING, HALF]), sb("ogw", [P, RING, HALF])
            sums, root_tile, rec = (sb(n, [P, RING, HALF // GDN_D]) for n in ("sums", "root", "rec"))
            gw = sb("gw", [P, GDN_D])
            s_gw = sem("gw")
            s_og = [sem("og0"), sem("og1")]
            s_osq = sem("osq_done")
            s_sum = sem("sum")
            s_root = sem("root_done")
            s_rec = sem("rec_done")
            s_pgw = sem("pgw")

        def by_head(a):
            return a.rearrange("p (h d) -> p h d", d=GDN_D)

        with nc.Block() as block:
            @block.sync
            def _(sp):
                def load_rows(n):
                    if n >= NR:
                        return
                    j, t = divmod(n, NT)
                    tokens = slice(t * P, (t + 1) * P)
                    if n < GR:
                        if n >= RING:
                            sp.wait_ge(s_turn, n - 1)
                        sp.dma_start(rows[:, n % 2], rows_d[tokens, j * HALF:(j + 1) * HALF]
                                     ).then_inc(s_row[n % 2], 16)
                        return
                    if n >= GR + RING:
                        sp.wait_ge(s_pgw, 2 * (n - GR - 1))
                        sp.wait_ge(s_osq, n - GR - 1)
                    c = (j - GQ) * HALF
                    sp.dma_start(orow[:, n % 2], rows_d[tokens, D + c:D + c + HALF]).then_inc(s_og[n % 2], 16)
                    sp.dma_start(grow[:, n % 2], A["scr"][tokens, G0 + c:G0 + c + HALF]).then_inc(s_og[n % 2], 16)

                def load_slab(s):
                    if s >= 2 * NQ:
                        return
                    if s >= RING:
                        sp.wait_ge(s_wl, s - 1)
                    sp.dma_start(raw[:, s % 2], w[(s // 2) * HALF:(s // 2 + 1) * HALF, (s % 2) * HALF:(s % 2 + 1) * HALF]
                                 .rearrange("(k p) n -> p k n", p=P)).then_inc(s_raw[s % 2], 16)
                load_rows(0)
                load_rows(1)
                load_slab(0)
                load_slab(1)
                for n in range(2, NT):
                    load_rows(n)
                if mixed:
                    for t in range(NT):
                        sp.dma_start(acc[:, t, :], A["x"][0, t * P:(t + 1) * P, :]).then_inc(s_res, 16)
                    sp.dma_start(gw[:, :], A["gdn_norm_w"][0].partition_broadcast(P)).then_inc(s_gw, 16)
                ln.load(sp)
                for j in range(NQ):
                    n = (j + 1) * NT
                    load_rows(n)
                    load_rows(n + 1)
                    load_slab(2 * j + 2)
                    for k in range(2, 6):
                        load_rows(n + k)
                    load_slab(2 * j + 3)
                    for k in range(6, NT):
                        load_rows(n + k)

            @block.gpsimd
            def _(pool):
                ln.prepare(pool)
                one = mem["ones"][:, 0:1].unsqueeze(1).broadcast_to([P, QK, HALF])

                def split(s):
                    if s >= 2 * NQ:
                        return
                    pool.wait_ge(s_raw[s % 2], 16 * (s // 2 + 1))
                    if s >= RING:
                        pool.wait_ge(s_mm, NT * (s - 1))
                    pool.tensor_tensor(wh[:, s % 2], raw[:, s % 2], one, ALU.mult).then_inc(s_wh, 1)
                    pool.wait_ge(s_wh, s + 1)
                    pool.tensor_tensor(wl[:, s % 2], raw[:, s % 2], wh[:, s % 2].bitcast(F32), ALU.subtract
                                       ).then_inc(s_wl, 1)

                def gate(n):
                    g = n - GR
                    if n >= NR or g < 0:
                        return
                    if g == 0:
                        pool.wait_ge(s_gw, 16)
                    pool.wait_ge(s_og[n % 2], 32 * (g // 2 + 1))
                    if g >= RING:
                        pool.wait_ge(s_rows, g - 1)
                    pool.tensor_tensor(by_head(ogw[:, n % 2]), by_head(grow[:, n % 2]),
                                       gw[:, :].unsqueeze(1).broadcast_to([P, HALF // GDN_D, GDN_D]), ALU.mult
                                       ).then_inc(s_pgw, 1)
                    pool.wait_ge(s_pgw, 2 * g + 1)
                    pool.tensor_tensor(ogw[:, n % 2], ogw[:, n % 2], orow[:, n % 2], ALU.mult).then_inc(s_pgw, 1)
                split(0)
                split(1)
                for j in range(NQ):
                    n = (j + 1) * NT
                    for k in range(2 if j else 0, NT):
                        gate(n + k)
                    split(2 * j + 2)
                    gate(n + NT)
                    gate(n + NT + 1)
                    split(2 * j + 3)
                ln.gpsimd(pool)

            @block.tensor
            def _(pe):
                def turn(n):
                    if n >= NR:
                        return
                    if n < GR:
                        pe.wait_ge(s_row[n % 2], 16 * (n // 2 + 1))
                    else:
                        pe.wait_ge(s_rows, n - GR + 1)
                    if n >= 4:
                        pe.wait_ge(s_lo, n - 3)
                    for k in range(QK):
                        last = pe.transpose(ps[:, n % 4, k * P:(k + 1) * P], rows[:, n % 2, k * P:(k + 1) * P], ident[:, :])
                    last.then_inc(s_turn, 1)
                for n in range(NT):
                    turn(n)
                for s in range(2 * NQ):
                    j, u = divmod(s, 2)
                    pe.wait_ge(s_wl, s + 1)
                    pe.wait_ge(s_lo, (j + 1) * NT)
                    if s == 2 * NQ - 1:
                        pe.wait_ge(s_hi, NR)
                    for t in range(NT):
                        m = s * NT + t
                        if m >= 4:
                            pe.wait_ge(s_ac, m - 3)
                        for k in range(QK):
                            f = QK * (j % 2) + k
                            last = product(pe, ps[:, 4 + t % 4, :], xh[:, f, t * P:(t + 1) * P], xl[:, f, t * P:(t + 1) * P],
                                           wh[:, u, k, :], wl[:, u, k, :], k == 0, k == QK - 1)
                        last.then_inc(s_mm, 1)
                        if u == 0:
                            turn((j + 1) * NT + t)
                        if s == 2 * NQ - 1 and t >= 4:
                            ln.tensor(pe, t - 4)
                for t in range(4, NT):
                    ln.tensor(pe, t)

            @block.scalar
            def _(act):
                def scale_residual(t):
                    if mixed:
                        act.wait_ge(s_res, 16 * NT)
                    act.activation(acc[:, t, :], acc[:, t, :], ACT.Copy, scale=ALPHA).then_inc(s_al, 1)

                def square(n):
                    g = n - GR
                    if n >= NR or g < 0:
                        return
                    act.wait_ge(s_og[n % 2], 32 * (g // 2 + 1))
                    if g >= RING:
                        act.wait_ge(s_sum, g - 1)
                    act.activation(osq[:, n % 2], orow[:, n % 2], ACT.Square).then_inc(s_osq, 1)

                def root(n):
                    g = n - GR
                    if n >= NR or g < 0:
                        return
                    act.wait_ge(s_sum, g + 1)
                    if g >= RING:
                        act.wait_ge(s_rec, g - 1)
                    act.wait_ge(ln.s_eps, 1)
                    act.activation(root_tile[:, n % 2], sums[:, n % 2], ACT.Sqrt, bias=ln.eps[:, 0:1], scale=1.0 / GDN_D
                                   ).then_inc(s_root, 1)
                for n in range(NR):
                    j, t = divmod(n, NT)
                    if j == 1:
                        scale_residual(t)
                    square(n + 1)
                    act.wait_ge(s_turn, n + 1)
                    act.activation(xh[:, QK * (j % 2):QK * (j % 2) + QK, t * P:(t + 1) * P],
                                   ps[:, n % 4, :].rearrange("p (k c) -> p k c", k=QK), ACT.Copy).then_inc(s_hi, 1)
                    root(n + 1)
                for i in range(LayerNorm.STEPS):
                    ln.scalar(act, i)

            @block.vector
            def _(dve):
                def low(n):
                    if n >= NR:
                        return
                    j, t = divmod(n, NT)
                    out = (slice(None), slice(QK * (j % 2), QK * (j % 2) + QK), slice(t * P, (t + 1) * P))
                    dve.wait_ge(s_hi, n + 1)
                    dve.tensor_tensor(xl[out], ps[:, n % 4, :].rearrange("p (k c) -> p k c", k=QK),
                                      xh[out].bitcast(F32), ALU.subtract).then_inc(s_lo, 1)

                def sum_squares(n):
                    g = n - GR
                    if n >= NR or g < 0:
                        return
                    dve.wait_ge(s_osq, g + 1)
                    if g >= RING:
                        dve.wait_ge(s_root, g - 1)
                    dve.tensor_reduce(sums[:, n % 2], by_head(osq[:, n % 2]), AX, ALU.add).then_inc(s_sum, 1)

                def norm(n):
                    g = n - GR
                    if n >= NR or g < 0:
                        return
                    dve.wait_ge(s_root, g + 1)
                    dve.reciprocal(rec[:, n % 2], root_tile[:, n % 2]).then_inc(s_rec, 1)
                    dve.wait_ge(s_rec, g + 1)
                    dve.wait_ge(s_pgw, 2 * g + 2)
                    dve.wait_ge(s_turn, n - 1)
                    dve.tensor_tensor(by_head(rows[:, n % 2]), by_head(ogw[:, n % 2]),
                                      rec[:, n % 2].unsqueeze(2).broadcast_to([P, HALF // GDN_D, GDN_D]), ALU.mult
                                      ).then_inc(s_rows, 1)

                def add(m):
                    t, u = m % NT, (m // NT) % 2
                    if m < NT:
                        dve.wait_ge(s_al, t + 1)
                    dve.wait_ge(s_mm, m + 1)
                    if m >= 2 * NT:
                        dve.wait_ge(s_ac, m - 2 * NT + 1)
                    out = acc[:, t, u * HALF:(u + 1) * HALF]
                    dve.tensor_tensor(out, ps[:, 4 + t % 4, :], out, ALU.add).then_inc(s_ac, 1)
                for n in range(NT):
                    low(n)
                for s in range(2 * NQ):
                    for t in range(NT):
                        n = (s // 2 + 1) * NT + t
                        if s % 2 == 0 and t < NT - 1:
                            sum_squares(n + 1)
                        elif s % 2 and t == NT - 1:
                            sum_squares(n + 1)
                            norm(n + 1)
                        add(s * NT + t)
                        if s % 2 == 0:
                            low(n)
                            if t < NT - 1:
                                norm(n + 1)
                        if s == 2 * NQ - 1:
                            dve.wait_ge(s_ac, s * NT + t + 1)
                            ln.vector(dve, t)
                for i in range(NT, LayerNorm.STEPS):
                    ln.vector(dve, i)


def phase_mlp(nc, A, mem, layer, out=None):
    ps, acc, xh, xl = (mem[n] for n in ("ps", "acc", "xh", "xl"))
    w1, w2 = A["mlp_w1"][layer].rearrange("(k p) n -> p k n", p=P), A["mlp_w2"][layer].rearrange("(k p) n -> p k n", p=P)
    FK = HALF // P
    NF = w2.shape[1] // FK
    with ExitStack() as ctx:
        ph = Phase(nc, ctx, f"ml{layer}")
        sb, sem = ph.sb, ph.sem
        ln = LayerNorm(ph, mem, A["ln_ffn_g"][layer], A["ln_ffn_b"][layer], out)
        SIZE = KT * SLAB
        raw = sb("raw", [P, RING, SIZE])
        wh, wl = sb("wh", [P, RING, SIZE], F32R), sb("wl", [P, RING, SIZE], F32R)
        pos, sqr = sb("pos", [P, RING, HALF]), sb("sqr", [P, RING, HALF])
        hh, hl = sb("hh", [P, FK, S], F32R), sb("hl", [P, FK, S], F32R)

        s_al = sem("al")
        s_raw = [sem("raw0"), sem("raw1")]
        s_wh = sem("wh_done")
        s_wl = sem("wl_done")
        s_m1 = sem("m1")
        s_pos = sem("pos_done")
        s_sqr = sem("sqr_done")
        s_hh = sem("hh_done")
        s_hl = sem("hl_done")
        s_m2 = sem("m2")
        s_ac = sem("ac")

        def slabs(eng, body, first=0, count=NF):
            with eng.Fori(first, first + count) as q:
                for c in range(4):
                    body(q, c)

        def w1_tile(w, c, k, f):
            return w[:, c % 2, k * SLAB + f * P:k * SLAB + (f + 1) * P]

        def w2_tile(w, c, k):
            return w[:, c % 2, k * HALF:(k + 1) * HALF]

        with nc.Block() as block:
            @block.sync
            def _(sp):
                def load(q, c):
                    sp.wait_ge(s_wl, q * 4 + (c + 1))
                    if c < 2:
                        src = w1[:, :, ds(q * HALF + c * SLAB, SLAB)]
                        dst = raw[:, c % 2].rearrange("p (k n) -> p k n", k=KT)
                    else:
                        src = w2[:, ds(q * FK, FK), (c - 2) * HALF:(c - 1) * HALF]
                        dst = raw[:, c % 2].rearrange("p (k n) -> p k n", k=FK)
                    sp.dma_start(dst, src).then_inc(s_raw[c % 2], 16)
                load(0, 0)
                load(0, 1)
                ln.load(sp)
                load(0, 2)
                load(0, 3)
                slabs(sp, load, 1, NF - 1)
                ln.store(sp)

            @block.gpsimd
            def _(pool):
                ln.prepare(pool)
                pool.sem_inc(s_wl, RING)
                one = mem["ones"][:, 0:1].broadcast_to([P, SIZE])

                def split(q, c):
                    u = c % 2
                    pool.wait_ge(s_raw[u], q * 32 + (16 * (c // 2) + 16))
                    if c < 2:
                        pool.wait_ge(s_m2, q * 16 + 8 * (c + 1))
                    else:
                        pool.wait_ge(s_m1, q * 8 + 4 * (c - 1))
                    pool.tensor_tensor(wh[:, u], raw[:, u], one, ALU.mult).then_inc(s_wh, 1)
                    pool.wait_ge(s_wh, q * 4 + (c + 1))
                    pool.tensor_tensor(wl[:, u], raw[:, u], wh[:, u].bitcast(F32), ALU.subtract).then_inc(s_wl, 1)
                slabs(pool, split)
                ln.gpsimd(pool)

            @block.tensor
            def _(pe):
                pe.sem_inc(s_m2, 16)

                def multiply(q, c, norm=False):
                    pe.wait_ge(s_wl, q * 4 + (c + 1 + RING))
                    if c < 2:
                        for half in range(2):
                            for f in range(2):
                                e = 4 * c + 2 * half + f
                                pe.wait_ge(s_pos, q * 8 + (e + 1))
                                for k in range(KT):
                                    last = product(pe, ps[:, 2 * half + f, :], w1_tile(wh, c, k, f), w1_tile(wl, c, k, f),
                                                   xh[:, k, half * HALF:(half + 1) * HALF],
                                                   xl[:, k, half * HALF:(half + 1) * HALF], k == 0, k == KT - 1)
                                last.then_inc(s_m1, 1)
                        return
                    for t in range(NT):
                        if c == 2 and t % 4 == 0:
                            pe.wait_ge(s_hl, q * 8 + (6 + t // 2 + RING))
                        pe.wait_ge(s_ac, q * 16 + (8 * (c - 2) + t + 1))
                        for k in range(FK):
                            last = product(pe, ps[:, 4 + t % 4, :], hh[:, k, t * P:(t + 1) * P], hl[:, k, t * P:(t + 1) * P],
                                           w2_tile(wh, c, k), w2_tile(wl, c, k), k == 0, k == FK - 1)
                        last.then_inc(s_m2, 1)
                        if norm and t >= 4:
                            ln.tensor(pe, t - 4)
                slabs(pe, multiply, 0, NF - 1)
                for c in range(4):
                    multiply(NF - 1, c, c == 3)
                for t in range(4, NT):
                    ln.tensor(pe, t)

            @block.scalar
            def _(act):
                act.sem_inc(s_pos, 4)
                for t in range(NT):
                    act.activation(acc[:, t, :], acc[:, t, :], ACT.Copy, scale=ALPHA).then_inc(s_al, 1)

                def hidden(q, c):
                    if c >= 2:
                        return
                    for n in range(4):
                        e = 4 * c + n
                        act.wait_ge(s_m1, q * 8 + (e + 1))
                        act.activation(pos[:, n % 2, :], ps[:, n, :], ACT.Relu).then_inc(s_pos, 1)
                        act.wait_ge(s_hl, q * 8 + (e + 1))
                        act.wait_ge(s_pos, q * 8 + (e + 1 + 4))
                        act.activation(sqr[:, n % 2, :], pos[:, n % 2, :], ACT.Square).then_inc(s_sqr, 1)
                slabs(act, hidden)
                for i in range(LayerNorm.STEPS):
                    ln.scalar(act, i)

            @block.vector
            def _(dve):
                dve.sem_inc(s_hl, RING)
                dve.sem_inc(s_ac, 4)
                dve.wait_ge(s_al, NT)

                def work(q, c, norm=False):
                    if c < 2:
                        for n in range(4):
                            e = 4 * c + n
                            out = (slice(None), 2 * c + n % 2, slice((n // 2) * HALF, (n // 2 + 1) * HALF))
                            dve.wait_ge(s_sqr, q * 8 + (e + 1))
                            dve.tensor_copy(hh[out], sqr[:, n % 2, :]).then_inc(s_hh, 1)
                            dve.wait_ge(s_hh, q * 8 + (e + 1))
                            dve.tensor_tensor(hl[out], sqr[:, n % 2, :], hh[out].bitcast(F32), ALU.subtract
                                              ).then_inc(s_hl, 1)
                        return
                    for t in range(NT):
                        m = 8 * (c - 2) + t
                        if m == 0:
                            dve.wait_ge(s_ac, q * 16 + 4)
                        dve.wait_ge(s_m2, q * 16 + (m + 1 + 16))
                        out = acc[:, t, (c - 2) * HALF:(c - 1) * HALF]
                        dve.tensor_tensor(out, ps[:, 4 + t % 4, :], out, ALU.add).then_inc(s_ac, 1)
                        if norm:
                            dve.wait_ge(s_ac, q * 16 + (m + 1 + 4))
                            ln.vector(dve, t)
                slabs(dve, work, 0, NF - 1)
                for c in range(4):
                    work(NF - 1, c, c == 3)
                for i in range(NT, LayerNorm.STEPS):
                    ln.vector(dve, i)


def phase_attn(nc, A, mem):
    ps, ident, xh, xl = (mem[n] for n in ("ps", "ident", "xh", "xl"))
    HEADS, KV, HD = 16, 4, 64
    REP = HEADS // KV
    NB = NT
    BAND = 3
    W = BAND * P
    GW = REP * HD
    COL_K, COL_V = HEADS * HD, (HEADS + KV) * HD
    UNITS = 4
    FAR = -1e30
    with ExitStack() as ctx:
        ph = Phase(nc, ctx, "at")
        sb, sem = ph.sb, ph.sem
        raw = sb("raw", [P, KT, SLAB])
        wh, wl = sb("wh", [P, RING, KT, SLAB], F32R), sb("wl", [P, RING, KT, SLAB], F32R)
        kt = sb("kt", [P, 2, S])
        kx = sb("kx", [P, 2, S])
        qt = sb("qt", [P, RING, 2, S])
        vt = sb("vt", [P, NT, GW])
        near = sb("near", [P, BAND, P])
        slope = sb("slope", [P, HEADS])
        sink = sb("sink", [P, HEADS])
        bias = sb("bias", [P, REP, W])
        prob = sb("prob", [P, RING, REP, W])
        pt = sb("pt", [P, BAND, REP * P])
        top, ntop, lift, esink, den = (sb(n, [P, RING, REP]) for n in ("top", "ntop", "lift", "esink", "den"))
        rec = sb("rec", [P, RING, REP])
        rows = sb("rows", [P, RING, GW])

        s_raw = sem("raw")
        s_wh = sem("wh_done")
        s_wl = sem("wl_done")
        s_small = sem("small")
        s_near = sem("near_done")
        s_neg = sem("neg")
        s_m = sem("m")
        s_me = sem("me")
        s_mv = sem("mv")
        s_ve = sem("ve")
        s_kx = sem("kx_done")
        s_bias = sem("bias_done")
        s_s = sem("s")
        s_sb = sem("sb_done")
        s_max = sem("max")
        s_exp = sem("exp")
        s_es = sem("es_done")
        s_pt = sem("pt")
        s_pe = sem("pe")
        s_o = sem("o")
        s_den = sem("den_done")
        s_row = sem("row_done")
        s_st = [sem("st0"), sem("st1")]

        w = A["attn_w_qkv"][0].rearrange("(k p) n -> p k n", p=P)
        slab_cols = [COL_K, COL_V] + [g * GW for g in range(KV)]

        def key_blocks(n):
            return range(1 if n == 0 else 0, BAND - 1 if n == NB - 1 else BAND)

        def turned(b):
            g, n = divmod(b, NB)
            return g * (BAND * NB - 2) + (BAND * n - 1 if n else 0)

        def cols(n):
            return slice(key_blocks(n)[0] * P, (key_blocks(n)[-1] + 1) * P)

        LAG_E, LAG_T, LAG_V = 1, 2, 3
        STEPS = NB + LAG_V
        UNIT_STEPS = (0, 1, NB, NB + 1)

        with nc.Block() as block:
            @block.sync
            def _(sp):
                sp.dma_start(sink[:, :], A["attn_sink"][0].partition_broadcast(P)).then_inc(s_small, 16)
                def load(s):
                    if s:
                        sp.wait_ge(s_wl, s)
                    sp.dma_start(raw[:, :, :], w[:, :, slab_cols[s]:slab_cols[s] + SLAB]).then_inc(s_raw, 16)
                for s in range(len(slab_cols) - 1):
                    load(s)
                    if s == 2:
                        sp.wait_ge(s_me, UNITS)
                        for a, b in ((0, HD), (HD, 0)):
                            sp.dma_start(kx[a:a + HD, :, :], kt[b:b + HD, :, :]).then_inc(s_kx, 16)
                for b in range(KV * NB):
                    g, n = divmod(b, NB)
                    sp.wait_ge(s_row, b + 1)
                    sp.dma_start(A["ao"][n * P:(n + 1) * P, g * GW:(g + 1) * GW], rows[:, b % 2]).then_inc(s_st[b % 2], 16)
                    if b == 0:
                        load(len(slab_cols) - 1)
                for q in range(2):
                    sp.wait_ge(s_st[q], 16 * (KV * NB // 2))

            @block.gpsimd
            def _(pool):
                one = mem["ones"][:, 0:1].unsqueeze(1).broadcast_to([P, KT, SLAB])

                def split(s):
                    u = s % 2
                    pool.wait_ge(s_raw, 16 * (s + 1))
                    if s in (2, 3):
                        pool.wait_ge(s_m, UNITS) if s == 2 else pool.wait_ge(s_mv, NT)
                    elif s > 3:
                        pool.wait_ge(s_m, UNITS * (s - 2))
                    pool.tensor_tensor(wh[:, u], raw[:, :, :], one, ALU.mult).then_inc(s_wh, 1)
                    pool.wait_ge(s_wh, s + 1)
                    pool.tensor_tensor(wl[:, u], raw[:, :, :], wh[:, u].bitcast(F32), ALU.subtract).then_inc(s_wl, 1)

                def penalties(g):
                    if g:
                        pool.wait_ge(s_sb, g * NB)
                    for h in range(REP):
                        pool.tensor_tensor(bias[:, h, :], near[:, :, :].rearrange("p b k -> p (b k)"),
                                           slope[:, g * REP + h:g * REP + h + 1].broadcast_to([P, W]), ALU.mult
                                           ).then_inc(s_bias, 1)
                pool.iota(near[:, :, :], pattern=[[-P, BAND], [-1, P]], base=P, channel_multiplier=1,
                          allow_small_or_imprecise_dtypes=True).then_inc(s_near, 1)
                for h in range(HEADS):
                    pool.memset(slope[:, h:h + 1], 2.0 ** (-8.0 * (h + 1) / HEADS)).then_inc(s_near, 1)
                split(0)
                split(1)
                pool.wait_ge(s_neg, 1)
                for i, (base, sign) in enumerate(((0, 1), (2 * P, -1))):
                    pool.affine_select(out=near[:, :, :], in_=near[:, :, :], compare_op=ALU.is_ge, fill=FAR, base=base,
                                       pattern=[[sign * P, BAND], [sign, P]], channel_multiplier=-sign).then_inc(s_near, 1)
                    pool.wait_ge(s_near, HEADS + 2 + i)
                split(2)
                penalties(0)
                split(3)
                split(4)
                penalties(1)
                split(5)
                penalties(2)
                penalties(3)

            @block.tensor
            def _(pe):
                def unit(n):
                    if n >= UNITS * (KV + 1):
                        return
                    g, (f, half) = n // UNITS, divmod(n % UNITS, 2)
                    u = (g + 1) % 2 if g else 0
                    bank = n % 4 if n < 2 * UNITS else 6
                    if n % UNITS == 0:
                        pe.wait_ge(s_wl, g + 2 if g else 1)
                    if UNITS <= n < 2 * UNITS:
                        pe.wait_ge(s_me, n - 3)
                    if n > 2 * UNITS:
                        pe.wait_ge(s_me, n)
                    for k in range(KT):
                        last = product(pe, ps[:, bank, :], wh[:, u, k, f * P:(f + 1) * P], wl[:, u, k, f * P:(f + 1) * P],
                                       xh[:, k, half * HALF:(half + 1) * HALF], xl[:, k, half * HALF:(half + 1) * HALF],
                                       k == 0, k == KT - 1)
                    last.then_inc(s_m, 1)

                def scores(g, n):
                    b = g * NB + n
                    if n == 0:
                        pe.wait_ge(s_me, UNITS * (g + 2))
                        pe.wait_ge(s_kx, 32)
                        pe.wait_ge(s_ve, NT)
                    if b:
                        pe.wait_ge(s_sb, b)
                    keys = slice((n - 1 + key_blocks(n)[0]) * P, (n + key_blocks(n)[-1]) * P)
                    for h in range(REP):
                        e = h % 2
                        half = slice(e * HD, (e + 1) * HD)
                        k = kt if e == g % 2 else kx
                        last = pe.matmul(ps[:, h, cols(n)], qt[half, g % 2, h // 2, n * P:(n + 1) * P],
                                         k[half, g // 2, keys], start=True, stop=True)
                    last.then_inc(s_s, 1)

                def turn(g, n):
                    b = g * NB + n
                    pe.wait_ge(s_exp, REP * (b + 1))
                    for i, kb in enumerate(key_blocks(n)):
                        c = turned(b) + i
                        if c >= 2:
                            pe.wait_ge(s_pe, c - 1)
                        for h in range(REP):
                            last = pe.transpose(ps[:, 4 + c % 2, h * P:(h + 1) * P],
                                                prob[:, b % 2, h, kb * P:(kb + 1) * P], ident[:, :])
                        last.then_inc(s_pt, 1)

                def values(g, n):
                    b = g * NB + n
                    pe.wait_ge(s_pe, turned(b + 1))
                    if b:
                        pe.wait_ge(s_row, b)
                    blocks = key_blocks(n)
                    for h in range(REP):
                        for kb in blocks:
                            last = pe.matmul(ps[:, 7, h * HD:(h + 1) * HD], pt[:, kb, h * P:(h + 1) * P],
                                             vt[:, n - 1 + kb, g * HD:(g + 1) * HD], start=kb == blocks[0],
                                             stop=kb == blocks[-1])
                    last.then_inc(s_o, 1)

                for n in range(UNITS):
                    unit(n)
                pe.wait_ge(s_wl, 2)
                for t in range(NT):
                    if t >= 4:
                        pe.wait_ge(s_ve, t - 3)
                    for k in range(KT):
                        last = product(pe, ps[:, 4 + t % 4, 0:GW], xh[:, k, t * P:(t + 1) * P], xl[:, k, t * P:(t + 1) * P],
                                       wh[:, 1, k, :], wl[:, 1, k, :], k == 0, k == KT - 1)
                    last.then_inc(s_mv, 1)
                for n in range(UNITS, 2 * UNITS):
                    unit(n)
                for g in range(KV):
                    for i in range(STEPS):
                        if i < NB:
                            scores(g, i)
                        if i >= LAG_V:
                            values(g, i - LAG_V)
                        if LAG_T <= i < NB + LAG_T:
                            turn(g, i - LAG_T)
                        if i in UNIT_STEPS:
                            unit(UNITS * (g + 2) + UNIT_STEPS.index(i))

            @block.scalar
            def _(act):
                def unit_out(n):
                    if n >= UNITS * (KV + 1):
                        return
                    g, (f, half) = n // UNITS, divmod(n % UNITS, 2)
                    bank = n % 4 if n < 2 * UNITS else 6
                    out = kt[:, f] if g == 0 else qt[:, (g - 1) % 2, f]
                    act.wait_ge(s_m, n + 1)
                    act.activation(out[:, half * HALF:(half + 1) * HALF], ps[:, bank, :], ACT.Copy).then_inc(s_me, 1)

                def exponentials(g, n):
                    b = g * NB + n
                    act.wait_ge(s_max, 4 * b + 3)
                    if b >= RING:
                        act.wait_ge(s_den, 2 * (b - 1))
                    for h in range(REP):
                        act.activation(prob[:, b % 2, h, cols(n)], prob[:, b % 2, h, cols(n)], ACT.Exp,
                                       bias=ntop[:, b % 2, h:h + 1], accum_out=den[:, b % 2, h:h + 1]).then_inc(s_exp, 1)
                    act.wait_ge(s_max, 4 * b + 4)
                    act.activation(esink[:, b % 2], lift[:, b % 2], ACT.Exp).then_inc(s_es, 1)

                def turned_out(g, n):
                    b = g * NB + n
                    if b:
                        act.wait_ge(s_o, b)
                    for i, kb in enumerate(key_blocks(n)):
                        c = turned(b) + i
                        act.wait_ge(s_pt, c + 1)
                        act.activation(pt[:, kb, :], ps[:, 4 + c % 2, :], ACT.Copy).then_inc(s_pe, 1)
                for n in range(2 * UNITS):
                    unit_out(n)
                for g in range(KV):
                    for i in range(STEPS):
                        if LAG_E <= i < NB + LAG_E:
                            exponentials(g, i - LAG_E)
                        if LAG_T <= i < NB + LAG_T:
                            turned_out(g, i - LAG_T)
                        if i in UNIT_STEPS:
                            unit_out(UNITS * (g + 2) + UNIT_STEPS.index(i))

            @block.vector
            def _(dve):
                flat = near[:, :, :].rearrange("p b k -> p (b k)")
                dve.wait_ge(s_near, HEADS + 1)
                dve.scalar_tensor_tensor(out=flat, in0=flat, scalar=-1.0, in1=flat, op0=ALU.mult, op1=ALU.min
                                         ).then_inc(s_neg, 1)
                for t in range(NT):
                    dve.wait_ge(s_mv, t + 1)
                    dve.tensor_copy(vt[:, t, :], ps[:, 4 + t % 4, 0:GW]).then_inc(s_ve, 1)
                dve.wait_ge(s_small, 16)

                def softmax(g, n):
                    b = g * NB + n
                    u, heads = b % 2, slice(g * REP, (g + 1) * REP)
                    if n == 0:
                        dve.wait_ge(s_bias, REP * (g + 1))
                    dve.wait_ge(s_s, b + 1)
                    if b >= RING:
                        dve.wait_ge(s_pt, turned(b - 1))
                        dve.wait_ge(s_es, b - 1)
                    dve.scalar_tensor_tensor(out=prob[:, u, :, cols(n)], in0=ps[:, 0:REP, cols(n)], scalar=HD ** -0.5,
                                             in1=bias[:, :, cols(n)], op0=ALU.mult, op1=ALU.add).then_inc(s_sb, 1)
                    dve.wait_ge(s_sb, b + 1)
                    dve.tensor_reduce(top[:, u], prob[:, u, :, cols(n)], AX, ALU.max).then_inc(s_max, 1)
                    dve.wait_ge(s_max, 4 * b + 1)
                    dve.tensor_tensor(top[:, u], top[:, u], sink[:, heads], ALU.max).then_inc(s_max, 1)
                    dve.wait_ge(s_max, 4 * b + 2)
                    dve.tensor_scalar(ntop[:, u], top[:, u], -1.0, None, ALU.mult).then_inc(s_max, 1)
                    dve.tensor_tensor(lift[:, u], sink[:, heads], top[:, u], ALU.subtract).then_inc(s_max, 1)

                def denominators(g, n):
                    b = g * NB + n
                    u = b % 2
                    dve.wait_ge(s_es, b + 1)
                    dve.wait_ge(s_exp, REP * (b + 1))
                    if b >= RING:
                        dve.wait_ge(s_row, b - 1)
                    dve.tensor_tensor(rec[:, u], den[:, u], esink[:, u], ALU.add).then_inc(s_den, 1)
                    dve.wait_ge(s_den, 2 * b + 1)
                    dve.reciprocal(rec[:, u], rec[:, u]).then_inc(s_den, 1)

                def output(g, n):
                    b = g * NB + n
                    u = b % 2
                    dve.wait_ge(s_den, 2 * b + 2)
                    dve.wait_ge(s_o, b + 1)
                    if b >= RING:
                        dve.wait_ge(s_st[u], 16 * (b // 2))
                    dve.tensor_tensor(rows[:, u].rearrange("p (h d) -> p h d", h=REP),
                                      ps[:, 7, 0:GW].rearrange("p (h d) -> p h d", h=REP),
                                      rec[:, u].unsqueeze(2).broadcast_to([P, REP, HD]), ALU.mult).then_inc(s_row, 1)
                for g in range(KV):
                    for i in range(STEPS):
                        if LAG_T <= i < NB + LAG_T:
                            denominators(g, i - LAG_T)
                        if i < NB:
                            softmax(g, i)
                        if i >= LAG_V:
                            output(g, i - LAG_V)


def build(nc, A, out):
    with ExitStack() as ctx:
        mem = {"ps": ctx.enter_context(nc.psum_tensor("ps", [P, 8, HALF], F32))}
        for name in ("ident", "ones"):
            mem[name] = ctx.enter_context(nc.sbuf_tensor(name, [P, P], F32))
        for name, shape in (("scr", (S, SCR_COLS)),
                            ("scr_t", (4 * P, S)),
                            ("low", (2 * NT, 4, 32, 32)),
                            ("inv", (2 * NT, 4, 2, 32, 16)),
                            ("mix", (S, 2 * D)),
                            ("ao", (S, D))):
            A[name] = nc.dram_tensor(name, shape, F32, kind="Internal").ap()
        with ExitStack() as part:
            for name, shape in (("le", [P, P]), ("gt", [P, P]), ("ge", [P, P]), ("lt", [P, P]),
                                ("step", [P, NT, 2 * SSD_H]), ("beta", [P, NT, 2 * GDN_H]),
                                ("dec", [P, NT, 2 * DIR_H]), ("ein", [P, NT, 2 * DIR_H]),
                                ("eout", [P, NT, 2 * DIR_H]), ("etot", [P, NT, 2 * DIR_H]), ("ssq", [P, 24 * NT])):
                mem[name] = part.enter_context(nc.sbuf_tensor(name, shape, F32))
            for phase in (phase_masks, phase_in, phase_ssd, phase_gdn):
                phase(nc, A, mem)
        mem["acc"] = ctx.enter_context(nc.sbuf_tensor("acc", [P, NT, D], F32))
        for name in ("xh", "xl"):
            mem[name] = ctx.enter_context(nc.sbuf_tensor(name, [P, KT, S], F32R))
        phase_project(nc, A, mem, 0)
        phase_mlp(nc, A, mem, 0)
        phase_attn(nc, A, mem)
        phase_project(nc, A, mem, 1)
        phase_mlp(nc, A, mem, 1, out)


_INS = ["x", "even_w_in", "ssd_conv_w", "ssd_conv_b", "ssd_dt_bias", "ssd_a_log", "ssd_d", "ssd_norm_w", "gdn_conv_w",
        "gdn_dt_bias", "gdn_a_log", "gdn_norm_w", "even_w_out", "attn_w_qkv", "attn_sink", "attn_w_o", "ln_mix_g",
        "ln_mix_b", "mlp_w1", "mlp_w2", "ln_ffn_g", "ln_ffn_b"]


def kernel(**inputs):
    import numpy as _np
    import concourse.bacc as _bacc
    from concourse import mybir as _mybir
    from concourse.bass_utils import run_bass_kernel_spmd as _run

    nc = _bacc.Bacc("TRN2", target_bir_lowering=False, num_devices=1)
    arrays, args = {}, {}
    for name in _INS:
        a = _np.ascontiguousarray(inputs[name])
        arrays[f"in_{name}_dram"] = a
        args[name] = nc.dram_tensor(f"in_{name}_dram", a.shape, _mybir.dt.from_np(a.dtype), kind="ExternalInput").ap()
    out = nc.dram_tensor("out_0_dram", (1, S, D), _mybir.dt.float32, kind="ExternalOutput").ap()
    build(nc, args, out[0])
    r = _run(nc, [arrays], core_ids=[0])
    return r.results[0]["out_0_dram"]
```

```python
from contextlib import ExitStack

import concourse.bass as bass
from concourse import mybir

F32 = mybir.dt.float32
F32R = mybir.dt.float32r
ALU = mybir.AluOpType
ACT = mybir.ActivationFunctionType
AX = mybir.AxisListType.X
ds = bass.ds

P = 128
S = 1024
D = 1024
NT = S // P
KT = D // P
HALF = 512
CONV = 5
PAD = CONV // 2
EPS = 1e-5

SSD_H, SSD_HD, SSD_G, SSD_N = 16, 64, 2, 128
SSD_GH = SSD_H // SSD_G
GDN_H, GDN_D = 8, 128
DIR_H = SSD_H + GDN_H
COL_DT, COL_A, COL_B = 2560, 6688, 6704
IN_TILES = 52
Z0, XS0, BC0, Q0, K0, V0, G0 = (P * (1 + n) for n in (0, 8, 16, 20, 28, 36, 44))
SCR_COLS = P * (1 + IN_TILES)

ATTN_K = 1024
SLAB = 256
RING = 2

ALPHA = 4 ** 0.25


class Phase:

    MANY = 100
    used = []

    def __init__(self, nc, ctx, name):
        self.nc, self.ctx, self.name, self.sems = nc, ctx, name, []
        ctx.callback(self.clear)

    def sb(self, name, shape, dt=F32):
        return self.ctx.enter_context(self.nc.sbuf_tensor(f"{self.name}_{name}", shape, dt))

    def sem(self, name):
        self.sems.append(self.nc.alloc_semaphore(name=f"{self.name}_{name}"))
        return self.sems[-1]

    def clear(self):
        Phase.used = Phase.used + self.sems
        if len(Phase.used) > Phase.MANY:
            self.nc.clear_and_free_semaphores(Phase.used)
            self.nc.all_engine_barrier()
            Phase.used = []


def product(pe, out, wh, wl, xh, xl, first=True, last=True):
    pe.matmul(out, wh, xh, start=first, stop=False)
    pe.matmul(out, wh, xl, start=False, stop=False)
    return pe.matmul(out, wl, xh, start=False, stop=last)


def phase_masks(nc, A, mem):
    masks = {"le": (1, -1, 0), "gt": (-1, 1, -1), "ge": (-1, 1, 0), "lt": (1, -1, -1)}
    with ExitStack() as ctx:
        ph = Phase(nc, ctx, "mk")
        s_ones = ph.sem("ones")
        s_mask = ph.sem("mask")
        with nc.Block() as block:
            @block.gpsimd
            def _(pool):
                names = ["ident", "ones", *masks]
                for n in names:
                    last = pool.memset(mem[n][:, :], 0.0 if n == "ident" else 1.0)
                last.then_inc(s_ones, 1)
                pool.wait_ge(s_ones, 1)
                pool.affine_select(out=mem["ident"][:, :], in_=mem["ident"][:, :], compare_op=ALU.not_equal,
                                   fill=1.0, base=0, pattern=[[-1, P]], channel_multiplier=1).then_inc(s_mask, 1)
                for n, (col, row, base) in masks.items():
                    pool.affine_select(out=mem[n][:, :], in_=mem[n][:, :], compare_op=ALU.is_ge, fill=0.0,
                                       base=base, pattern=[[col, P]], channel_multiplier=row).then_inc(s_mask, 1)
                pool.wait_ge(s_mask, 5)


def phase_in(nc, A, mem):
    ps, ident = mem["ps"], mem["ident"]
    with ExitStack() as ctx:
        ph = Phase(nc, ctx, "in")
        sb, sem = ph.sb, ph.sem
        xh, xl = sb("xh", [P, KT, S], F32R), sb("xl", [P, KT, S], F32R)
        raw = sb("raw", [P, RING, KT, SLAB])
        wh, wl = sb("wh", [P, RING, KT, SLAB], F32R), sb("wl", [P, RING, KT, SLAB], F32R)
        xrow = sb("xrow", [P, RING, D])
        SC, GC = 12, 24
        cw_rows = sb("cw_rows", [P, 3, P])
        cw = sb("cw", [P, CONV * (SC + GC)])
        cb = sb("cb", [P, SC + GC])
        cbuf = sb("cbuf", [P, RING, S + 2 * PAD])
        cacc = sb("cacc", [P, RING, S])
        sil = sb("sil", [P, RING, S])
        tok = sb("tok", [P, RING, NT, P])
        sq = sb("sq", [P, NT, P])
        nraw = sb("nraw", [P, KT, P])
        nwh, nwl = sb("nwh", [P, KT, P], F32R), sb("nwl", [P, KT, P], F32R)
        narrow = sb("narrow", [P, 4, S])
        hcol = sb("hcol", [P, 4])

        s_x = [sem("x0"), sem("x1")]
        s_small = sem("small")
        s_zero = sem("zero")
        s_xt = sem("xt")
        s_xh = sem("xh_done")
        s_xl = sem("xl_done")
        s_cwt = sem("cwt")
        s_cw = sem("cw_done")
        s_raw = [sem("raw0"), sem("raw1")]
        s_wh = sem("wh_done")
        s_wl = sem("wl_done")
        s_mm = sem("mm")
        s_ev = sem("ev")
        s_tap = sem("tap")
        s_conv = sem("conv")
        s_sil = sem("sil_done")
        s_tr = sem("tr")
        s_tok = sem("tok_done")
        s_sq = sem("sq_done")
        s_ss = sem("ss_done")
        s_st = [sem("st0"), sem("st1")]
        s_stc = [sem("stc0"), sem("stc1")]
        s_nw = sem("nw")
        s_nmm = sem("nmm")
        s_na = sem("na")
        s_nv = sem("nv")
        s_nt = sem("nt")
        s_sum = sem("sum")

        CLASSES = [(0, 4, False, False, False), (1024, 4, True, False, False), (2048, 2, True, True, False),
                   (2592, 12, True, False, True), (5664, 4, False, False, False)]
        CONV_T, SUM_T = 8, 20
        SMALL = 10 * 16
        w_in = A["even_w_in"][0].rearrange("(k p) n -> p k n", p=P)
        scr = A["scr"].rearrange("(t p) n -> p t n", p=P)

        def by_class(eng, body, between=None):
            first = 0
            for c in CLASSES:
                if between:
                    between(c)
                with eng.Fori(0, c[1] // 2) as i:
                    for u in range(2):
                        body(c, i * 2 + (first + u), u, i * 2 + u)
                first += c[1]

        one = mem["ones"][:, 0:1].unsqueeze(1).broadcast_to([P, KT, SLAB])

        with nc.Block() as block:
            @block.sync
            def _(sp):
                for t in range(NT):
                    if t == RING:
                        sp.wait_ge(s_zero, 1)
                        for o, c, n in ((0, COL_DT, 32), (32, COL_A, 16), (64, COL_B, 16)):
                            sp.dma_start(nraw[:, :, o:o + n], w_in[:, :, c:c + n]).then_inc(s_small, 16)
                    if t >= RING:
                        sp.wait_ge(s_xt, 2 * (t - 1))
                    sp.dma_start(xrow[:, t % 2, :], A["x"][0, t * P:(t + 1) * P, :]).then_inc(s_x[t % 2], 16)

                def body(c, j, u, m):
                    sp.wait_ge(s_wl, j + 1)
                    sp.dma_start(raw[:, u], w_in[:, :, ds(m * SLAB + c[0], SLAB)]).then_inc(s_raw[u], 16)
                by_class(sp, body)

            @block.gpsimd
            def _(pool):
                pool.memset(nraw[:, :, :], 0.0)
                pool.memset(cb[:, :], 0.0)
                pool.memset(sil[:, 1, :], 0.0)
                pool.memset(cbuf[:, :, :], 0.0).then_inc(s_zero, 1)
                pool.sem_inc(s_wl, RING)
                pool.wait_ge(s_small, SMALL)
                pool.tensor_copy(nwh[:, :, :], nraw[:, :, :]).then_inc(s_nw, 1)
                pool.wait_ge(s_nw, 1)
                pool.tensor_tensor(nwl[:, :, :], nraw[:, :, :], nwh[:, :, :].bitcast(F32), ALU.subtract).then_inc(s_nw, 1)

                def body(c, j, u, m):
                    pool.wait_ge(s_raw[u], j * 8 + (16 - 8 * u))
                    pool.wait_ge(s_mm, j * 2 + 2)
                    pool.tensor_tensor(wh[:, u], raw[:, u], one, ALU.mult).then_inc(s_wh, 1)
                    pool.wait_ge(s_wh, j + 1)
                    pool.tensor_tensor(wl[:, u], raw[:, u], wh[:, u].bitcast(F32), ALU.subtract).then_inc(s_wl, 1)
                by_class(pool, body)

            @block.tensor
            def _(pe):
                for n in range(2 * NT):
                    t, q = n // 2, n % 2
                    pe.wait_ge(s_x[t % 2], 16 * (t // 2 + 1))
                    if n >= 4:
                        pe.wait_ge(s_xl, n - 3)
                    for k in range(4):
                        last = pe.transpose(ps[:, n % 4, k * P:(k + 1) * P],
                                            xrow[:, t % 2, (4 * q + k) * P:(4 * q + k + 1) * P], ident[:, :])
                    last.then_inc(s_xt, 1)
                pe.wait_ge(s_small, SMALL)
                pe.transpose(ps[:, 4, 0:CONV * SC], cw_rows[0:CONV * SC, 0, :], ident[0:CONV * SC, 0:CONV * SC])
                pe.transpose(ps[:, 4, CONV * SC:CONV * (SC + GC)], cw_rows[0:CONV * GC, 1, :],
                             ident[0:CONV * GC, 0:CONV * GC])
                pe.transpose(ps[:, 4, 256:256 + SC], cw_rows[0:SC, 2, :], ident[0:SC, 0:SC]).then_inc(s_cwt, 1)
                pe.wait_ge(s_xl, 2 * NT)
                pe.wait_ge(s_cw, 2)
                pe.wait_ge(s_zero, 1)
                pe.sem_inc(s_mm, 2 * RING)

                pe.wait_ge(s_nw, 2)
                for half in range(2):
                    for k in range(KT):
                        last = product(pe, ps[:, half, :], nwh[:, k, :], nwl[:, k, :],
                                       xh[:, k, half * HALF:(half + 1) * HALF],
                                       xl[:, k, half * HALF:(half + 1) * HALF], k == 0, k == KT - 1)
                last.then_inc(s_nmm, 1)
                pe.wait_ge(s_nv, 1)
                pe.wait_ge(s_na, 1)

                def between(c):
                    if c[0] != 1024:
                        return
                    pe.wait_ge(s_ev, CONV_T + RING)
                    pe.wait_ge(s_tok, CONV_T + RING)
                    pe.wait_ge(s_nv, 13)
                    pe.wait_ge(s_na, 4)
                    step, decay, beta = cacc[:, 0, :], cacc[:, 1, :], narrow[:, 0, :]
                    for t in range(NT):
                        pe.transpose(ps[:, 2, t * 32:(t + 1) * 32], step[0:32, t * P:(t + 1) * P], ident[0:32, 0:32])
                        pe.transpose(ps[:, 3, t * 48:(t + 1) * 48], decay[0:48, t * P:(t + 1) * P], ident[0:48, 0:48])
                        last = pe.transpose(ps[:, 7, t * 16:(t + 1) * 16], beta[64:80, t * P:(t + 1) * P],
                                            ident[64:80, 64:80])
                    last.then_inc(s_nt, 1)
                    pe.wait_ge(s_na, 7)
                    dec = mem["dec"]
                    for b, forward, backward in ((4, "le", "ge"), (5, "gt", "lt")):
                        out = ps[:, b, 0:NT * 48].rearrange("p (t c) -> p t c", c=48)
                        for c0, c1, m in ((0, 16, forward), (16, 32, backward), (32, 40, forward), (40, 48, backward)):
                            pe.matmul(out[:, :, c0:c1], mem[m][:, :], dec[:, :, c0:c1], start=True, stop=True)
                    pe.matmul(ps[:, 6, 0:NT * 48], mem["ones"][:, :], dec[:, :, :].rearrange("p t c -> p (t c)"),
                              start=True, stop=True).then_inc(s_sum, 1)
                    pe.wait_ge(s_na, 10)

                def turn(n, par):
                    pe.wait_ge(s_sil, n + 1)
                    pe.wait_ge(s_tok, n + 1)
                    for t in range(NT):
                        last = pe.transpose(ps[:, 4 + 2 * par + t // 4, (t % 4) * P:(t % 4 + 1) * P],
                                            sil[:, 1 - par, t * P:(t + 1) * P], ident[:, :])
                    last.then_inc(s_tr, 1)

                def body(c, j, u, m):
                    pe.wait_ge(s_wl, j + 1 + RING)
                    for h in range(2):
                        T = j * 2 + h
                        pe.wait_ge(s_ev, T + 1)
                        for half in range(2):
                            for k in range(KT):
                                last = product(pe, ps[:, 2 * h + half, :], wh[:, u, k, h * P:(h + 1) * P],
                                               wl[:, u, k, h * P:(h + 1) * P],
                                               xh[:, k, half * HALF:(half + 1) * HALF],
                                               xl[:, k, half * HALF:(half + 1) * HALF],
                                               k == 0, k == KT - 1)
                        last.then_inc(s_mm, 1)
                        turn(T, h)
                by_class(pe, body, between)
                turn(IN_TILES, 0)

            @block.scalar
            def _(act):
                for dst, src in ((cw_rows[0:CONV * SC, 0, :], A["ssd_conv_w"][0].rearrange("j (c p) -> (j c) p", p=P)),
                                 (cw_rows[0:CONV * GC, 1, :], A["gdn_conv_w"][0].rearrange("j (c p) -> (j c) p", p=P)),
                                 (cw_rows[0:SC, 2, :], A["ssd_conv_b"][0].rearrange("(c p) -> c p", p=P))):
                    act.dma_start(dst, src).then_inc(s_small, 16)
                for col, names in ((0, ("ssd_dt_bias", "gdn_dt_bias")), (1, ("ssd_a_log", "gdn_a_log"))):
                    for r, n in zip((0, 32), names):
                        src = A[n][0].rearrange("a (h o) -> (a h) o", o=1)
                        act.dma_start(hcol[r:r + src.shape[0], col:col + 1], src).then_inc(s_small, 16)
                for n in range(2 * NT):
                    t, q = n // 2, n % 2
                    act.wait_ge(s_xt, n + 1)
                    act.activation(xh[:, 4 * q:4 * q + 4, t * P:(t + 1) * P],
                                   ps[:, n % 4, :].rearrange("p (k c) -> p k c", k=4), ACT.Copy).then_inc(s_xh, 1)
                act.wait_ge(s_cwt, 1)
                act.wait_ge(s_zero, 1)
                act.activation(cw[:, :], ps[:, 4, 0:CONV * (SC + GC)], ACT.Copy).then_inc(s_cw, 1)
                act.activation(cb[:, 0:SC], ps[:, 4, 256:256 + SC], ACT.Copy).then_inc(s_cw, 1)
                act.sem_inc(s_ev, RING)
                act.sem_inc(s_tok, RING)
                act.sem_inc(s_sil, 1)
                for q in range(2):
                    act.sem_inc(s_st[q], 16)
                act.wait_ge(s_cw, 2)
                act.wait_ge(s_small, SMALL)

                act.wait_ge(s_nmm, 1)
                act.activation(narrow[64:80, 0, :], ps[64:80, 0:2, :].rearrange("p b n -> p (b n)"),
                               ACT.Sigmoid).then_inc(s_na, 1)
                act.activation(hcol[0:48, 2:3], hcol[0:48, 1:2], ACT.Exp).then_inc(s_na, 1)
                act.wait_ge(s_nv, 2)
                act.activation(narrow[0:48, 1, :], xrow[0:48, 1, :], ACT.Exp, scale=-1.0).then_inc(s_na, 1)
                act.wait_ge(s_nv, 3)
                act.activation(narrow[0:48, 2, :], sq[0:48, :, :].rearrange("p a b -> p (a b)"), ACT.Ln).then_inc(s_na, 1)

                def rows_out(n, par, stores, sums):
                    act.wait_ge(s_tr, n + 1)
                    if sums:
                        act.wait_ge(s_ss, n - SUM_T + 1)
                    act.wait_ge(s_st[par], stores)
                    act.activation(tok[:, par], ps[:, 4 + 2 * par:6 + 2 * par, :].rearrange("p b (t c) -> p (b t) c", c=P),
                                   ACT.Copy).then_inc(s_tok, 1)
                    act.wait_ge(s_tok, n + 1 + RING)
                    act.dma_start(scr[:, :, ds(n * P, P)], tok[:, par]).then_inc(s_st[par], 16)

                def between(c):
                    if c[0] == 1024:
                        act.wait_ge(s_nt, 1)
                        act.activation(mem["step"][:, :, :], ps[:, 2, 0:256].rearrange("p (t c) -> p t c", c=32),
                                       ACT.Copy).then_inc(s_na, 1)
                        act.activation(mem["beta"][:, :, :], ps[:, 7, 0:128].rearrange("p (t c) -> p t c", c=16),
                                       ACT.Copy).then_inc(s_na, 1)
                        act.activation(mem["dec"][:, :, :], ps[:, 3, 0:384].rearrange("p (t c) -> p t c", c=48),
                                       ACT.Copy).then_inc(s_na, 1)
                        act.wait_ge(s_sum, 1)
                        for b, n in ((4, "ein"), (5, "eout"), (6, "etot")):
                            act.activation(mem[n][:, :, :], ps[:, b, 0:384].rearrange("p (t c) -> p t c", c=48),
                                           ACT.Exp).then_inc(s_na, 1)
                    if c[0] == 2592:
                        for q in range(2):
                            act.wait_ge(s_stc[q], 32)
                    if c[0] == 5664:
                        act.wait_ge(s_ss, 24 + RING)

                def body(c, j, u, m):
                    for h in range(2):
                        T = j * 2 + h
                        act.wait_ge(s_mm, T + 1 + 2 * RING)
                        if c[2]:
                            act.wait_ge(s_conv, T - CONV_T + 1)
                        act.activation(cbuf[:, h, PAD:PAD + S], ps[:, 2 * h:2 * h + 2, :].rearrange("p b n -> p (b n)"),
                                       ACT.Copy).then_inc(s_ev, 1)
                        rows_out(T, h, j * 16 + 16, c[4])
                        if c[2]:
                            act.wait_ge(s_conv, T - CONV_T + 1 + RING)
                            if c[3] and u == 1:
                                act.wait_ge(s_stc[h], 16)
                            act.activation(sil[:, h, :], cacc[:, h, :], ACT.Silu,
                                           bias=cb[:, ds(T - CONV_T, 1)]).then_inc(s_sil, 1)
                        else:
                            act.wait_ge(s_ev, T + 1 + RING)
                            act.activation(sil[:, h, :], cbuf[:, h, PAD:PAD + S], ACT.Silu).then_inc(s_sil, 1)
                        if c[3]:
                            act.wait_ge(s_sil, T + 2)
                            act.dma_start(A["scr_t"][(2 * u + h) * P:(2 * u + h + 1) * P, :], sil[:, h, :]
                                          ).then_inc(s_stc[h], 16)
                by_class(act, body, between)
                rows_out(IN_TILES, 0, IN_TILES * 8 + 16, False)
                act.wait_ge(s_st[0], 16 * (IN_TILES // 2 + 2))
                act.wait_ge(s_st[1], 16 * (IN_TILES // 2 + 1))

            @block.vector
            def _(dve):
                for n in range(2 * NT):
                    t, q = n // 2, n % 2
                    out = (slice(None), slice(4 * q, 4 * q + 4), slice(t * P, (t + 1) * P))
                    dve.wait_ge(s_xh, n + 1)
                    dve.tensor_tensor(xl[out], ps[:, n % 4, :].rearrange("p (k c) -> p k c", k=4),
                                      xh[out].bitcast(F32), ALU.subtract).then_inc(s_xl, 1)
                dve.sem_inc(s_conv, RING)
                dve.sem_inc(s_ss, RING)
                R = slice(0, 48)
                pre, mag, expo, onep = xrow[R, 0, :], xrow[R, 1, :], narrow[R, 1, :], sq[R, :, :].rearrange("p a b -> p (a b)")
                eqz, lnp, step, decay = narrow[R, 3, :], narrow[R, 2, :], cacc[R, 0, :], cacc[R, 1, :]
                n = 0

                def done(ins):
                    nonlocal n
                    n += 1
                    ins.then_inc(s_nv, 1)
                    dve.wait_ge(s_nv, n)

                dve.wait_ge(s_nmm, 1)
                dve.wait_ge(s_small, SMALL)
                done(dve.tensor_scalar(pre, ps[R, 0:2, :].rearrange("p b n -> p (b n)"), hcol[R, 0:1], None, ALU.add))
                done(dve.scalar_tensor_tensor(out=mag, in0=pre, scalar=-1.0, in1=pre, op0=ALU.mult, op1=ALU.max))
                dve.wait_ge(s_na, 3)
                done(dve.tensor_scalar(onep, expo, 1.0, None, ALU.add))
                done(dve.tensor_scalar(mag, onep, -1.0, None, ALU.add))
                done(dve.tensor_scalar(eqz, mag, 0.0, None, ALU.is_equal))
                done(dve.tensor_tensor(mag, mag, eqz, ALU.add))
                done(dve.reciprocal(mag, mag))
                dve.wait_ge(s_na, 4)
                done(dve.tensor_tensor(lnp, lnp, eqz, ALU.add))
                done(dve.tensor_tensor(lnp, lnp, mag, ALU.mult))
                done(dve.tensor_tensor(lnp, lnp, expo, ALU.mult))
                done(dve.scalar_tensor_tensor(out=step, in0=pre, scalar=0.0, in1=lnp, op0=ALU.max, op1=ALU.add))
                done(dve.tensor_scalar(hcol[R, 3:4], hcol[R, 2:3], -1.0, None, ALU.mult))
                done(dve.tensor_scalar(decay, step, hcol[R, 3:4], None, ALU.mult))
                dve.wait_ge(s_nt, 1)
                dve.wait_ge(s_cw, 1)

                def body(c, j, u, m):
                    if not c[2]:
                        return
                    for h in range(2):
                        T = j * 2 + h
                        ct = T - CONV_T
                        off, st = (ct, SC) if c[0] < COL_DT else (ct + (CONV * SC - SC), GC)
                        dve.wait_ge(s_ev, T + 1 + RING)
                        dve.wait_ge(s_sil, T)
                        dve.tensor_scalar(cacc[:, h, :], cbuf[:, h, 0:S], cw[:, ds(off, 1)], None,
                                          ALU.mult).then_inc(s_tap, 1)
                        for k in range(1, CONV):
                            dve.wait_ge(s_tap, ct * (CONV - 1) + k)
                            ins = dve.scalar_tensor_tensor(out=cacc[:, h, :], in0=cbuf[:, h, k:k + S],
                                                           scalar=cw[:, ds(off + k * st, 1)], in1=cacc[:, h, :],
                                                           op0=ALU.mult, op1=ALU.add)
                            ins.then_inc(s_tap if k < CONV - 1 else s_conv, 1)
                        if c[4]:
                            g = T - SUM_T
                            dve.wait_ge(s_tok, T + 1 + RING)
                            dve.tensor_tensor(sq[:, :, :], tok[:, h], tok[:, h], ALU.mult).then_inc(s_sq, 1)
                            dve.wait_ge(s_sq, g + 1)
                            dve.tensor_reduce(mem["ssq"][:, ds(g * NT, NT)], sq[:, :, :], AX, ALU.add).then_inc(s_ss, 1)
                by_class(dve, body)


def phase_ssd(nc, A, mem):
    ps = mem["ps"]
    W = SSD_H * SSD_HD
    GW = W // SSD_G
    QH = 4
    D0 = 16
    with ExitStack() as ctx:
        ph = Phase(nc, ctx, "sd")
        sb, sem = ph.sb, ph.sem
        xs, y, z = (sb(n, [P, NT, W]) for n in ("x", "y", "z"))
        bc = sb("bc", [P, 4, 4, P])
        bt = sb("bt", [P, 4, SSD_G, SSD_N])
        state = sb("state", [P, 2, SSD_G, GW])
        faded = sb("faded", [P, 2, SSD_G, GW])
        xdt, xde = sb("xdt", [P, 2, SSD_H, SSD_HD]), sb("xde", [P, 2, SSD_H, SSD_HD])
        am, ed, sc = (sb(n, [P, 4, QH, P]) for n in ("am", "ed", "sc"))
        cbm = sb("cbm", [P, 2, SSD_G, P])
        part = sb("part", [P, 2, SSD_G, GW])
        drow = sb("drow", [P, SSD_H])
        wrow = sb("wrow", [P, W])
        sq = sb("sq", [P, GW])
        ss, rstd = sb("ss", [P, NT * SSD_G]), sb("rstd", [P, NT * SSD_G])
        eps = sb("eps", [P, 1])

        s_in = sem("in")
        s_x = sem("x")
        s_z = sem("z")
        s_ld = [sem(f"ld{k}") for k in range(4)]
        s_zero = sem("zero")
        s_y0 = sem("y0")
        s_xdt = sem("xdt_done")
        s_xde = sem("xde_done")
        s_cb = sem("cb")
        s_cbm = sem("cbm_done")
        s_am = sem("am_done")
        s_seg = sem("seg")
        s_exp = sem("exp")
        s_sc = sem("sc_done")
        s_diag = sem("diag")
        s_off = sem("off")
        s_part = sem("part_done")
        s_both = sem("both")
        s_y = sem("y_done")
        s_fade = sem("fade")
        s_new = sem("new")
        s_state = sem("state_done")
        s_gate = sem("gate")
        s_gate2 = sem("gate2")
        s_sq = sem("sq_done")
        s_rt = sem("rt")
        s_rs = sem("rs")
        s_nrm = sem("nrm")
        s_st = sem("st")

        scr = A["scr"].rearrange("(t p) n -> p t n", p=P)
        within = ("le", "ge")
        past = ("gt", "lt")

        DONE = (3, 4, 2, 5, 6, 1, 7, 0)
        POOLED = 6

        def chunk(u, i):
            return i * 2 + u // 2 if u % 2 == 0 else i * (-2) + (NT - 1 - u // 2)

        def units(eng, body):
            def turn(i):
                for u in range(4):
                    body(i * 4 + u, u, u % 2, chunk(u, i), i, isinstance(i, int) and u == 3)
            with eng.Fori(0, NT // 2 - 1) as i:
                turn(i)
            turn(NT // 2 - 1)

        with nc.Block() as block:
            @block.sync
            def _(sp):
                sp.dma_start(drow[:, :], A["ssd_d"][0].partition_broadcast(P)).then_inc(s_in, 16)
                for t in (0, NT - 1):
                    sp.dma_start(xs[:, t, :], A["scr"][t * P:(t + 1) * P, XS0:XS0 + W]).then_inc(s_in, 16)

                def load(n, u, d, t, i, last):
                    sp.wait_ge(s_diag, n * 4 + (D0 - 12))
                    sp.dma_start(bc[:, u], A["scr_t"].rearrange("(a p) s -> p a s", p=P)[:, :, ds(t * P, P)]
                                 ).then_inc(s_ld[u], 16)
                    sp.dma_start(bt[:, u], A["scr"][ds(t * P, P), BC0:BC0 + SSD_G * SSD_N].rearrange(
                        "p (g n) -> p g n", g=SSD_G)).then_inc(s_ld[u], 16)
                for u in range(2):
                    load(u, u, u, chunk(u, 0), 0, False)
                sp.dma_start(xs[:, 1:NT - 1, :], scr[:, 1:NT - 1, XS0:XS0 + W]).then_inc(s_x, 16)
                for u in range(2, 4):
                    load(u, u, u % 2, chunk(u, 0), 0, False)
                sp.dma_start(wrow[:, :], A["ssd_norm_w"][0].partition_broadcast(P)).then_inc(s_z, 16)
                sp.dma_start(z[:, :, :], scr[:, :, Z0:Z0 + W]).then_inc(s_z, 16)
                with sp.Fori(1, NT // 2) as i:
                    for u in range(4):
                        load(i * 4 + u, u, u % 2, chunk(u, i), i, False)
                for k, t in enumerate(DONE):
                    sp.wait_ge(s_nrm, 2 * (k + 1))
                    sp.dma_start(A["mix"][t * P:(t + 1) * P, 0:W], y[:, t, :]).then_inc(s_st, 16)
                sp.wait_ge(s_st, 16 * NT)

            @block.gpsimd
            def _(pool):
                pool.memset(eps[:, :], EPS)
                pool.memset(state[:, :, :, :], 0.0).then_inc(s_zero, 1)
                pool.sem_inc(s_xde, 2)
                pool.wait_ge(s_in, 48)

                def unit(n, u, d, t, i, last):
                    if u == 2:
                        pool.wait_ge(s_x, 16)
                    pool.wait_ge(s_diag, n * 4 + (D0 - 4))
                    stp = mem["step"][:, ds(t, 1), d * SSD_H:(d + 1) * SSD_H].rearrange("p o h -> p (o h)")
                    out = mem["eout"][:, ds(t, 1), d * SSD_H:(d + 1) * SSD_H].rearrange("p o h -> p (o h)")
                    tot = mem["etot"][:, ds(t, 1), d * SSD_H:(d + 1) * SSD_H].rearrange("p o h -> p (o h)")
                    wide = [P, SSD_H, SSD_HD]
                    pool.tensor_tensor(xdt[:, d], xs[:, ds(t, 1), :].rearrange("p o (h c) -> p (o h) c", h=SSD_H),
                                       stp.unsqueeze(2).broadcast_to(wide), ALU.mult).then_inc(s_xdt, 1)
                    pool.wait_ge(s_new, n * 2 + 2)
                    pool.wait_ge(s_xdt, n + 1)
                    pool.tensor_tensor(xde[:, d], xdt[:, d], out.unsqueeze(2).broadcast_to(wide),
                                       ALU.mult).then_inc(s_xde, 1)
                    for g in range(SSD_G):
                        pool.wait_ge(s_state, n * 2 + (g + 1))
                        pool.tensor_tensor(faded[:, d, g, :].rearrange("p (h c) -> p h c", c=SSD_HD),
                                           state[:, d, g, :].rearrange("p (h c) -> p h c", c=SSD_HD),
                                           tot[:, g * SSD_GH:(g + 1) * SSD_GH].unsqueeze(2).broadcast_to(
                                               [P, SSD_GH, SSD_HD]), ALU.mult).then_inc(s_fade, 1)
                    if isinstance(i, int):
                        if u == 0:
                            pool.wait_ge(s_z, 32)
                        for k in (2 * u, 2 * u + 1):
                            if k < POOLED:
                                t = DONE[k]
                                pool.wait_ge(s_y, 24 if k < 4 else 28)
                                pool.tensor_tensor(y[:, t, :], y[:, t, :], z[:, t, :], ALU.mult).then_inc(s_gate, 1)
                units(pool, unit)

            @block.tensor
            def _(pe):
                pe.sem_inc(s_seg, 4)
                pe.sem_inc(s_diag, D0)
                pe.sem_inc(s_new, 4)
                pe.wait_ge(s_zero, 1)

                def gram(n, u, i):
                    pe.wait_ge(s_ld[u], i * 32 + 32)
                    pe.wait_ge(s_cbm, n + 1)
                    for g in range(SSD_G):
                        last = pe.matmul(ps[:, 0, g * P:(g + 1) * P], bc[:, u, g, :], bc[:, u, 2 + g, :],
                                         start=True, stop=True)
                    last.then_inc(s_cb, 1)

                def seg(n, d, q):
                    Q = n * 4 + q
                    pe.wait_ge(s_am, Q + 1)
                    pe.wait_ge(s_exp, Q + 1)
                    pe.matmul(ps[:, 1 + q % 2, :], mem[past[d]][:, :], am[:, q].rearrange("p h l -> p (h l)"),
                              start=True, stop=True).then_inc(s_seg, 1)

                gram(0, 0, 0)
                seg(0, 0, 0)
                seg(0, 0, 1)

                def unit(n, u, d, t, i, last):
                    def off(g):
                        pe.wait_ge(s_part, n * 2 + (g + 1))
                        pe.wait_ge(s_state, n * 2 + (g + 1) if g else n * 2 + 4)
                        pe.matmul(ps[:, 5 + g, :], bc[:, u, 2 + g, :], state[:, d, g, :],
                                  start=True, stop=True).then_inc(s_off, 1)

                    def diag(q):
                        Q = n * 4 + q
                        pe.wait_ge(s_sc, Q + 1 + 4)
                        if q == 0:
                            pe.wait_ge(s_xdt, n + 1)
                        if q % 2 == 0:
                            pe.wait_ge(s_both, n * 2 + (q // 2 + 1))
                        for k in range(QH):
                            h = q * QH + k
                            ins = pe.matmul(ps[:, 3 + q // 2, (h % 8) * SSD_HD:(h % 8 + 1) * SSD_HD],
                                            sc[:, q, k, :], xdt[:, d, h, :], start=True, stop=True)
                        ins.then_inc(s_diag, 1)

                    def new(g):
                        if g == 0:
                            pe.wait_ge(s_xde, n + 1 + 2)
                            pe.wait_ge(s_state, n * 2 + 4)
                        else:
                            pe.wait_ge(s_part, n * 2 + 1 + 2)
                        pe.matmul(ps[:, 7 - 2 * g, :], bt[:, u, g, :], xde[:, d].rearrange("p h c -> p (h c)")[:, g * GW:(g + 1) * GW],
                                  start=True, stop=True).then_inc(s_new, 1)

                    off(0)
                    off(1)
                    diag(0)
                    seg(n, d, 2)
                    diag(1)
                    seg(n, d, 3)
                    new(0)
                    if not last:
                        gram(n + 1, (u + 1) % 4, i + (u + 1) // 4)
                    diag(2)
                    if not last:
                        seg(n + 1, 1 - d, 0)
                    new(1)
                    if not last:
                        seg(n + 1, 1 - d, 1)
                    diag(3)
                units(pe, unit)

            @block.scalar
            def _(act):
                act.sem_inc(s_exp, 2)

                def masks(n, u, i, q):
                    d, t = u % 2, chunk(u, i)
                    act.wait_ge(s_seg, n * 4 + (q + 1))
                    for k in range(QH):
                        a = mem["dec"][:, ds(t, 1), d * SSD_H + q * QH + k:d * SSD_H + q * QH + k + 1]
                        ins = act.activation(am[:, q, k, :], mem[within[d]][:, :], ACT.Copy,
                                             scale=a.rearrange("p o h -> p (o h)"))
                    ins.then_inc(s_am, 1)

                def squares(j):
                    t = DONE[j]
                    act.wait_ge(s_gate, j + 1) if j < POOLED else act.wait_ge(s_gate2, j + 1 - POOLED)
                    for g in range(SSD_G):
                        k = SSD_G * j + g
                        if k >= 1:
                            act.wait_ge(s_sq, k)
                        act.activation(sq[:, :], y[:, t, g * GW:(g + 1) * GW], ACT.Square,
                                       accum_out=ss[:, k:k + 1]).then_inc(s_sq, 1)
                    k = SSD_G * j
                    act.wait_ge(s_sq, k + SSD_G)
                    act.activation(rstd[:, k:k + SSD_G], ss[:, k:k + SSD_G], ACT.Sqrt, bias=eps[:, 0:1], scale=1.0 / GW
                                   ).then_inc(s_rt, 1)

                for q in range(4):
                    masks(0, 0, 0, q)

                def unit(n, u, d, t, i, last):
                    for q in range(4):
                        act.wait_ge(s_seg, n * 4 + (q + 1 + 4))
                        act.wait_ge(s_sc, n * 4 + (q + 1))
                        act.activation(ed[:, q].rearrange("p h l -> p (h l)"), ps[:, 1 + q % 2, :],
                                       ACT.Exp).then_inc(s_exp, 1)
                        if not last:
                            masks(n + 1, (u + 1) % 4, i + (u + 1) // 4, q)
                    if isinstance(i, int) and u >= 2:
                        squares(2 * u - 4)
                        squares(2 * u - 3)
                units(act, unit)
                for k in range(4, NT):
                    squares(k)

            @block.vector
            def _(dve):
                dve.sem_inc(s_cbm, 1)
                dve.sem_inc(s_part, 2)
                dve.sem_inc(s_sc, 4)
                dve.sem_inc(s_both, 2)
                dve.sem_inc(s_state, 4)
                def masked(n, d):
                    dve.wait_ge(s_cb, n + 1)
                    dve.tensor_tensor(cbm[:, d], ps[:, 0, 0:SSD_G * P].rearrange("p (g l) -> p g l", g=SSD_G),
                                      mem[within[d]][:, :].unsqueeze(1).broadcast_to([P, SSD_G, P]),
                                      ALU.mult).then_inc(s_cbm, 1)

                def score(n, d, q):
                    Q = n * 4 + q
                    dve.wait_ge(s_exp, Q + 1 + 2)
                    dve.wait_ge(s_diag, Q + (D0 - 3))
                    if q == 0:
                        dve.wait_ge(s_cbm, n + 2)
                    dve.tensor_tensor(sc[:, q], ed[:, q],
                                      cbm[:, d, q // 2, :].unsqueeze(1).broadcast_to([P, QH, P]),
                                      ALU.mult).then_inc(s_sc, 1)

                def normed(j):
                    t, k = DONE[j], SSD_G * j
                    dve.wait_ge(s_rt, j + 1)
                    dve.reciprocal(rstd[:, k:k + SSD_G], rstd[:, k:k + SSD_G]).then_inc(s_rs, 1)
                    dve.wait_ge(s_rs, j + 1)
                    dve.wait_ge(s_z, 32)
                    for g in range(SSD_G):
                        dve.scalar_tensor_tensor(out=y[:, t, g * GW:(g + 1) * GW], in0=y[:, t, g * GW:(g + 1) * GW],
                                                 scalar=rstd[:, k + g:k + g + 1], in1=wrow[:, g * GW:(g + 1) * GW],
                                                 op0=ALU.mult, op1=ALU.mult).then_inc(s_nrm, 1)

                def skip_term(t):
                    dve.tensor_tensor(y[:, t, :].rearrange("p (h c) -> p h c", c=SSD_HD),
                                      xs[:, t, :].rearrange("p (h c) -> p h c", c=SSD_HD),
                                      drow[:, :].unsqueeze(2).broadcast_to([P, SSD_H, SSD_HD]), ALU.mult).then_inc(s_y0, 1)

                dve.wait_ge(s_zero, 1)
                dve.wait_ge(s_in, 48)
                skip_term(0)
                skip_term(NT - 1)
                masked(0, 0)
                dve.wait_ge(s_x, 16)
                for t in range(1, NT - 1):
                    skip_term(t)
                dve.wait_ge(s_y0, NT)
                score(0, 0, 0)
                score(0, 0, 1)

                def unit(n, u, d, t, i, last):
                    ein = mem["ein"][:, ds(t, 1), d * SSD_H:(d + 1) * SSD_H].rearrange("p o h -> p (o h)")

                    def from_state(g):
                        dve.wait_ge(s_off, n * 2 + (g + 1))
                        dve.tensor_tensor(part[:, d, g, :].rearrange("p (h c) -> p h c", c=SSD_HD),
                                          ps[:, 5 + g, :].rearrange("p (h c) -> p h c", c=SSD_HD),
                                          ein[:, g * SSD_GH:(g + 1) * SSD_GH].unsqueeze(2).broadcast_to(
                                              [P, SSD_GH, SSD_HD]), ALU.mult).then_inc(s_part, 1)

                    def to_y(g):
                        dve.wait_ge(s_part, n * 2 + (g + 1 + 2))
                        dve.wait_ge(s_diag, n * 4 + (2 * g + 2 + D0))
                        dve.tensor_tensor(part[:, d, g, :], ps[:, 3 + g, :], part[:, d, g, :],
                                          ALU.add).then_inc(s_both, 1)
                        dve.wait_ge(s_both, n * 2 + (g + 1 + 2))
                        out = y[:, ds(t, 1), g * GW:(g + 1) * GW].rearrange("p o c -> p (o c)")
                        dve.tensor_tensor(out, out, part[:, d, g, :], ALU.add).then_inc(s_y, 1)

                    def to_state(g):
                        dve.wait_ge(s_fade, n * 2 + (g + 1))
                        dve.wait_ge(s_new, n * 2 + (g + 1 + 4))
                        dve.tensor_tensor(state[:, d, g, :], ps[:, 7 - 2 * g, :], faded[:, d, g, :],
                                          ALU.add).then_inc(s_state, 1)
                    from_state(0)
                    from_state(1)
                    score(n, d, 2)
                    to_y(0)
                    score(n, d, 3)
                    if not last:
                        masked(n + 1, 1 - d)
                    to_state(0)
                    to_state(1)
                    if not last:
                        score(n + 1, 1 - d, 0)
                        score(n + 1, 1 - d, 1)
                    to_y(1)
                    if isinstance(i, int) and u == 3:
                        normed(0)
                        normed(1)
                units(dve, unit)
                dve.wait_ge(s_y, 4 * NT)
                for k in range(POOLED, NT):
                    t = DONE[k]
                    dve.tensor_tensor(y[:, t, :], y[:, t, :], z[:, t, :], ALU.mult).then_inc(s_gate2, 1)
                for k in range(2, NT):
                    normed(k)


def phase_gdn(nc, A, mem):
    ps, ident = mem["ps"], mem["ident"]
    H0 = 2 * SSD_H
    B = 32
    NB = P // B
    HB = B // 2
    LN = 2 * (B - 1) + 1
    SLOTS = 3
    with ExitStack() as ctx:
        ph = Phase(nc, ctx, "gd")
        sb, sem = ph.sb, ph.sem
        kraw, qhat = sb("kraw", [P, NT, P]), sb("qhat", [P, NT, P])
        khat = sb("khat", [P, SLOTS, NT, P])
        v = sb("v", [P, SLOTS, NT, P])
        kqt = sb("kqt", [P, SLOTS, NT, 2, P])
        qk = sb("qk", [P, SLOTS, 2, NT, P])
        nt = sb("nt", [P, SLOTS, 2, NT, P])
        ut = sb("ut", [P, SLOTS, 2, NT, P])
        nf = sb("nf", [P, NT, P])
        low = nf[:, :, :].rearrange("p t j -> p (t j)").rearrange("p (r k) -> p r k", k=B)
        m5 = sb("m5", [P, 2, NT, P])
        y5 = m5
        x, xt = sb("x", [P, 2, NT, P]), sb("xt", [P, 2, NT, P])
        xs = sb("xs", [P, 2 * NT, 2, HB])
        t64 = sb("t64", [P, NT, 64])
        y6 = sb("y6", [P, NT, 64])
        am, ed = sb("am", [P, 2, 4, P]), sb("ed", [P, 2, 4, P])
        inv, tmp, inv0 = sb("inv", [P, B, HB]), sb("tmp", [P, B, HB]), sb("inv0", [P, B, HB])
        mask5 = sb("mask5", [P, P])
        st = sb("st", [P, 2, P])
        rv = sb("rv", [P, 2, P])
        vn = sb("vn", [P, 2, 2, P])
        o = sb("o", [P, SLOTS, NT, P])
        nein = sb("nein", [P, NT, 2 * GDN_H])
        bout = sb("bout", [P, NT, 2 * GDN_H])
        rn = sb("rn", [P, 16, NT])
        eps6 = sb("eps6", [P, 1])

        s_own = sem("own")
        s_sp = sem("sp")
        s_pre = sem("pre")
        s_prv = sem("prv")
        s_kq = sem("kq")
        s_v = [sem(f"v{n}") for n in range(SLOTS)]
        s_hat = sem("hat")
        s_pt = sem("pt")
        s_kqt = sem("kqt_done")
        s_kk = sem("kk")
        s_km = sem("km")
        s_am = sem("am_done")
        s_seg = sem("seg")
        s_exp = sem("exp")
        s_nt = sem("nt_done")
        s_qk = sem("qk_done")
        s_pnf = sem("pnf")
        s_nf = sem("nf_done")
        s_m5 = sem("m5_done")
        s_lo = sem("lo")
        s_li = sem("li")
        s_ln = sem("ln")
        s_go = sem("go")
        s_xi = sem("xi")
        s_x = sem("x_done")
        s_pxt = sem("pxt")
        s_xt = sem("xt_done")
        s_py5 = sem("py5")
        s_y5 = sem("y5_done")
        s_pu5 = sem("pu5")
        s_u5 = sem("u5_done")
        s_pt5 = sem("pt5")
        s_t5 = sem("t5_done")
        s_py6 = sem("py6")
        s_y6 = sem("y6_done")
        s_pu6 = sem("pu6")
        s_u6 = sem("u6_done")
        s_ks = sem("ks")
        s_rv = sem("rv_done")
        s_oq = sem("oq")
        s_tr = sem("tr")
        s_vn = sem("vn_done")
        s_c = sem("c")
        s_st = sem("st_done")
        s_o = sem("o_done")
        s_os = [sem(f"os{n}") for n in range(SLOTS)]

        scr = A["scr"].rearrange("(t p) n -> p t n", p=P)
        strict = ("lt", "gt")
        within = ("le", "ge")
        past = ("gt", "lt")
        low_d, inv_d = A["low"], A["inv"]
        quads = [(d, 4 * q) for d in range(2) for q in range(2)]

        def is_first(h):
            return isinstance(h, int) and h == 0

        def heads(eng, body):
            def at(h, r, turn):
                known = isinstance(h, int)
                def part(k):
                    return h + k if not known or 0 <= h + k < GDN_H else None
                body(part(2), part(1), part(0), (r + 2) % SLOTS, (r + 1) % SLOTS, r, turn)
            for h in range(-2, 0):
                at(h, h % SLOTS, 0)
            with eng.Fori(0, (GDN_H - 2) // SLOTS) as i:
                for r in range(SLOTS):
                    at(i * SLOTS + r, r, i)
            for h in range(GDN_H - 2, GDN_H):
                at(h, h % SLOTS, h // SLOTS)

        def slice_of(items, s, h):
            if h is not None:
                for n, item, *args in items:
                    if n == s:
                        item(*args)

        def column(name, t, c):
            return mem[name][:, t, ds(c, 1)]

        def unit(c, d):
            return c if d == 0 else NT - 1 - c

        with nc.Block() as block:
            @block.sync
            def _(sp):
                def load_kq(h):
                    sp.dma_start(kraw[:, :, :], scr[:, :, ds(h * P + K0, P)]).then_inc(s_kq, 16)
                    sp.dma_start(qhat[:, :, :], scr[:, :, ds(h * P + Q0, P)]).then_inc(s_kq, 16)

                load_kq(0)

                def body(hp, hf, hs, rp, rf, rs, turn):
                    if hp is not None:
                        sp.wait_ge(s_pt, hp * 4 + 4)
                        sp.sem_inc(s_sp, 1)
                        load_kq(hp + 1)
                        if not is_first(hp):
                            sp.wait_ge(s_li, hp * 32)
                            sp.sem_inc(s_sp, 1)
                        sp.wait_ge(s_nt, hp * 4 + 4 + 2)
                        sp.sem_inc(s_sp, 1)
                        sp.wait_ge(s_nf, hp * 2 + 2)
                        sp.sem_inc(s_sp, 1)
                        for b in range(NB):
                            for d, src in ((0, nf), (1, nt[:, rp, 1])):
                                sp.dma_start(low_d[d * NT:(d + 1) * NT, b].rearrange("c r k -> r c k"),
                                             src[b * B:(b + 1) * B, :, b * B:(b + 1) * B]).then_inc(s_lo, 16)
                        sp.wait_ge(s_lo, hp * 128 + 128)
                        sp.sem_inc(s_sp, 1)
                        for half in range(2):
                            sp.dma_start(low[64 * half:64 * half + 64, :, :],
                                         low_d[:, :, :, :].rearrange("x b r k -> (x b) r k")).then_inc(s_li, 16)
                        if not isinstance(hp, int):
                            sp.wait_ge(s_c, hp * 16 + (16 - 16 * SLOTS + 16))
                            sp.sem_inc(s_sp, 1)
                        sp.dma_start(v[:, rp], scr[:, :, ds(hp * P + V0, P)]).then_inc(s_v[rp], 16)
                        sp.wait_ge(s_ln, hp * LN + LN)
                        sp.sem_inc(s_sp, 1)
                        if not is_first(hp):
                            sp.wait_ge(s_xi, hp * 128)
                            sp.sem_inc(s_sp, 1)
                            sp.wait_ge(s_x, hp * 4)
                        for half in range(2):
                            sp.dma_start(inv_d[:, :, half].rearrange("x b r m -> (x b) r m"),
                                         inv[64 * half:64 * half + 64, :, :]).then_inc(s_go, 16)
                        sp.wait_ge(s_go, hp * 32 + 32)
                        for b in range(NB):
                            for half in range(2):
                                sp.dma_start(xs[b * B:(b + 1) * B, :, half, :],
                                             inv_d[:, b, half].rearrange("x r m -> r x m")).then_inc(s_xi, 16)
                heads(sp, body)
                sp.wait_ge(s_kq, (GDN_H + 1) * 32)

            @block.gpsimd
            def _(pool):
                pool.memset(eps6[:, :], 1e-6)
                pool.memset(inv0[:, :, :], 0.0)
                pool.memset(mask5[:, :], 0.0)
                pool.memset(x[:, :, :, :], 0.0).then_inc(s_pre, 1)
                pool.wait_ge(s_pre, 1)
                for half in range(2):
                    q = slice(64 * half, 64 * half + 64)
                    pool.affine_select(out=inv0[q, :, :], in_=inv0[q, :, :], compare_op=ALU.not_equal, fill=1.0,
                                       base=-half, pattern=[[1, B], [-2, HB]], channel_multiplier=0).then_inc(s_pre, 1)
                    pool.wait_ge(s_pre, 2 + half)
                for b in range(NB):
                    c = (b ^ 1) * B
                    pool.memset(mask5[b * B:(b + 1) * B, c:c + B], 1.0).then_inc(s_pre, 1)
                pool.wait_ge(s_pre, 7)
                one = mem["ones"][:, 0:1].unsqueeze(1).broadcast_to([P, B, HB])

                def substitute(h):
                    pool.wait_ge(s_li, h * 32 + 32)
                    if not is_first(h):
                        pool.wait_ge(s_go, h * 32)
                    pool.tensor_tensor(inv[:, :, :], inv0[:, :, :], one, ALU.mult).then_inc(s_ln, 1)
                    for s in range(1, LN):
                        k, w = (s - 1) // 2, (s - 1) // 4 + 1
                        rows, shape = slice(k + 1, B), [P, B - 1 - k, w]
                        pool.wait_ge(s_ln, h * LN + s)
                        if s % 2:
                            pool.tensor_tensor(tmp[:, rows, 0:w], low[:, rows, k:k + 1].broadcast_to(shape),
                                               inv[:, k:k + 1, 0:w].broadcast_to(shape), ALU.mult).then_inc(s_ln, 1)
                        else:
                            pool.tensor_tensor(inv[:, rows, 0:w], inv[:, rows, 0:w], tmp[:, rows, 0:w],
                                               ALU.subtract).then_inc(s_ln, 1)

                def body(hp, hf, hs, rp, rf, rs, turn):
                    if hp is not None:
                        for q, (d, c) in enumerate(quads):
                            pool.wait_ge(s_km, hp * 4 + (c // 2 + 2))
                            pool.wait_ge(s_exp, hp * 4 + (q + 1 + 2))
                            s = qk[:, rp, d, c:c + 4, :]
                            pool.tensor_tensor(s, s, ed[:, q % 2], ALU.mult).then_inc(s_qk, 1)
                    if hf is not None:
                        if not is_first(hf):
                            pool.wait_ge(s_pt5, hf * 2)
                        pool.wait_ge(s_nt, hf * 4 + 4 + 2)
                        pool.tensor_tensor(m5[:, :, :, :].rearrange("p d t i -> p (d t) i"),
                                           nt[:, rf].rearrange("p d t i -> p (d t) i"),
                                           mask5[:, :].unsqueeze(1).broadcast_to([P, 2 * NT, P]), ALU.mult).then_inc(s_m5, 1)
                    if hp is not None:
                        substitute(hp)
                heads(pool, body)

            @block.tensor
            def _(pe):
                pe.sem_inc(s_seg, 2)
                pe.sem_inc(s_c, 16)

                def prepare(h, r):
                    def turned(g):
                        src = khat[:, r] if g < 2 else qhat[:, :, :]
                        pe.wait_ge(s_hat, h * 2 + (g // 2 + 1))
                        if g == 0 and isinstance(h, int) and h == 1:
                            pe.wait_ge(s_nf, 2)
                            pe.wait_ge(s_exp, 4 + 2)
                        elif g == 0 and not is_first(h):
                            pe.wait_ge(s_u6, h * 2 + (-2))
                        for k in range(4):
                            last = pe.transpose(ps[:, g, k * P:(k + 1) * P], src[:, 4 * (g % 2) + k, :], ident[:, :])
                        last.then_inc(s_pt, 1)

                    def gram(pair):
                        if pair == 0:
                            pe.wait_ge(s_kqt, h * 4 + 4)
                        for k in range(2):
                            t = 2 * pair + k
                            last = pe.matmul(ps[:, pair, 256 * k:256 * k + 256], kqt[:, r, t, 0, :],
                                             kqt[:, r, t, :, :].rearrange("p a i -> p (a i)"), start=True, stop=True)
                        last.then_inc(s_kk, 1)

                    def between(q):
                        d = quads[q][0]
                        pe.wait_ge(s_am, h * 4 + (q + 1))
                        if q < 2:
                            pe.wait_ge(s_km, h * 4 + (q + 1))
                        else:
                            pe.wait_ge(s_exp, h * 4 + (q + 1))
                        pe.matmul(ps[:, q % 2, :], mem[past[d]][:, :], am[:, q % 2].rearrange("p t i -> p (t i)"),
                                  start=True, stop=True).then_inc(s_seg, 1)

                    def rows(g):
                        pe.wait_ge(s_km, h * 4 + (g + 3))
                        pe.wait_ge(s_nt, h * 4 + (g + 1 + 2))
                        for k in range(4):
                            last = pe.transpose(ps[:, 2 + g, k * P:(k + 1) * P], nt[:, r, 0, 4 * g + k, :], ident[:, :])
                        last.then_inc(s_pnf, 1)
                    return [(1, turned, 0), (1, turned, 1), (2, turned, 2), (2, turned, 3),
                            (4, gram, 0), (4, gram, 1), (5, gram, 2), (5, gram, 3),
                            (7, between, 0), (8, between, 1), (9, between, 2), (10, between, 3),
                            (10, rows, 0), (11, rows, 1)]

                def finish(h, r, beside):
                    tm, um = (x, xt), (xt, x)

                    def turned(q):
                        d, c = quads[q]
                        if q == 0:
                            if beside is not None:
                                pe.wait_ge(s_exp, beside * 4 + 4 + 2)
                                pe.wait_ge(s_nf, beside * 2 + 2)
                            else:
                                pe.wait_ge(s_u6, h * 2)
                            pe.wait_ge(s_x, h * 4 + 4)
                        for k in range(4):
                            last = pe.transpose(ps[:, q, k * P:(k + 1) * P], x[:, d, c + k, :], ident[:, :])
                        last.then_inc(s_pxt, 1)

                    def m5t(q):
                        d, c = quads[q]
                        pe.wait_ge(s_m5, h + 1)
                        pe.wait_ge(s_xt, h * 4 + (q + 1))
                        for k in range(4):
                            last = pe.matmul(ps[:, q, k * P:(k + 1) * P], m5[:, d, c + k, :], tm[d][:, d, c + k, :],
                                             start=True, stop=True)
                        last.then_inc(s_py5, 1)

                    def u5(q):
                        d, c = quads[q]
                        pe.wait_ge(s_y5, h * 4 + (q + 1))
                        for k in range(4):
                            last = pe.matmul(ps[:, q, k * P:(k + 1) * P], y5[:, d, c + k, :], um[d][:, d, c + k, :],
                                             start=True, stop=True)
                        last.then_inc(s_pu5, 1)

                    def t5(d):
                        e = 64 * d
                        pe.wait_ge(s_u5, h * 4 + (d + 1))
                        pe.sem_inc(s_own, 1)
                        for t in range(NT):
                            last = pe.matmul(ps[e:e + 64, d, t * 64:(t + 1) * 64], um[d][:, d, t, e:e + 64],
                                             y5[:, d, t, e:e + 64], start=True, stop=True)
                        last.then_inc(s_pt5, 1)

                    def y6_(d):
                        e, f = 64 * d, 64 - 64 * d
                        pe.wait_ge(s_u5, h * 4 + (d + 3))
                        pe.wait_ge(s_t5, h * 2 + (d + 1))
                        pe.sem_inc(s_own, 1)
                        for t in range(NT):
                            last = pe.matmul(ps[f:f + 64, 2 + d, t * 64:(t + 1) * 64], nt[e:e + 64, r, d, t, f:f + 64],
                                             t64[e:e + 64, t, :], start=True, stop=True)
                        last.then_inc(s_py6, 1)

                    def u6(d):
                        e, f = 64 * d, 64 - 64 * d
                        pe.wait_ge(s_u5, h * 4 + 4)
                        pe.wait_ge(s_y6, h * 2 + (d + 1))
                        pe.sem_inc(s_own, 1)
                        for t in range(NT):
                            last = pe.matmul(ps[e:e + 64, d, t * 64:(t + 1) * 64], y6[f:f + 64, t, :],
                                             ut[f:f + 64, r, d, t, f:f + 64], start=True, stop=True)
                        last.then_inc(s_pu6, 1)
                    return [(13, turned, 0), (13, turned, 1), (14, turned, 2), (14, turned, 3),
                            (15, m5t, 0), (15, m5t, 1), (16, m5t, 2), (16, m5t, 3),
                            (17, u5, 0), (17, u5, 1), (18, u5, 2), (18, u5, 3),
                            (19, t5, 0), (19, t5, 1), (21, y6_, 0), (21, y6_, 1), (23, u6, 0), (23, u6, 1)]

                def from_state(h, r, c, d):
                    pe.wait_ge(s_st, h * 16 + (2 * (c - 1) + d + 1))
                    if c >= 2:
                        pe.wait_ge(s_oq, h * 14 + (2 * (c - 2) + d + 1))
                    for a in range(2):
                        last = pe.matmul(ps[:, 4 + d, a * P:(a + 1) * P], kqt[:, r, unit(c, d), a, :], st[:, d, :],
                                         start=True, stop=True)
                    last.then_inc(s_ks, 1)

                def solve(h, r, turn, c, d):
                    if c == 0 and d == 0:
                        pe.wait_ge(s_o, h * 16 + 1)
                        pe.wait_ge(s_u6, h * 2 + 2)
                        pe.wait_ge(s_v[r], turn * 16 + 16)
                    if c >= 1:
                        pe.wait_ge(s_rv, h * 14 + (2 * (c - 1) + d + 1))
                        pe.wait_ge(s_o, h * 16 + (2 * (c - 1) + d + 2))
                    pe.matmul(ps[:, 6 + d, 0:P], ut[:, r, d, unit(c, d), :],
                              v[:, r, unit(c, d), :] if c == 0 else rv[:, d, :], start=True, stop=True).then_inc(s_tr, 1)

                def use(h, r, c, d):
                    if c == 0 and d == 0:
                        pe.wait_ge(s_qk, h * 4 + 4 + 2)
                    pe.wait_ge(s_vn, h * 32 + (4 * c + 2 * d + 2))
                    pe.matmul(ps[:, 6 + d, 2 * P:3 * P], khat[:, r, unit(c, d), :], vn[:, d, 0, :], start=True, stop=True)
                    pe.matmul(ps[:, 6 + d, P:2 * P], qk[:, r, d, unit(c, d), :], vn[:, d, 1, :],
                              start=True, stop=True).then_inc(s_c, 1)

                def body(hp, hf, hs, rp, rf, rs, turn):
                    prep, fin = prepare(hp, rp), finish(hf, rf, hp)
                    for c in range(NT):
                        if hs is not None and c >= 1:
                            for d in range(2):
                                from_state(hs, rs, c, d)
                        slice_of(prep, 3 * c, hp)
                        slice_of(fin, 3 * c, hf)
                        if hs is not None:
                            for d in range(2):
                                solve(hs, rs, turn, c, d)
                        slice_of(prep, 3 * c + 1, hp)
                        slice_of(fin, 3 * c + 1, hf)
                        if hs is not None:
                            for d in range(2):
                                use(hs, rs, c, d)
                        slice_of(prep, 3 * c + 2, hp)
                        slice_of(fin, 3 * c + 2, hf)
                heads(pe, body)

            @block.scalar
            def _(act):
                act.sem_inc(s_exp, 2)
                for q in range(SLOTS):
                    act.sem_inc(s_os[q], 16)
                act.wait_ge(s_pre, 7)
                act.activation(rn[:, :, :].rearrange("p a t -> p (a t)"), mem["ssq"][:, NT:17 * NT], ACT.Sqrt,
                               bias=eps6[:, 0:1]).then_inc(s_prv, 1)

                def prepare(h, r):
                    def turned_out(g):
                        act.wait_ge(s_pt, h * 4 + (g + 1))
                        act.activation(kqt[:, r, 4 * (g % 2):4 * (g % 2) + 4, g // 2, :],
                                       ps[:, g, :].rearrange("p (t i) -> p t i", t=4), ACT.Copy).then_inc(s_kqt, 1)

                    def masks(q):
                        d, c = quads[q]
                        act.wait_ge(s_seg, h * 4 + (q + 1))
                        for k in range(4):
                            last = act.activation(am[:, q % 2, k, :], mem[within[d]][:, :], ACT.Copy,
                                                  scale=column("dec", c + k, h + (H0 + d * GDN_H)))
                        last.then_inc(s_am, 1)

                    def exps(q):
                        act.wait_ge(s_seg, h * 4 + (q + 1 + 2))
                        act.wait_ge(s_nt, h * 4 + (q + 1))
                        act.wait_ge(s_qk, h * 4 + (q + 1))
                        act.activation(ed[:, q % 2], ps[:, q % 2, :].rearrange("p (t i) -> p t i", t=4),
                                       ACT.Exp).then_inc(s_exp, 1)

                    def rows_out(g):
                        if g == 0 and not is_first(h):
                            act.wait_ge(s_ln, h * LN)
                        act.wait_ge(s_pnf, h * 2 + (g + 1))
                        act.activation(nf[:, 4 * g:4 * g + 4, :], ps[:, 2 + g, :].rearrange("p (t i) -> p t i", t=4),
                                       ACT.Copy).then_inc(s_nf, 1)
                    return [(0, masks, 0), (2, turned_out, 0), (2, turned_out, 1), (3, turned_out, 2), (3, turned_out, 3),
                            (4, masks, 1), (8, exps, 0), (8, masks, 2), (9, exps, 1), (9, masks, 3),
                            (10, exps, 2), (11, exps, 3), (12, rows_out, 0), (12, rows_out, 1)]

                def finish(h, r):
                    def place(b):
                        if b == 0:
                            if not is_first(h):
                                act.wait_ge(s_pu6, h * 2)
                            act.wait_ge(s_xi, h * 128 + 128)
                        q = slice(b * B, (b + 1) * B)
                        act.activation(x[q, :, :, b * B:(b + 1) * B].rearrange("p d t (m s) -> p (d t) s m", s=2),
                                       xs[q, :, :, :], ACT.Copy).then_inc(s_x, 1)

                    def turned_out(q):
                        d, c = quads[q]
                        act.wait_ge(s_pxt, h * 4 + (q + 1))
                        act.activation(xt[:, d, c:c + 4, :], ps[:, q, :].rearrange("p (t i) -> p t i", t=4),
                                       ACT.Copy).then_inc(s_xt, 1)

                    def y5_out(q):
                        d, c = quads[q]
                        act.wait_ge(s_py5, h * 4 + (q + 1))
                        act.activation(y5[:, d, c:c + 4, :], ps[:, q, :].rearrange("p (t i) -> p t i", t=4),
                                       ACT.Copy).then_inc(s_y5, 1)

                    def y6_out(d):
                        f = slice(64 - 64 * d, 128 - 64 * d)
                        act.wait_ge(s_py6, h * 2 + (d + 1))
                        act.activation(y6[f, :, :], ps[f, 2 + d, :].rearrange("p (t i) -> p t i", t=NT),
                                       ACT.Copy).then_inc(s_y6, 1)

                    def u6_out(d):
                        e, f = slice(64 * d, 64 * d + 64), slice(64 - 64 * d, 128 - 64 * d)
                        act.wait_ge(s_u5, h * 4 + 4)
                        act.wait_ge(s_pu6, h * 2 + (d + 1))
                        act.activation(ut[e, r, d, :, f], ps[e, d, :].rearrange("p (t i) -> p t i", t=NT),
                                       ACT.Copy, scale=-1.0).then_inc(s_u6, 1)
                    return [(11, place, 0), (11, place, 1), (12, place, 2), (12, place, 3),
                            (14, turned_out, 0), (14, turned_out, 1), (15, turned_out, 2), (15, turned_out, 3),
                            (16, y5_out, 0), (16, y5_out, 1), (17, y5_out, 2), (17, y5_out, 3),
                            (22, y6_out, 0), (22, y6_out, 1), (24, u6_out, 0), (24, u6_out, 1)]

                def values(h, c, d):
                    act.wait_ge(s_tr, h * 16 + (2 * c + d + 1))
                    if c >= 1:
                        act.wait_ge(s_c, h * 16 + (2 * (c - 1) + d + 1 + 16))
                    t = unit(c, d)
                    for k, scale in enumerate((bout[:, t, ds(h + d * GDN_H, 1)], column("beta", t, h + d * GDN_H))):
                        act.activation(vn[:, d, k, :], ps[:, 6 + d, 0:P], ACT.Copy, scale=scale).then_inc(s_vn, 1)

                def body(hp, hf, hs, rp, rf, rs, turn):
                    prep, fin = prepare(hp, rp), finish(hf, rf)
                    for c in range(NT):
                        slice_of(prep, 3 * c, hp)
                        slice_of(fin, 3 * c, hf)
                        if hs is not None:
                            for d in range(2):
                                values(hs, c, d)
                        for s in range(3 * c + 1, 3 * c + 3):
                            slice_of(prep, s, hp)
                            slice_of(fin, s, hf)
                    slice_of(fin, 3 * NT, hf)
                    if hs is not None:
                        act.wait_ge(s_o, hs * 16 + 16 + 1)
                        act.dma_start(A["mix"].rearrange("(t p) n -> p t n", p=P)[:, :, ds(hs * P + D, P)], o[:, rs]
                                      ).then_inc(s_os[rs], 16)
                act.wait_ge(s_prv, 5)
                heads(act, body)
                for q in range(SLOTS):
                    act.wait_ge(s_os[q], 16 * ((GDN_H - 1 - q) // SLOTS + 2))

            @block.vector
            def _(dve):
                dve.sem_inc(s_nt, 2)
                dve.sem_inc(s_qk, 2)
                dve.sem_inc(s_o, 1)
                dve.tensor_scalar(nein[:, :, :], mem["ein"][:, :, H0:], -1.0, None, ALU.mult).then_inc(s_prv, 1)
                dve.tensor_tensor(bout[:, :, :], mem["eout"][:, :, H0:], mem["beta"][:, :, :], ALU.mult).then_inc(s_prv, 1)
                dve.wait_ge(s_prv, 3)
                dve.reciprocal(rn[:, :, :], rn[:, :, :]).then_inc(s_prv, 1)
                dve.wait_ge(s_prv, 4)
                dve.tensor_scalar(rn[:, 0:8, :], rn[:, 0:8, :], GDN_D ** -0.5, None, ALU.mult).then_inc(s_prv, 1)
                dve.wait_ge(s_prv, 5)

                def prepare(h, r):
                    def scaled(g):
                        src, dst = ((kraw, khat[:, r]), (qhat, qhat[:, :, :]))[g]
                        if g == 0:
                            dve.wait_ge(s_kq, h * 32 + 32)
                        by = rn[:, ds(h + 8 * (1 - g), 1), :].rearrange("p o t -> p (o t)").unsqueeze(2)
                        dve.tensor_tensor(dst, src[:, :, :], by.broadcast_to([P, NT, P]), ALU.mult).then_inc(s_hat, 1)

                    def masked(pair):
                        dve.wait_ge(s_kk, h * 4 + (pair + 1))
                        for d in range(2):
                            for k in range(2):
                                t = 2 * pair + k
                                dve.scalar_tensor_tensor(out=nt[:, r, d, t, :], in0=ps[:, pair, 256 * k:256 * k + P],
                                                         scalar=column("beta", t, h + d * GDN_H),
                                                         in1=mem[strict[d]][:, :], op0=ALU.mult, op1=ALU.mult)
                            last = dve.tensor_tensor(
                                qk[:, r, d, 2 * pair:2 * pair + 2, :],
                                ps[:, pair, :].rearrange("p (t a i) -> p t a i", t=2, a=2)[:, :, 1, :],
                                mem[within[d]][:, :].unsqueeze(1).broadcast_to([P, 2, P]), ALU.mult)
                        last.then_inc(s_km, 1)

                    def decayed(q):
                        d, c = quads[q]
                        if q == 0:
                            dve.wait_ge(s_km, h * 4 + 4)
                        dve.wait_ge(s_exp, h * 4 + (q + 1 + 2))
                        dve.tensor_tensor(nt[:, r, d, c:c + 4, :], nt[:, r, d, c:c + 4, :], ed[:, q % 2],
                                          ALU.mult).then_inc(s_nt, 1)
                    return [(0, scaled, 0), (1, scaled, 1), (5, masked, 0), (5, masked, 1), (6, masked, 2), (6, masked, 3),
                            (9, decayed, 0), (10, decayed, 1), (11, decayed, 2), (12, decayed, 3)]

                def finish(h, r):
                    tm, um = (x, xt), (xt, x)

                    def u5(q):
                        d, c = quads[q]
                        dve.wait_ge(s_pu5, h * 4 + (q + 1))
                        dve.tensor_tensor(ut[:, r, d, c:c + 4, :], um[d][:, d, c:c + 4, :],
                                          ps[:, q, :].rearrange("p (t i) -> p t i", t=4), ALU.subtract).then_inc(s_u5, 1)

                    def t5(d):
                        e = slice(64 * d, 64 * d + 64)
                        dve.wait_ge(s_pt5, h * 2 + (d + 1))
                        dve.tensor_tensor(t64[e, :, :], tm[d][e, d, :, e],
                                          ps[e, d, :].rearrange("p (t i) -> p t i", t=NT),
                                          ALU.subtract).then_inc(s_t5, 1)
                    return [(18, u5, 0), (18, u5, 1), (19, u5, 2), (19, u5, 3), (20, t5, 0), (20, t5, 1)]

                def residual(h, r, c, d):
                    n14, n16 = h * 14 + (2 * (c - 1) + d), h * 16 + (2 * c + d)
                    dve.wait_ge(s_ks, n14 + 1)
                    dve.wait_ge(s_tr, n16 - 1)
                    dve.scalar_tensor_tensor(out=rv[:, d, :], in0=ps[:, 4 + d, 0:P],
                                             scalar=nein[:, unit(c, d), ds(h + d * GDN_H, 1)],
                                             in1=v[:, r, unit(c, d), :], op0=ALU.mult, op1=ALU.add).then_inc(s_rv, 1)

                def output_from_state(h, r, c, d):
                    t, ein = unit(c, d), H0 + d * GDN_H
                    if c < NT // 2:
                        dve.tensor_scalar(o[:, r, t, :], ps[:, 4 + d, P:2 * P], column("ein", t, h + ein), None,
                                          ALU.mult).then_inc(s_oq, 1)
                        return
                    dve.wait_ge(s_o, h * 16 + (2 * (NT - 1 - c) + (1 - d) + 2))
                    dve.scalar_tensor_tensor(out=o[:, r, t, :], in0=ps[:, 4 + d, P:2 * P], scalar=column("ein", t, h + ein),
                                             in1=o[:, r, t, :], op0=ALU.mult, op1=ALU.add).then_inc(s_oq, 1)

                def update(h, r, c, d):
                    t, n16 = unit(c, d), h * 16 + (2 * c + d)
                    dve.wait_ge(s_c, n16 + 1 + 16)
                    if c == 0:
                        dve.tensor_copy(st[:, d, :], ps[:, 6 + d, 2 * P:3 * P]).then_inc(s_st, 1)
                        dve.tensor_copy(o[:, r, t, :], ps[:, 6 + d, P:2 * P]).then_inc(s_o, 1)
                        return
                    dve.wait_ge(s_st, n16 - 1)
                    dve.scalar_tensor_tensor(out=st[:, d, :], in0=st[:, d, :],
                                             scalar=column("etot", t, h + (H0 + d * GDN_H)),
                                             in1=ps[:, 6 + d, 2 * P:3 * P], op0=ALU.mult, op1=ALU.add).then_inc(s_st, 1)
                    dve.wait_ge(s_oq, h * 14 + (2 * (c - 1) + d + 1))
                    dve.tensor_tensor(o[:, r, t, :], ps[:, 6 + d, P:2 * P], o[:, r, t, :], ALU.add).then_inc(s_o, 1)

                def body(hp, hf, hs, rp, rf, rs, turn):
                    prep, fin = prepare(hp, rp), finish(hf, rf)
                    if hs is not None:
                        dve.wait_ge(s_os[rs], turn * 16 + 16)
                        dve.wait_ge(s_v[rs], turn * 16 + 16)
                    for c in range(NT):
                        if hs is not None and c >= 1:
                            for d in range(2):
                                residual(hs, rs, c, d)
                            for d in range(2):
                                output_from_state(hs, rs, c, d)
                        for s in range(3 * c, 3 * c + 2):
                            slice_of(prep, s, hp)
                            slice_of(fin, s, hf)
                        if hs is not None:
                            for d in range(2):
                                update(hs, rs, c, d)
                        slice_of(prep, 3 * c + 2, hp)
                        slice_of(fin, 3 * c + 2, hf)
                heads(dve, body)


class LayerNorm:

    STEPS = NT + 4

    def __init__(self, ph, mem, gain, shift, out=None):
        self.ps, self.ident, self.acc, self.xh, self.xl = (mem[n] for n in ("ps", "ident", "acc", "xh", "xl"))
        self.out = out
        self.gain, self.shift = ph.sb("ln_g", [P, D]), ph.sb("ln_b", [P, D])
        self.sources = gain, shift
        self.stats, self.mv = ph.sb("ln_stats", [P, 2, 2, 6]), ph.sb("ln_mv", [P, NT, 2])
        self.dev, self.rstd, self.off = ph.sb("ln_dev", [P, NT]), ph.sb("ln_rstd", [P, NT]), ph.sb("ln_off", [P, NT])
        self.eps = ph.sb("ln_eps", [P, 1])
        self.s_par = ph.sem("ln_par")
        self.s_eps = ph.sem("ln_eps")
        self.s_sta = ph.sem("ln_sta")
        self.s_var = ph.sem("ln_var")
        self.s_dev = ph.sem("ln_dev")
        self.s_rec = ph.sem("ln_rec")
        self.s_nrm = ph.sem("ln_nrm")
        self.s_gain = ph.sem("ln_gain")
        self.s_done = ph.sem("ln_done")
        self.s_turn = ph.sem("ln_turn")
        self.s_hi = ph.sem("ln_hi")
        self.s_lo = ph.sem("ln_lo")
        self.s_out = ph.sem("ln_out")

    def banks(self, t):
        return self.ps[:, 2 * (t % 2):2 * (t % 2) + 2, :].rearrange("p b (k c) -> p (b k) c", c=P)

    def load(self, sp):
        for dst, src in zip((self.gain, self.shift), self.sources):
            sp.dma_start(dst[:, :], src.partition_broadcast(P)).then_inc(self.s_par, 16)

    def prepare(self, pool):
        pool.memset(self.eps[:, :], EPS).then_inc(self.s_eps, 1)

    def vector(self, dve, i):
        if i < NT:
            for half in range(2):
                if i >= 2:
                    dve.wait_ge(self.s_var, i - 1)
                dve.bn_stats(self.stats[:, i % 2, half, :], self.acc[:, i, half * HALF:(half + 1) * HALF]
                             ).then_inc(self.s_sta, 1)
            dve.wait_ge(self.s_sta, 2 * i + 2)
            dve.bn_aggr(self.mv[:, i, :], self.stats[:, i % 2]).then_inc(self.s_var, 1)
        t = i - 1
        if 0 <= t < NT:
            dve.wait_ge(self.s_dev, t + 1)
            dve.reciprocal(self.rstd[:, t:t + 1], self.dev[:, t:t + 1]).then_inc(self.s_rec, 1)
            dve.wait_ge(self.s_rec, 2 * t + 1)
            dve.scalar_tensor_tensor(out=self.off[:, t:t + 1], in0=self.mv[:, t, 0:1], scalar=-1.0,
                                     in1=self.rstd[:, t:t + 1], op0=ALU.mult, op1=ALU.mult).then_inc(self.s_rec, 1)
        t = i - 2
        if 0 <= t < NT:
            dve.wait_ge(self.s_nrm, t + 1)
            dve.wait_ge(self.s_par, 32)
            dve.tensor_tensor(self.acc[:, t, :], self.acc[:, t, :], self.gain[:, :], ALU.mult).then_inc(self.s_gain, 1)
        t = i - 4
        if self.out is None and 0 <= t < NT:
            out = (slice(None), slice(None), slice(t * P, (t + 1) * P))
            dve.wait_ge(self.s_hi, t + 1)
            dve.tensor_tensor(self.xl[out], self.banks(t), self.xh[out].bitcast(F32), ALU.subtract).then_inc(self.s_lo, 1)

    def scalar(self, act, i):
        if i < NT:
            act.wait_ge(self.s_var, i + 1)
            act.wait_ge(self.s_eps, 1)
            act.activation(self.dev[:, i:i + 1], self.mv[:, i, 1:2], ACT.Sqrt, bias=self.eps[:, 0:1]
                           ).then_inc(self.s_dev, 1)
        t = i - 1
        if 0 <= t < NT:
            act.wait_ge(self.s_rec, 2 * t + 2)
            act.activation(self.acc[:, t, :], self.acc[:, t, :], ACT.Identity, scale=self.rstd[:, t:t + 1],
                           bias=self.off[:, t:t + 1]).then_inc(self.s_nrm, 1)
        t = i - 3
        if self.out is None and 0 <= t < NT:
            act.wait_ge(self.s_turn, t + 1)
            act.activation(self.xh[:, :, t * P:(t + 1) * P], self.banks(t), ACT.Copy).then_inc(self.s_hi, 1)

    def gpsimd(self, pool):
        pool.wait_ge(self.s_par, 32)
        for t in range(NT):
            pool.wait_ge(self.s_gain, t + 1)
            pool.tensor_tensor(self.acc[:, t, :], self.acc[:, t, :], self.shift[:, :], ALU.add).then_inc(self.s_done, 1)

    def tensor(self, pe, t):
        if self.out is not None:
            return
        pe.wait_ge(self.s_done, t + 1)
        if t >= 2:
            pe.wait_ge(self.s_lo, t - 1)
        for k in range(KT):
            last = pe.transpose(self.banks(t)[:, k, :], self.acc[:, t, k * P:(k + 1) * P], self.ident[:, :])
        last.then_inc(self.s_turn, 1)

    def store(self, sp):
        if self.out is not None:
            for t in range(NT):
                sp.wait_ge(self.s_done, t + 1)
                sp.dma_start(self.out[t * P:(t + 1) * P, :], self.acc[:, t, :]).then_inc(self.s_out, 16)
            sp.wait_ge(self.s_out, 16 * NT)


def first_slab(A, layer, kind):
    if kind == "mlp":
        return A["mlp_w1"][layer].rearrange("(k p) n -> p k n", p=P)[:, :, 0:SLAB]
    if kind == "attn":
        return A["attn_w_qkv"][0].rearrange("(k p) n -> p k n", p=P)[:, :, ATTN_K:ATTN_K + SLAB]
    return A["attn_w_o"][0][0:HALF, 0:HALF].rearrange("(k p) n -> p k n", p=P)


def phase_project(nc, A, mem, layer, ahead):
    ps, ident, acc, xh, xl = (mem[n] for n in ("ps", "ident", "acc", "xh", "xl"))
    mixed = layer == 0
    rows_d, w = (A["mix"], A["even_w_out"][0]) if mixed else (A["ao"], A["attn_w_o"][0])
    QK = HALF // P
    NQ = w.shape[0] // HALF
    GQ = NQ // 2 if mixed else NQ
    NR = NQ * NT
    GR = GQ * NT
    with ExitStack() as ctx:
        ph = Phase(nc, ctx, f"pr{layer}")
        sb, sem = ph.sb, ph.sem
        ln = LayerNorm(ph, mem, A["ln_mix_g"][layer], A["ln_mix_b"][layer])
        raw = sb("raw", [P, RING, QK, HALF])
        wh, wl = (mem[n][:, :, :].rearrange("p u (k n) -> p u k n", k=QK) for n in ("wh", "wl"))
        ROWS = 4
        rows = sb("rows", [P, ROWS, HALF])

        s_res = [sem("res0"), sem("res1")]
        s_add = sem("add")
        s_al = sem("al")
        s_row = [sem(f"row{n}") for n in range(ROWS)]
        s_rows = sem("rows_done")
        s_turn = sem("turn")
        s_hi = sem("hi")
        s_lo = sem("lo")
        s_raw = [sem("raw0"), sem("raw1")]
        s_wh = sem("wh_done")
        s_wl = sem("wl_done")
        s_mm = sem("mm")
        s_ac = sem("ac")
        if mixed:
            orow, grow = sb("orow", [P, RING, HALF]), sb("grow", [P, RING, HALF])
            osq, ogw = sb("osq", [P, RING, HALF]), sb("ogw", [P, RING, HALF])
            sums, root_tile, rec = (sb(n, [P, RING, HALF // GDN_D]) for n in ("sums", "root", "rec"))
            gw = sb("gw", [P, GDN_D])
            res = sb("res", [P, RING, D])
            s_gw = sem("gw")
            s_og = [sem("og0"), sem("og1")]
            s_osq = sem("osq_done")
            s_sum = sem("sum")
            s_root = sem("root_done")
            s_rec = sem("rec_done")
            s_pgw = sem("pgw")

        def by_head(a):
            return a.rearrange("p (h d) -> p h d", d=GDN_D)

        with nc.Block() as block:
            @block.sync
            def _(sp):
                def load_rows(n):
                    if n >= NR:
                        return
                    j, t = divmod(n, NT)
                    tokens = slice(t * P, (t + 1) * P)
                    if n < GR:
                        if n >= ROWS:
                            sp.wait_ge(s_turn, n - ROWS + 1)
                        sp.dma_start(rows[:, n % ROWS], rows_d[tokens, j * HALF:(j + 1) * HALF]
                                     ).then_inc(s_row[n % ROWS], 16)
                        return
                    if n >= GR + RING:
                        sp.wait_ge(s_pgw, 2 * (n - GR - 1))
                        sp.wait_ge(s_osq, n - GR - 1)
                    c = (j - GQ) * HALF
                    sp.dma_start(orow[:, n % 2], rows_d[tokens, D + c:D + c + HALF]).then_inc(s_og[n % 2], 16)
                    sp.dma_start(grow[:, n % 2], A["scr"][tokens, G0 + c:G0 + c + HALF]).then_inc(s_og[n % 2], 16)

                def load_slab(s):
                    if s > 2 * NQ or (s == 0 and not mixed):
                        return
                    if s >= RING:
                        sp.wait_ge(s_wl, s - 1)
                    if s == 2 * NQ:
                        sp.dma_start(raw[:, 0].rearrange("p k n -> p (k n)").rearrange("p (k n) -> p k n", k=ahead.shape[1]),
                                     ahead).then_inc(s_raw[0], 16)
                        return
                    sp.dma_start(raw[:, s % 2], w[(s // 2) * HALF:(s // 2 + 1) * HALF, (s % 2) * HALF:(s % 2 + 1) * HALF]
                                 .rearrange("(k p) n -> p k n", p=P)).then_inc(s_raw[s % 2], 16)
                if not mixed:
                    sp.sem_inc(s_raw[0], 16)
                for n in range(ROWS):
                    load_rows(n)
                load_slab(0)
                load_slab(1)
                for n in range(ROWS, NT):
                    load_rows(n)
                if mixed:
                    sp.dma_start(gw[:, :], A["gdn_norm_w"][0].partition_broadcast(P)).then_inc(s_gw, 16)
                ln.load(sp)
                for j in range(NQ):
                    n = (j + 1) * NT
                    load_rows(n)
                    load_rows(n + 1)
                    if mixed and j == 1:
                        for t in range(NT):
                            if t >= RING:
                                sp.wait_ge(s_add, t - 1)
                            sp.dma_start(res[:, t % 2], A["x"][0, t * P:(t + 1) * P, :]).then_inc(s_res[t % 2], 16)
                    load_slab(2 * j + 2)
                    for k in range(2, 6):
                        load_rows(n + k)
                    load_slab(2 * j + 3)
                    for k in range(6, NT):
                        load_rows(n + k)

            @block.gpsimd
            def _(pool):
                ln.prepare(pool)
                one = mem["ones"][:, 0:1].unsqueeze(1).broadcast_to([P, QK, HALF])

                def split(s):
                    if s > 2 * NQ:
                        return
                    pool.wait_ge(s_raw[s % 2], 16 * (s // 2 + 1))
                    if s == 0 and not mixed:
                        pool.sem_inc(s_wh, 1)
                        pool.sem_inc(s_wl, 1)
                        return
                    if s >= RING:
                        pool.wait_ge(s_mm, NT * (s - 1))
                    pool.tensor_tensor(wh[:, s % 2], raw[:, s % 2], one, ALU.mult).then_inc(s_wh, 1)
                    pool.wait_ge(s_wh, s + 1)
                    pool.tensor_tensor(wl[:, s % 2], raw[:, s % 2], wh[:, s % 2].bitcast(F32), ALU.subtract
                                       ).then_inc(s_wl, 1)

                def gate(n):
                    g = n - GR
                    if n >= NR or g < 0:
                        return
                    if g == 0:
                        pool.wait_ge(s_gw, 16)
                    pool.wait_ge(s_og[n % 2], 32 * (g // 2 + 1))
                    if g >= RING:
                        pool.wait_ge(s_rows, g - 1)
                    pool.tensor_tensor(by_head(ogw[:, n % 2]), by_head(grow[:, n % 2]),
                                       gw[:, :].unsqueeze(1).broadcast_to([P, HALF // GDN_D, GDN_D]), ALU.mult
                                       ).then_inc(s_pgw, 1)
                    pool.wait_ge(s_pgw, 2 * g + 1)
                    pool.tensor_tensor(ogw[:, n % 2], ogw[:, n % 2], orow[:, n % 2], ALU.mult).then_inc(s_pgw, 1)
                split(0)
                split(1)
                for j in range(NQ):
                    n = (j + 1) * NT
                    for k in range(2 if j else 0, NT):
                        gate(n + k)
                    split(2 * j + 2)
                    gate(n + NT)
                    gate(n + NT + 1)
                    split(2 * j + 3)
                ln.gpsimd(pool)

            @block.tensor
            def _(pe):
                def turn(n):
                    if n >= NR:
                        return
                    if n < GR:
                        pe.wait_ge(s_row[n % ROWS], 16 * (n // ROWS + 1))
                    else:
                        pe.wait_ge(s_rows, n - GR + 1)
                    if n >= 4:
                        pe.wait_ge(s_lo, n - 3)
                    for k in range(QK):
                        last = pe.transpose(ps[:, n % 4, k * P:(k + 1) * P], rows[:, n % ROWS, k * P:(k + 1) * P], ident[:, :])
                    last.then_inc(s_turn, 1)
                for n in range(NT):
                    turn(n)
                for s in range(2 * NQ):
                    j, u = divmod(s, 2)
                    pe.wait_ge(s_wl, s + 1)
                    pe.wait_ge(s_lo, (j + 1) * NT)
                    if s == 2 * NQ - 1:
                        pe.wait_ge(s_hi, NR)
                    for t in range(NT):
                        m = s * NT + t
                        if m >= 4:
                            pe.wait_ge(s_ac, m - 3)
                        for k in range(QK):
                            f = QK * (j % 2) + k
                            last = product(pe, ps[:, 4 + t % 4, :], xh[:, f, t * P:(t + 1) * P], xl[:, f, t * P:(t + 1) * P],
                                           wh[:, u, k, :], wl[:, u, k, :], k == 0, k == QK - 1)
                        last.then_inc(s_mm, 1)
                        if u == 0:
                            turn((j + 1) * NT + t)
                        if s == 2 * NQ - 1 and t >= 4:
                            ln.tensor(pe, t - 4)
                for t in range(4, NT):
                    ln.tensor(pe, t)

            @block.scalar
            def _(act):
                def scale_residual(t):
                    act.activation(acc[:, t, :], acc[:, t, :], ACT.Copy, scale=ALPHA).then_inc(s_al, 1)

                def square(n):
                    g = n - GR
                    if n >= NR or g < 0:
                        return
                    act.wait_ge(s_og[n % 2], 32 * (g // 2 + 1))
                    if g >= RING:
                        act.wait_ge(s_sum, g - 1)
                    act.activation(osq[:, n % 2], orow[:, n % 2], ACT.Square).then_inc(s_osq, 1)

                def root(n):
                    g = n - GR
                    if n >= NR or g < 0:
                        return
                    act.wait_ge(s_sum, g + 1)
                    if g >= RING:
                        act.wait_ge(s_rec, g - 1)
                    act.wait_ge(ln.s_eps, 1)
                    act.activation(root_tile[:, n % 2], sums[:, n % 2], ACT.Sqrt, bias=ln.eps[:, 0:1], scale=1.0 / GDN_D
                                   ).then_inc(s_root, 1)
                for n in range(NR):
                    j, t = divmod(n, NT)
                    if j == 1 and not mixed:
                        scale_residual(t)
                    square(n + 1)
                    act.wait_ge(s_turn, n + 1)
                    act.activation(xh[:, QK * (j % 2):QK * (j % 2) + QK, t * P:(t + 1) * P],
                                   ps[:, n % 4, :].rearrange("p (k c) -> p k c", k=QK), ACT.Copy).then_inc(s_hi, 1)
                    root(n + 1)
                for i in range(LayerNorm.STEPS):
                    ln.scalar(act, i)

            @block.vector
            def _(dve):
                def low(n):
                    if n >= NR:
                        return
                    j, t = divmod(n, NT)
                    out = (slice(None), slice(QK * (j % 2), QK * (j % 2) + QK), slice(t * P, (t + 1) * P))
                    dve.wait_ge(s_hi, n + 1)
                    dve.tensor_tensor(xl[out], ps[:, n % 4, :].rearrange("p (k c) -> p k c", k=QK),
                                      xh[out].bitcast(F32), ALU.subtract).then_inc(s_lo, 1)

                def sum_squares(n):
                    g = n - GR
                    if n >= NR or g < 0:
                        return
                    dve.wait_ge(s_osq, g + 1)
                    if g >= RING:
                        dve.wait_ge(s_root, g - 1)
                    dve.tensor_reduce(sums[:, n % 2], by_head(osq[:, n % 2]), AX, ALU.add).then_inc(s_sum, 1)

                def norm(n):
                    g = n - GR
                    if n >= NR or g < 0:
                        return
                    dve.wait_ge(s_root, g + 1)
                    dve.reciprocal(rec[:, n % 2], root_tile[:, n % 2]).then_inc(s_rec, 1)
                    dve.wait_ge(s_rec, g + 1)
                    dve.wait_ge(s_pgw, 2 * g + 2)
                    dve.wait_ge(s_turn, n - ROWS + 1)
                    dve.tensor_tensor(by_head(rows[:, n % ROWS]), by_head(ogw[:, n % 2]),
                                      rec[:, n % 2].unsqueeze(2).broadcast_to([P, HALF // GDN_D, GDN_D]), ALU.mult
                                      ).then_inc(s_rows, 1)

                def add(m):
                    t, u = m % NT, (m // NT) % 2
                    if m < NT and not mixed:
                        dve.wait_ge(s_al, t + 1)
                    dve.wait_ge(s_mm, m + 1)
                    if m >= 2 * NT:
                        dve.wait_ge(s_ac, m - 2 * NT + 1)
                    out = acc[:, t, u * HALF:(u + 1) * HALF]
                    if m < 2 * NT and mixed:
                        dve.tensor_copy(out, ps[:, 4 + t % 4, :]).then_inc(s_ac, 1)
                    else:
                        dve.tensor_tensor(out, ps[:, 4 + t % 4, :], out, ALU.add).then_inc(s_ac, 1)

                def add_residual(t):
                    dve.wait_ge(s_res[t % 2], 16 * (t // 2 + 1))
                    dve.wait_ge(s_ac, NT + t + 1)
                    dve.scalar_tensor_tensor(out=acc[:, t, :], in0=res[:, t % 2], scalar=ALPHA, in1=acc[:, t, :],
                                             op0=ALU.mult, op1=ALU.add).then_inc(s_add, 1)
                for n in range(NT):
                    low(n)
                for s in range(2 * NQ):
                    for t in range(NT):
                        n = (s // 2 + 1) * NT + t
                        if s % 2 == 0 and t < NT - 1:
                            sum_squares(n + 1)
                        elif s % 2 and t == NT - 1:
                            sum_squares(n + 1)
                            norm(n + 1)
                        if mixed and s == 2:
                            dve.wait_ge(s_add, t + 1)
                        add(s * NT + t)
                        if mixed and s == 1:
                            add_residual(t)
                        if s % 2 == 0:
                            low(n)
                            if t < NT - 1:
                                norm(n + 1)
                        if s == 2 * NQ - 1:
                            dve.wait_ge(s_ac, s * NT + t + 1)
                            ln.vector(dve, t)
                for i in range(NT, LayerNorm.STEPS):
                    ln.vector(dve, i)


def phase_mlp(nc, A, mem, layer, out=None, ahead=None):
    ps, acc, xh, xl = (mem[n] for n in ("ps", "acc", "xh", "xl"))
    w1, w2 = A["mlp_w1"][layer].rearrange("(k p) n -> p k n", p=P), A["mlp_w2"][layer].rearrange("(k p) n -> p k n", p=P)
    FK = HALF // P
    NF = w2.shape[1] // FK
    with ExitStack() as ctx:
        ph = Phase(nc, ctx, f"ml{layer}")
        sb, sem = ph.sb, ph.sem
        ln = LayerNorm(ph, mem, A["ln_ffn_g"][layer], A["ln_ffn_b"][layer], out)
        SIZE = KT * SLAB
        raw = sb("raw", [P, RING, SIZE])
        wh, wl = mem["wh"], mem["wl"]
        pos, sqr = sb("pos", [P, RING, HALF]), sb("sqr", [P, RING, HALF])
        hh, hl = sb("hh", [P, FK, S], F32R), sb("hl", [P, FK, S], F32R)

        s_al = sem("al")
        s_raw = [sem("raw0"), sem("raw1")]
        s_wh = sem("wh_done")
        s_wl = sem("wl_done")
        s_m1 = sem("m1")
        s_pos = sem("pos_done")
        s_sqr = sem("sqr_done")
        s_hh = sem("hh_done")
        s_hl = sem("hl_done")
        s_m2 = sem("m2")
        s_ac = sem("ac")

        def slabs(eng, body, first=0, count=NF):
            with eng.Fori(first, first + count) as q:
                for c in range(4):
                    body(q, c)

        def w1_tile(w, c, k, f):
            return w[:, c % 2, k * SLAB + f * P:k * SLAB + (f + 1) * P]

        def w2_tile(w, c, k):
            return w[:, c % 2, k * HALF:(k + 1) * HALF]

        with nc.Block() as block:
            @block.sync
            def _(sp):
                def load(q, c):
                    sp.wait_ge(s_wl, q * 4 + (c + 1))
                    if c < 2:
                        src = w1[:, :, ds(q * HALF + c * SLAB, SLAB)]
                        dst = raw[:, c % 2].rearrange("p (k n) -> p k n", k=KT)
                    else:
                        src = w2[:, ds(q * FK, FK), (c - 2) * HALF:(c - 1) * HALF]
                        dst = raw[:, c % 2].rearrange("p (k n) -> p k n", k=FK)
                    sp.dma_start(dst, src).then_inc(s_raw[c % 2], 16)
                sp.sem_inc(s_raw[0], 16)
                load(0, 1)
                ln.load(sp)
                load(0, 2)
                load(0, 3)
                slabs(sp, load, 1, NF - 1)
                if ahead is not None:
                    sp.wait_ge(s_wl, NF * 4 + 1)
                    sp.dma_start(raw[:, 0].rearrange("p (k n) -> p k n", k=ahead.shape[1]), ahead).then_inc(s_raw[0], 16)
                ln.store(sp)

            @block.gpsimd
            def _(pool):
                ln.prepare(pool)
                pool.sem_inc(s_wl, RING)
                one = mem["ones"][:, 0:1].broadcast_to([P, SIZE])

                def split(q, c):
                    if isinstance(q, int) and q == 0 and c == 0:
                        pool.sem_inc(s_wh, 1)
                        pool.sem_inc(s_wl, 1)
                        return
                    u = c % 2
                    pool.wait_ge(s_raw[u], q * 32 + (16 * (c // 2) + 16))
                    if c < 2:
                        pool.wait_ge(s_m2, q * 16 + 8 * (c + 1))
                    else:
                        pool.wait_ge(s_m1, q * 8 + 4 * (c - 1))
                    pool.tensor_tensor(wh[:, u], raw[:, u], one, ALU.mult).then_inc(s_wh, 1)
                    pool.wait_ge(s_wh, q * 4 + (c + 1))
                    pool.tensor_tensor(wl[:, u], raw[:, u], wh[:, u].bitcast(F32), ALU.subtract).then_inc(s_wl, 1)
                for c in range(4):
                    split(0, c)
                slabs(pool, split, 1, NF - 1)
                if ahead is not None:
                    split(NF, 0)
                ln.gpsimd(pool)

            @block.tensor
            def _(pe):
                pe.sem_inc(s_m2, 16)

                def multiply(q, c, norm=False):
                    pe.wait_ge(s_wl, q * 4 + (c + 1 + RING))
                    if c < 2:
                        for half in range(2):
                            for f in range(2):
                                e = 4 * c + 2 * half + f
                                pe.wait_ge(s_pos, q * 8 + (e + 1))
                                for k in range(KT):
                                    last = product(pe, ps[:, 2 * half + f, :], w1_tile(wh, c, k, f), w1_tile(wl, c, k, f),
                                                   xh[:, k, half * HALF:(half + 1) * HALF],
                                                   xl[:, k, half * HALF:(half + 1) * HALF], k == 0, k == KT - 1)
                                last.then_inc(s_m1, 1)
                        return
                    for t in range(NT):
                        if c == 2 and t % 4 == 0:
                            pe.wait_ge(s_hl, q * 8 + (6 + t // 2 + RING))
                        pe.wait_ge(s_ac, q * 16 + (8 * (c - 2) + t + 1))
                        for k in range(FK):
                            last = product(pe, ps[:, 4 + t % 4, :], hh[:, k, t * P:(t + 1) * P], hl[:, k, t * P:(t + 1) * P],
                                           w2_tile(wh, c, k), w2_tile(wl, c, k), k == 0, k == FK - 1)
                        last.then_inc(s_m2, 1)
                        if norm and t >= 4:
                            ln.tensor(pe, t - 4)
                slabs(pe, multiply, 0, NF - 1)
                for c in range(4):
                    multiply(NF - 1, c, c == 3)
                for t in range(4, NT):
                    ln.tensor(pe, t)

            @block.scalar
            def _(act):
                act.sem_inc(s_pos, 4)
                for t in range(NT):
                    act.activation(acc[:, t, :], acc[:, t, :], ACT.Copy, scale=ALPHA).then_inc(s_al, 1)

                def hidden(q, c):
                    if c >= 2:
                        return
                    for n in range(4):
                        e = 4 * c + n
                        act.wait_ge(s_m1, q * 8 + (e + 1))
                        act.activation(pos[:, n % 2, :], ps[:, n, :], ACT.Relu).then_inc(s_pos, 1)
                        act.wait_ge(s_hl, q * 8 + (e + 1))
                        act.wait_ge(s_pos, q * 8 + (e + 1 + 4))
                        act.activation(sqr[:, n % 2, :], pos[:, n % 2, :], ACT.Square).then_inc(s_sqr, 1)
                slabs(act, hidden)
                for i in range(LayerNorm.STEPS):
                    ln.scalar(act, i)

            @block.vector
            def _(dve):
                dve.sem_inc(s_hl, RING)
                dve.sem_inc(s_ac, 4)
                dve.wait_ge(s_al, NT)

                def work(q, c, norm=False):
                    if c < 2:
                        for n in range(4):
                            e = 4 * c + n
                            out = (slice(None), 2 * c + n % 2, slice((n // 2) * HALF, (n // 2 + 1) * HALF))
                            dve.wait_ge(s_sqr, q * 8 + (e + 1))
                            dve.tensor_copy(hh[out], sqr[:, n % 2, :]).then_inc(s_hh, 1)
                            dve.wait_ge(s_hh, q * 8 + (e + 1))
                            dve.tensor_tensor(hl[out], sqr[:, n % 2, :], hh[out].bitcast(F32), ALU.subtract
                                              ).then_inc(s_hl, 1)
                        return
                    for t in range(NT):
                        m = 8 * (c - 2) + t
                        if m == 0:
                            dve.wait_ge(s_ac, q * 16 + 4)
                        dve.wait_ge(s_m2, q * 16 + (m + 1 + 16))
                        out = acc[:, t, (c - 2) * HALF:(c - 1) * HALF]
                        dve.tensor_tensor(out, ps[:, 4 + t % 4, :], out, ALU.add).then_inc(s_ac, 1)
                        if norm:
                            dve.wait_ge(s_ac, q * 16 + (m + 1 + 4))
                            ln.vector(dve, t)
                slabs(dve, work, 0, NF - 1)
                for c in range(4):
                    work(NF - 1, c, c == 3)
                for i in range(NT, LayerNorm.STEPS):
                    ln.vector(dve, i)


def phase_attn(nc, A, mem, ahead):
    ps, ident, xh, xl = (mem[n] for n in ("ps", "ident", "xh", "xl"))
    HEADS, KV, HD = 16, 4, 64
    REP = HEADS // KV
    NB = NT
    BAND = 3
    W = BAND * P
    GW = REP * HD
    COL_K, COL_V = ATTN_K, (HEADS + KV) * HD
    UNITS = 4
    FAR = -1e30
    PROBS = 3
    with ExitStack() as ctx:
        ph = Phase(nc, ctx, "at")
        sb, sem = ph.sb, ph.sem
        raw = sb("raw", [P, KT, SLAB])
        wh, wl = (mem[n][:, :, :].rearrange("p u (k n) -> p u k n", k=KT) for n in ("wh", "wl"))
        kt = sb("kt", [P, 2, S])
        kx = sb("kx", [P, 2, S])
        qt = sb("qt", [P, RING, 2, S])
        vt = sb("vt", [P, NT, GW])
        near = sb("near", [P, BAND, P])
        slope = sb("slope", [P, HEADS])
        sink = sb("sink", [P, HEADS])
        prob = sb("prob", [P, PROBS, REP, W])
        pt = sb("pt", [P, BAND, REP * P])
        top, ntop, lift, esink, den = (sb(n, [P, RING, REP]) for n in ("top", "ntop", "lift", "esink", "den"))
        rec = sb("rec", [P, RING, REP])
        rows = sb("rows", [P, RING, GW])

        s_raw = sem("raw")
        s_wh = sem("wh_done")
        s_wl = sem("wl_done")
        s_small = sem("small")
        s_near = sem("near_done")
        s_neg = sem("neg")
        s_m = sem("m")
        s_me = sem("me")
        s_mv = sem("mv")
        s_ve = sem("ve")
        s_kx = sem("kx_done")
        s_s = sem("s")
        s_sb = sem("sb_done")
        s_max = sem("max")
        s_exp = sem("exp")
        s_es = sem("es_done")
        s_pt = sem("pt")
        s_pe = sem("pe")
        s_o = sem("o")
        s_den = sem("den_done")
        s_row = sem("row_done")
        s_st = [sem("st0"), sem("st1")]

        w = A["attn_w_qkv"][0].rearrange("(k p) n -> p k n", p=P)
        slab_cols = [COL_K, COL_V] + [g * GW for g in range(KV)]

        def key_blocks(n):
            return range(1 if n == 0 else 0, BAND - 1 if n == NB - 1 else BAND)

        def turned(b):
            g, n = divmod(b, NB)
            return g * (BAND * NB - 2) + (BAND * n - 1 if n else 0)

        def cols(n):
            return slice(key_blocks(n)[0] * P, (key_blocks(n)[-1] + 1) * P)

        LAG_E, LAG_T, LAG_V = 1, 2, 3
        STEPS = NB + LAG_V
        UNIT_STEPS = (0, 1, NB, NB + 1)

        with nc.Block() as block:
            @block.sync
            def _(sp):
                sp.dma_start(sink[:, :], A["attn_sink"][0].partition_broadcast(P)).then_inc(s_small, 16)
                def load(s):
                    if s > 1:
                        sp.wait_ge(s_wl, s)
                    if s == len(slab_cols):
                        sp.dma_start(raw[:, :, :].rearrange("p k n -> p (k n)").rearrange("p (k n) -> p k n", k=ahead.shape[1]),
                                     ahead).then_inc(s_raw, 16)
                        return
                    sp.dma_start(raw[:, :, :], w[:, :, slab_cols[s]:slab_cols[s] + SLAB]).then_inc(s_raw, 16)
                sp.sem_inc(s_raw, 16)
                for s in range(1, len(slab_cols) - 1):
                    load(s)
                    if s == 2:
                        sp.wait_ge(s_me, UNITS)
                        for a, b in ((0, HD), (HD, 0)):
                            sp.dma_start(kx[a:a + HD, :, :], kt[b:b + HD, :, :]).then_inc(s_kx, 16)
                for b in range(KV * NB):
                    g, n = divmod(b, NB)
                    sp.wait_ge(s_row, b + 1)
                    sp.dma_start(A["ao"][n * P:(n + 1) * P, g * GW:(g + 1) * GW], rows[:, b % 2]).then_inc(s_st[b % 2], 16)
                    if b in (0, 2 * NB):
                        load(len(slab_cols) - (b == 0))
                for q in range(2):
                    sp.wait_ge(s_st[q], 16 * (KV * NB // 2))

            @block.gpsimd
            def _(pool):
                one = mem["ones"][:, 0:1].unsqueeze(1).broadcast_to([P, KT, SLAB])

                def split(s):
                    u = s % 2
                    pool.wait_ge(s_raw, 16 * (s + 1))
                    if s in (2, 3):
                        pool.wait_ge(s_m, UNITS) if s == 2 else pool.wait_ge(s_mv, NT)
                    elif s > 3:
                        pool.wait_ge(s_m, UNITS * (s - 2))
                    pool.tensor_tensor(wh[:, u], raw[:, :, :], one, ALU.mult).then_inc(s_wh, 1)
                    pool.wait_ge(s_wh, s + 1)
                    pool.tensor_tensor(wl[:, u], raw[:, :, :], wh[:, u].bitcast(F32), ALU.subtract).then_inc(s_wl, 1)

                pool.iota(near[:, :, :], pattern=[[-P, BAND], [-1, P]], base=P, channel_multiplier=1,
                          allow_small_or_imprecise_dtypes=True).then_inc(s_near, 1)
                for h in range(HEADS):
                    pool.memset(slope[:, h:h + 1], 2.0 ** (-8.0 * (h + 1) / HEADS)).then_inc(s_near, 1)
                pool.sem_inc(s_wh, 1)
                pool.sem_inc(s_wl, 1)
                split(1)
                pool.wait_ge(s_neg, 1)
                for i, (base, sign) in enumerate(((0, 1), (2 * P, -1))):
                    pool.affine_select(out=near[:, :, :], in_=near[:, :, :], compare_op=ALU.is_ge, fill=FAR, base=base,
                                       pattern=[[sign * P, BAND], [sign, P]], channel_multiplier=-sign).then_inc(s_near, 1)
                    pool.wait_ge(s_near, HEADS + 2 + i)
                split(2)
                for n in range(3, len(slab_cols) + 1):
                    split(n)

            @block.tensor
            def _(pe):
                def unit(n):
                    if n >= UNITS * (KV + 1):
                        return
                    g, (f, half) = n // UNITS, divmod(n % UNITS, 2)
                    u = (g + 1) % 2 if g else 0
                    bank = n % 4 if n < 2 * UNITS else 6
                    if n % UNITS == 0:
                        pe.wait_ge(s_wl, g + 2 if g else 1)
                    if UNITS <= n < 2 * UNITS:
                        pe.wait_ge(s_me, n - 3)
                    if n > 2 * UNITS:
                        pe.wait_ge(s_me, n)
                    for k in range(KT):
                        last = product(pe, ps[:, bank, :], wh[:, u, k, f * P:(f + 1) * P], wl[:, u, k, f * P:(f + 1) * P],
                                       xh[:, k, half * HALF:(half + 1) * HALF], xl[:, k, half * HALF:(half + 1) * HALF],
                                       k == 0, k == KT - 1)
                    last.then_inc(s_m, 1)

                def scores(g, n):
                    b = g * NB + n
                    if n == 0:
                        pe.wait_ge(s_me, UNITS * (g + 2))
                        pe.wait_ge(s_kx, 32)
                        pe.wait_ge(s_ve, NT)
                    keys = slice((n - 1 + key_blocks(n)[0]) * P, (n + key_blocks(n)[-1]) * P)
                    for h in range(REP):
                        if b:
                            pe.wait_ge(s_sb, REP * (b - 1) + h + 1)
                        e = h % 2
                        half = slice(e * HD, (e + 1) * HD)
                        k = kt if e == g % 2 else kx
                        last = pe.matmul(ps[:, h, cols(n)], qt[half, g % 2, h // 2, n * P:(n + 1) * P],
                                         k[half, g // 2, keys], start=True, stop=True)
                    last.then_inc(s_s, 1)

                def turn(g, n):
                    b = g * NB + n
                    pe.wait_ge(s_exp, REP * (b + 1))
                    for i, kb in enumerate(key_blocks(n)):
                        c = turned(b) + i
                        if c >= 2:
                            pe.wait_ge(s_pe, c - 1)
                        for h in range(REP):
                            last = pe.transpose(ps[:, 4 + c % 2, h * P:(h + 1) * P],
                                                prob[:, b % PROBS, h, kb * P:(kb + 1) * P], ident[:, :])
                        last.then_inc(s_pt, 1)

                def values(g, n):
                    b = g * NB + n
                    pe.wait_ge(s_pe, turned(b + 1))
                    if b:
                        pe.wait_ge(s_row, b)
                    blocks = key_blocks(n)
                    for h in range(REP):
                        for kb in blocks:
                            last = pe.matmul(ps[:, 7, h * HD:(h + 1) * HD], pt[:, kb, h * P:(h + 1) * P],
                                             vt[:, n - 1 + kb, g * HD:(g + 1) * HD], start=kb == blocks[0],
                                             stop=kb == blocks[-1])
                    last.then_inc(s_o, 1)

                for n in range(UNITS):
                    unit(n)
                pe.wait_ge(s_wl, 2)
                for t in range(NT):
                    if t >= 4:
                        pe.wait_ge(s_ve, t - 3)
                    for k in range(KT):
                        last = product(pe, ps[:, 4 + t % 4, 0:GW], xh[:, k, t * P:(t + 1) * P], xl[:, k, t * P:(t + 1) * P],
                                       wh[:, 1, k, :], wl[:, 1, k, :], k == 0, k == KT - 1)
                    last.then_inc(s_mv, 1)
                for n in range(UNITS, 2 * UNITS):
                    unit(n)
                for g in range(KV):
                    for i in range(STEPS):
                        if i < NB:
                            scores(g, i)
                        if i >= LAG_V:
                            values(g, i - LAG_V)
                        if LAG_T <= i < NB + LAG_T:
                            turn(g, i - LAG_T)
                        if i in UNIT_STEPS:
                            unit(UNITS * (g + 2) + UNIT_STEPS.index(i))

            @block.scalar
            def _(act):
                def unit_out(n):
                    if n >= UNITS * (KV + 1):
                        return
                    g, (f, half) = n // UNITS, divmod(n % UNITS, 2)
                    bank = n % 4 if n < 2 * UNITS else 6
                    out = kt[:, f] if g == 0 else qt[:, (g - 1) % 2, f]
                    act.wait_ge(s_m, n + 1)
                    act.activation(out[:, half * HALF:(half + 1) * HALF], ps[:, bank, :], ACT.Copy,
                                   scale=HD ** -0.5 if g else 1.0).then_inc(s_me, 1)

                def exponentials(g, n):
                    b = g * NB + n
                    act.wait_ge(s_max, 4 * b + 3)
                    if b >= RING:
                        act.wait_ge(s_den, 2 * (b - 1))
                    for h in range(REP):
                        act.activation(prob[:, b % PROBS, h, cols(n)], prob[:, b % PROBS, h, cols(n)], ACT.Exp,
                                       bias=ntop[:, b % 2, h:h + 1], accum_out=den[:, b % 2, h:h + 1]).then_inc(s_exp, 1)
                    act.wait_ge(s_max, 4 * b + 4)
                    act.activation(esink[:, b % 2], lift[:, b % 2], ACT.Exp).then_inc(s_es, 1)

                def turned_out(g, n):
                    b = g * NB + n
                    if b:
                        act.wait_ge(s_o, b)
                    for i, kb in enumerate(key_blocks(n)):
                        c = turned(b) + i
                        act.wait_ge(s_pt, c + 1)
                        act.activation(pt[:, kb, :], ps[:, 4 + c % 2, :], ACT.Copy).then_inc(s_pe, 1)
                for n in range(2 * UNITS):
                    unit_out(n)
                for g in range(KV):
                    for i in range(STEPS):
                        if LAG_E <= i < NB + LAG_E:
                            exponentials(g, i - LAG_E)
                        if LAG_T <= i < NB + LAG_T:
                            turned_out(g, i - LAG_T)
                        if i in UNIT_STEPS:
                            unit_out(UNITS * (g + 2) + UNIT_STEPS.index(i))

            @block.vector
            def _(dve):
                flat = near[:, :, :].rearrange("p b k -> p (b k)")
                dve.wait_ge(s_near, HEADS + 1)
                dve.scalar_tensor_tensor(out=flat, in0=flat, scalar=-1.0, in1=flat, op0=ALU.mult, op1=ALU.min
                                         ).then_inc(s_neg, 1)
                for t in range(NT):
                    dve.wait_ge(s_mv, t + 1)
                    dve.tensor_copy(vt[:, t, :], ps[:, 4 + t % 4, 0:GW]).then_inc(s_ve, 1)
                dve.wait_ge(s_small, 16)
                dve.wait_ge(s_near, HEADS + 3)

                def softmax(g, n):
                    b = g * NB + n
                    u, heads = b % 2, slice(g * REP, (g + 1) * REP)
                    dve.wait_ge(s_s, b + 1)
                    if b >= PROBS:
                        dve.wait_ge(s_pt, turned(b - PROBS + 1))
                    for h in range(REP):
                        k = g * REP + h
                        dve.scalar_tensor_tensor(out=prob[:, b % PROBS, h, cols(n)], in0=flat[:, cols(n)],
                                                 scalar=slope[:, k:k + 1], in1=ps[:, h, cols(n)], op0=ALU.mult,
                                                 op1=ALU.add).then_inc(s_sb, 1)
                    dve.wait_ge(s_sb, REP * (b + 1))
                    if b >= RING:
                        dve.wait_ge(s_es, b - 1)
                    dve.tensor_reduce(top[:, u], prob[:, b % PROBS, :, cols(n)], AX, ALU.max).then_inc(s_max, 1)
                    dve.wait_ge(s_max, 4 * b + 1)
                    dve.tensor_tensor(top[:, u], top[:, u], sink[:, heads], ALU.max).then_inc(s_max, 1)
                    dve.wait_ge(s_max, 4 * b + 2)
                    dve.tensor_scalar(ntop[:, u], top[:, u], -1.0, None, ALU.mult).then_inc(s_max, 1)
                    dve.tensor_tensor(lift[:, u], sink[:, heads], top[:, u], ALU.subtract).then_inc(s_max, 1)

                def denominators(g, n):
                    b = g * NB + n
                    u = b % 2
                    dve.wait_ge(s_es, b + 1)
                    dve.wait_ge(s_exp, REP * (b + 1))
                    if b >= RING:
                        dve.wait_ge(s_row, b - 1)
                    dve.tensor_tensor(rec[:, u], den[:, u], esink[:, u], ALU.add).then_inc(s_den, 1)
                    dve.wait_ge(s_den, 2 * b + 1)
                    dve.reciprocal(rec[:, u], rec[:, u]).then_inc(s_den, 1)

                def output(g, n):
                    b = g * NB + n
                    u = b % 2
                    dve.wait_ge(s_den, 2 * b + 2)
                    dve.wait_ge(s_o, b + 1)
                    if b >= RING:
                        dve.wait_ge(s_st[u], 16 * (b // 2))
                    dve.tensor_tensor(rows[:, u].rearrange("p (h d) -> p h d", h=REP),
                                      ps[:, 7, 0:GW].rearrange("p (h d) -> p h d", h=REP),
                                      rec[:, u].unsqueeze(2).broadcast_to([P, REP, HD]), ALU.mult).then_inc(s_row, 1)
                for g in range(KV):
                    for i in range(STEPS):
                        if LAG_T <= i < NB + LAG_T:
                            denominators(g, i - LAG_T)
                        if i < NB:
                            softmax(g, i)
                        if i >= LAG_V:
                            output(g, i - LAG_V)


def build(nc, A, out):
    Phase.used = []
    with ExitStack() as ctx:
        mem = {"ps": ctx.enter_context(nc.psum_tensor("ps", [P, 8, HALF], F32))}
        for name in ("ident", "ones"):
            mem[name] = ctx.enter_context(nc.sbuf_tensor(name, [P, P], F32))
        for name, shape in (("scr", (S, SCR_COLS)),
                            ("scr_t", (4 * P, S)),
                            ("low", (2 * NT, 4, 32, 32)),
                            ("inv", (2 * NT, 4, 2, 32, 16)),
                            ("mix", (S, 2 * D)),
                            ("ao", (S, D))):
            A[name] = nc.dram_tensor(name, shape, F32, kind="Internal").ap()
        with ExitStack() as part:
            for name, shape in (("le", [P, P]), ("gt", [P, P]), ("ge", [P, P]), ("lt", [P, P]),
                                ("step", [P, NT, 2 * SSD_H]), ("beta", [P, NT, 2 * GDN_H]),
                                ("dec", [P, NT, 2 * DIR_H]), ("ein", [P, NT, 2 * DIR_H]),
                                ("eout", [P, NT, 2 * DIR_H]), ("etot", [P, NT, 2 * DIR_H]), ("ssq", [P, 24 * NT])):
                mem[name] = part.enter_context(nc.sbuf_tensor(name, shape, F32))
            for phase in (phase_masks, phase_in, phase_ssd, phase_gdn):
                phase(nc, A, mem)
        mem["acc"] = ctx.enter_context(nc.sbuf_tensor("acc", [P, NT, D], F32))
        for name in ("xh", "xl"):
            mem[name] = ctx.enter_context(nc.sbuf_tensor(name, [P, KT, S], F32R))
        for name in ("wh", "wl"):
            mem[name] = ctx.enter_context(nc.sbuf_tensor(name, [P, RING, KT * SLAB], F32R))
        phase_project(nc, A, mem, 0, first_slab(A, 0, "mlp"))
        phase_mlp(nc, A, mem, 0, None, first_slab(A, 1, "attn"))
        phase_attn(nc, A, mem, first_slab(A, 1, "project"))
        phase_project(nc, A, mem, 1, first_slab(A, 1, "mlp"))
        phase_mlp(nc, A, mem, 1, out)


_INS = ["x", "even_w_in", "ssd_conv_w", "ssd_conv_b", "ssd_dt_bias", "ssd_a_log", "ssd_d", "ssd_norm_w", "gdn_conv_w",
        "gdn_dt_bias", "gdn_a_log", "gdn_norm_w", "even_w_out", "attn_w_qkv", "attn_sink", "attn_w_o", "ln_mix_g",
        "ln_mix_b", "mlp_w1", "mlp_w2", "ln_ffn_g", "ln_ffn_b"]


def kernel(**inputs):
    import numpy as _np
    import concourse.bacc as _bacc
    from concourse import mybir as _mybir
    from concourse.bass_utils import run_bass_kernel_spmd as _run

    nc = _bacc.Bacc("TRN2", target_bir_lowering=False, num_devices=1)
    arrays, args = {}, {}
    for name in _INS:
        a = _np.ascontiguousarray(inputs[name])
        arrays[f"in_{name}_dram"] = a
        args[name] = nc.dram_tensor(f"in_{name}_dram", a.shape, _mybir.dt.from_np(a.dtype), kind="ExternalInput").ap()
    out = nc.dram_tensor("out_0_dram", (1, S, D), _mybir.dt.float32, kind="ExternalOutput").ap()
    build(nc, args, out[0])
    r = _run(nc, [arrays], core_ids=[0])
    return r.results[0]["out_0_dram"]
```
